# Optimizing a Trainium2 kernel written in Bass

```python
import jax, jax.numpy as jnp
from jax import lax
import numpy as np

D_MODEL = 1024
BATCH = 1
SEQ = 256
DEPTH = 1

GLA_HEADS = 4
GLA_DK = D_MODEL // 2 // GLA_HEADS
GLA_DV = D_MODEL // GLA_HEADS
GLA_QK_W = GLA_HEADS * GLA_DK
GLA_V_W = GLA_HEADS * GLA_DV
GLA_GATE_RANK = 16
GLA_GATE_NORMALIZER = 16.0
GLA_LOG_GATE_MIN = -0.5
GLA_CHUNK = 64
SWA_HEADS = 8
SWA_KV_HEADS = 2
SWA_HEAD_DIM = 128
SWA_Q_W = SWA_HEADS * SWA_HEAD_DIM
SWA_KV_W = SWA_KV_HEADS * SWA_HEAD_DIM
SWA_WINDOW = 128
SWA_BLOCK = 128
ROPE_THETA = 10000.0
D_FF = -(-8 * D_MODEL // (3 * 256)) * 256
NORM_EPS = 1e-6
IN_SPLITS = (GLA_QK_W, GLA_QK_W, GLA_V_W, GLA_V_W, GLA_GATE_RANK, GLA_GATE_RANK,
             SWA_Q_W, SWA_KV_W, SWA_KV_W, D_MODEL, D_MODEL)
D_IN = sum(IN_SPLITS)


def _rms_norm(x, g):
    xf = x.astype(jnp.float32)
    y = xf * lax.rsqrt(jnp.mean(xf * xf, axis=-1, keepdims=True) + NORM_EPS)
    return (y * g.astype(jnp.float32)).astype(x.dtype)

def _rope(x, pos):
    half = x.shape[-1] // 2
    inv_freq = ROPE_THETA ** (-jnp.arange(half, dtype=jnp.float32) / half)
    ang = pos.astype(jnp.float32)[:, None] * inv_freq[None, :]
    cos = jnp.cos(ang)[None, :, None, :]
    sin = jnp.sin(ang)[None, :, None, :]
    x1, x2 = x[..., :half], x[..., half:]
    return jnp.concatenate([x1 * cos - x2 * sin, x2 * cos + x1 * sin], axis=-1)

def _gla_direction(q, k, v, log_g, include_diag):
    bsz, nh, s, dk = q.shape
    dv = v.shape[-1]
    c = GLA_CHUNK
    n = s // c
    q = q.reshape(bsz, nh, n, c, dk)
    k = k.reshape(bsz, nh, n, c, dk)
    log_g = log_g.reshape(bsz, nh, n, c, dk)
    v = v.reshape(bsz, nh, n, c, dv)
    b = jnp.cumsum(log_g, axis=3)
    b_last = b[:, :, :, -1:, :]
    q_dec = q * jnp.exp(b)
    k_inv = k * jnp.exp(-b)
    k_tail = k * jnp.exp(b_last - b)
    mask = jnp.tril(jnp.ones((c, c), dtype=bool), k=0 if include_diag else -1)
    scores = jnp.where(mask, jnp.einsum("bhncd,bhnmd->bhncm", q_dec, k_inv), 0.0)
    o_intra = jnp.einsum("bhncm,bhnme->bhnce", scores, v)
    chunk_kv = jnp.einsum("bhnmd,bhnme->nbhde", k_tail, v)
    chunk_decay = jnp.exp(jnp.moveaxis(b_last[:, :, :, 0, :], 2, 0))

    def step(state, inp):
        kv_n, dec_n = inp
        return dec_n[..., None] * state + kv_n, state

    _, states = lax.scan(step, jnp.zeros((bsz, nh, dk, dv), q.dtype), (chunk_kv, chunk_decay))
    o_inter = jnp.einsum("bhncd,nbhde->bhnce", q_dec, states)
    return (o_intra + o_inter).reshape(bsz, nh, s, dv)

def _gla_branch(q, k, v, r, lr_f, lr_b, up_f, bias_f, up_b, bias_b, out_g):
    bsz, s, _ = q.shape
    f32 = jnp.float32

    def heads(t, d):
        return t.astype(f32).reshape(bsz, s, GLA_HEADS, d).transpose(0, 2, 1, 3)

    def log_gate(lr, up, bias):
        z = lr.astype(f32) @ up.astype(f32) + bias.astype(f32)
        lg = jnp.maximum(jax.nn.log_sigmoid(z) / GLA_GATE_NORMALIZER, GLA_LOG_GATE_MIN)
        return heads(lg, GLA_DK)

    qh = heads(q, GLA_DK) * (GLA_DK ** -0.5)
    kh = heads(k, GLA_DK)
    vh = heads(v, GLA_DV)
    o_fwd = _gla_direction(qh, kh, vh, log_gate(lr_f, up_f, bias_f), True)
    flip = lambda t: jnp.flip(t, axis=2)
    o_bwd = flip(_gla_direction(flip(qh), flip(kh), flip(vh),
                                flip(log_gate(lr_b, up_b, bias_b)), False))
    o = _rms_norm(o_fwd + o_bwd, out_g)
    o = o.transpose(0, 2, 1, 3).reshape(bsz, s, GLA_V_W)
    return (o * jax.nn.silu(r.astype(f32))).astype(q.dtype)

def _swa_branch(q, k, v, q_g, k_g, sinks):
    bsz, s, _ = q.shape
    f32 = jnp.float32
    hd, hkv, blk = SWA_HEAD_DIM, SWA_KV_HEADS, SWA_BLOCK
    grp = SWA_HEADS // SWA_KV_HEADS
    n = s // blk
    pos = jnp.arange(s)
    q = _rope(_rms_norm(q.astype(f32).reshape(bsz, s, SWA_HEADS, hd), q_g), pos)
    k = _rope(_rms_norm(k.astype(f32).reshape(bsz, s, hkv, hd), k_g), pos)
    v = v.astype(f32).reshape(bsz, s, hkv, hd)

    def context(t):
        tp = jnp.pad(t, ((0, 0), (blk, blk), (0, 0), (0, 0)))
        return jnp.concatenate(
            [tp[:, o * blk:o * blk + s].reshape(bsz, n, blk, hkv, hd) for o in range(3)], axis=2)

    kc, vc = context(k), context(v)
    qb = q.reshape(bsz, n, blk, hkv, grp, hd)
    scores = jnp.einsum("bnqhgd,bnkhd->bnhgqk", qb, kc) * (hd ** -0.5)
    q_off = jnp.arange(blk)
    k_off = jnp.arange(3 * blk) - blk
    in_window = jnp.abs(k_off[None, :] - q_off[:, None]) <= SWA_WINDOW
    k_abs = jnp.arange(n)[:, None] * blk + k_off[None, :]
    in_seq = (k_abs >= 0) & (k_abs < s)
    mask = in_window[None, :, :] & in_seq[:, None, :]
    scores = jnp.where(mask[None, :, None, None], scores, -jnp.inf)
    sink = sinks.astype(f32).reshape(1, 1, hkv, grp, 1, 1)
    m = jnp.maximum(scores.max(axis=-1, keepdims=True), sink)
    p = jnp.exp(scores - m)
    denom = p.sum(axis=-1, keepdims=True) + jnp.exp(sink - m)
    o = jnp.einsum("bnhgqk,bnkhd->bnqhgd", p / denom, vc)
    return o.reshape(bsz, s, SWA_Q_W)

def first_inputs(seed: int = 0) -> dict:
    key = jax.random.key(seed)
    ks = jax.random.split(key, 20)
    f32 = jnp.float32
    nrm = lambda k, shape, scale: jax.random.normal(k, shape, f32) * scale
    gain = lambda k, d: 1.0 + 0.02 * jax.random.normal(k, (DEPTH, d), f32)
    return {
        "x": nrm(ks[0], (BATCH, SEQ, D_MODEL), 1.0),
        "norm_mix_g": gain(ks[1], D_MODEL),
        "w_in": nrm(ks[2], (DEPTH, D_MODEL, D_IN), D_MODEL ** -0.5),
        "gla_gate_up_fwd": nrm(ks[3], (DEPTH, GLA_GATE_RANK, GLA_QK_W), GLA_GATE_RANK ** -0.5),
        "gla_gate_bias_fwd": nrm(ks[4], (DEPTH, GLA_QK_W), 0.02),
        "gla_gate_up_bwd": nrm(ks[5], (DEPTH, GLA_GATE_RANK, GLA_QK_W), GLA_GATE_RANK ** -0.5),
        "gla_gate_bias_bwd": nrm(ks[6], (DEPTH, GLA_QK_W), 0.02),
        "gla_out_norm_g": gain(ks[7], GLA_DV),
        "w_o_gla": nrm(ks[8], (DEPTH, GLA_V_W, D_MODEL), GLA_V_W ** -0.5),
        "swa_q_norm_g": gain(ks[9], SWA_HEAD_DIM),
        "swa_k_norm_g": gain(ks[10], SWA_HEAD_DIM),
        "swa_sinks": nrm(ks[11], (DEPTH, SWA_HEADS), 0.5),
        "w_o_swa": nrm(ks[12], (DEPTH, SWA_Q_W, D_MODEL), SWA_Q_W ** -0.5),
        "w_out": nrm(ks[13], (DEPTH, D_MODEL, D_MODEL), D_MODEL ** -0.5),
        "norm_ffn_g": gain(ks[14], D_MODEL),
        "w_ffn_in": nrm(ks[15], (DEPTH, D_MODEL, 2 * D_FF), D_MODEL ** -0.5),
        "w_ffn_out": nrm(ks[16], (DEPTH, D_FF, D_MODEL), D_FF ** -0.5),
    }

def first_block(x, norm_mix_g, w_in, gla_gate_up_fwd, gla_gate_bias_fwd, gla_gate_up_bwd,
              gla_gate_bias_bwd, gla_out_norm_g, w_o_gla, swa_q_norm_g, swa_k_norm_g,
              swa_sinks, w_o_swa, w_out, norm_ffn_g, w_ffn_in, w_ffn_out):
    split_at = tuple(int(i) for i in np.cumsum(IN_SPLITS)[:-1])
    for l in range(DEPTH):
        h = _rms_norm(x, norm_mix_g[l])
        proj = h @ w_in[l]
        (g_q, g_k, g_v, g_r, g_lr_f, g_lr_b,
         s_q, s_k, s_v, gate_a, gate_b) = jnp.split(proj, split_at, axis=-1)
        y_gla = _gla_branch(g_q, g_k, g_v, g_r, g_lr_f, g_lr_b,
                            gla_gate_up_fwd[l], gla_gate_bias_fwd[l],
                            gla_gate_up_bwd[l], gla_gate_bias_bwd[l],
                            gla_out_norm_g[l]) @ w_o_gla[l]
        y_swa = _swa_branch(s_q, s_k, s_v, swa_q_norm_g[l], swa_k_norm_g[l],
                            swa_sinks[l]).astype(x.dtype) @ w_o_swa[l]
        merged = jax.nn.sigmoid(gate_a) * y_gla + jax.nn.sigmoid(gate_b) * y_swa
        x = x + merged @ w_out[l]
        h2 = _rms_norm(x, norm_ffn_g[l])
        gu = h2 @ w_ffn_in[l]
        ff_gate, ff_up = gu[..., :D_FF], gu[..., D_FF:]
        x = x + (jax.nn.silu(ff_gate) * ff_up) @ w_ffn_out[l]
    return x


DEPTH_2 = 2

MLA_HEADS = 4
QK_NOPE = 128
QK_ROPE = 64
V_HEAD = 128
Q_RANK = 384
KV_RANK = 256
Q_BLOCK = 128
HG_HEADS = 4
HG_KEY = 128
HG_VAL = 128
HG_CHUNK = 64
MLA_WIDTH = MLA_HEADS * V_HEAD
HG_WIDTH = HG_HEADS * HG_VAL
HG_FDIM = HG_HEADS * HG_KEY
MIX_WIDTH = MLA_WIDTH + HG_WIDTH
IN_COLS = Q_RANK + KV_RANK + QK_ROPE + 2 * HG_FDIM + 2 * HG_WIDTH
DENSE_FF = 2816
N_EXPERTS = 8
TOP_K = 2
EXPERT_FF = 3584
N_DENSE = (DEPTH_2 + 1) // 2
N_MOE = DEPTH_2 // 2
EPS = 1e-6
F_FLOOR = 1e-30


F32 = jnp.float32
NEG_BIG = float(np.finfo(np.float32).min)

def _rmsnorm(x, gain):
    xf = x.astype(F32)
    y = xf * lax.rsqrt(jnp.mean(xf * xf, axis=-1, keepdims=True) + EPS)
    return (y * gain.astype(F32)).astype(x.dtype)

def _rope_tables(positions):
    inv = ROPE_THETA ** (-jnp.arange(0, QK_ROPE, 2, dtype=F32) / QK_ROPE)
    ang = positions.astype(F32)[..., None] * inv
    return jnp.cos(ang), jnp.sin(ang)

def _apply_rope(x, cos, sin):
    x1, x2 = jnp.split(x, 2, axis=-1)
    cos = cos.astype(x.dtype)
    sin = sin.astype(x.dtype)
    return jnp.concatenate([x1 * cos - x2 * sin, x1 * sin + x2 * cos], axis=-1)

def _mla(c_q, c_kv, k_pe, positions, q_a_norm, w_q_b, kv_a_norm, w_kv_b):
    B, S, _ = c_q.shape
    q = (_rmsnorm(c_q, q_a_norm) @ w_q_b).reshape(B, S, MLA_HEADS, QK_NOPE + QK_ROPE)
    q_nope, q_pe = q[..., :QK_NOPE], q[..., QK_NOPE:]
    cos, sin = _rope_tables(positions)
    q_pe = _apply_rope(q_pe, cos[:, :, None, :], sin[:, :, None, :])
    k_pe = _apply_rope(k_pe, cos, sin)
    kv = (_rmsnorm(c_kv, kv_a_norm) @ w_kv_b).reshape(B, S, MLA_HEADS, QK_NOPE + V_HEAD)
    k_nope, v = kv[..., :QK_NOPE], kv[..., QK_NOPE:]
    scale = (QK_NOPE + QK_ROPE) ** -0.5
    nb = S // Q_BLOCK
    qn_blk = (q_nope * scale).reshape(B, nb, Q_BLOCK, MLA_HEADS, QK_NOPE).transpose(1, 0, 2, 3, 4)
    qp_blk = (q_pe * scale).reshape(B, nb, Q_BLOCK, MLA_HEADS, QK_ROPE).transpose(1, 0, 2, 3, 4)
    starts = jnp.arange(nb, dtype=jnp.int32) * Q_BLOCK
    key_idx = jnp.arange(S, dtype=jnp.int32)

    def block(args):
        qn, qp, start = args
        s = jnp.einsum('bqhd,bkhd->bhqk', qn, k_nope, preferred_element_type=F32)
        s = s + jnp.einsum('bqhr,bkr->bhqk', qp, k_pe, preferred_element_type=F32)
        q_idx = start + jnp.arange(Q_BLOCK, dtype=jnp.int32)
        s = jnp.where(key_idx[None, :] <= q_idx[:, None], s, NEG_BIG)
        p = jax.nn.softmax(s, axis=-1).astype(v.dtype)
        return jnp.einsum('bhqk,bkhd->bqhd', p, v)

    o = lax.map(block, (qn_blk, qp_blk, starts))
    return o.transpose(1, 0, 2, 3, 4).reshape(B, S, MLA_WIDTH)

def _hgrn2(q_raw, f_raw, i_in, g_raw, lower_bound, out_norm):
    B, S, _ = q_raw.shape
    nc = S // HG_CHUNK
    q = jax.nn.silu(q_raw.astype(F32))
    z = f_raw.astype(F32)
    lb = lower_bound.astype(F32)
    f = lb + (1.0 - lb) * jax.nn.sigmoid(z)
    log_f = jnp.log(jnp.maximum(f, F_FLOOR))
    k = (1.0 - lb) * jax.nn.sigmoid(-z)

    def to_chunks(t, d):
        return t.reshape(B, nc, HG_CHUNK, HG_HEADS, d).transpose(1, 0, 3, 2, 4)

    qc = to_chunks(q, HG_KEY)
    kc = to_chunks(k, HG_KEY)
    lfc = to_chunks(log_f, HG_KEY)
    vc = to_chunks(i_in.astype(F32), HG_VAL)
    tri = jnp.tril(jnp.ones((HG_CHUNK, HG_CHUNK), dtype=bool))[:, :, None]

    def step(state, inp):
        qb, kb, vb, lfb = inp
        b = jnp.cumsum(lfb, axis=2)
        diff = b[:, :, :, None, :] - b[:, :, None, :, :]
        decay = jnp.where(tri, jnp.exp(jnp.where(tri, diff, 0.0)), 0.0)
        attn = jnp.einsum('bhtd,bhsd,bhtsd->bhts', qb, kb, decay)
        o = jnp.einsum('bhts,bhsv->bhtv', attn, vb) + jnp.einsum('bhtd,bhdv->bhtv', qb * jnp.exp(b), state)
        b_last = b[:, :, -1:, :]
        new_state = jnp.exp(b_last[:, :, 0, :])[..., None] * state + jnp.einsum('bhsd,bhsv->bhdv', kb * jnp.exp(b_last - b), vb)
        return new_state, o

    s0 = jnp.zeros((B, HG_HEADS, HG_KEY, HG_VAL), F32)
    _, o = lax.scan(step, s0, (qc, kc, vc, lfc))
    o = o.transpose(1, 0, 3, 2, 4).reshape(B, S, HG_HEADS, HG_VAL)
    o = _rmsnorm(o, out_norm) * jax.nn.silu(g_raw.astype(F32).reshape(B, S, HG_HEADS, HG_VAL))
    return o.reshape(B, S, HG_WIDTH)

def _swiglu(h, w_gate, w_up, w_down):
    return (jax.nn.silu(h @ w_gate) * (h @ w_up)) @ w_down

def _moe(h, w_router, w_gate, w_up, w_down):
    B, S, D = h.shape
    T = B * S
    xf = h.reshape(T, D)
    logits = jnp.einsum('td,de->te', xf, w_router, preferred_element_type=F32)
    top_logits, top_idx = lax.top_k(logits, TOP_K)
    gates = jax.nn.softmax(top_logits, axis=-1)
    flat_e = top_idx.reshape(-1)
    flat_tok = jnp.repeat(jnp.arange(T, dtype=jnp.int32), TOP_K)
    order = jnp.argsort(flat_e)
    tok_sorted = flat_tok[order]
    xs = xf[tok_sorted]
    group_sizes = jnp.bincount(flat_e, length=N_EXPERTS).astype(jnp.int32)
    hid = jax.nn.silu(lax.ragged_dot(xs, w_gate, group_sizes)) * lax.ragged_dot(xs, w_up, group_sizes)
    ys = lax.ragged_dot(hid, w_down, group_sizes)
    ys = ys * gates.reshape(-1)[order][:, None].astype(ys.dtype)
    out = jnp.zeros_like(xf).at[tok_sorted].add(ys)
    return out.reshape(B, S, D)

def _normal(key, shape, fan_in):
    return jax.random.normal(key, shape, F32) * (fan_in ** -0.5)

def _gain(key, shape):
    return 1.0 + 0.02 * jax.random.normal(key, shape, F32)

def second_inputs(seed: int = 0) -> dict:
    key = jax.random.key(seed)
    ks = jax.random.split(key, 24)
    x = jax.random.normal(ks[0], (BATCH, SEQ, D_MODEL), F32)
    offset = jax.random.randint(ks[1], (BATCH, 1), 0, 4096, dtype=jnp.int32)
    positions = offset + jnp.arange(SEQ, dtype=jnp.int32)[None, :]
    return {
        "x": x,
        "positions": positions,
        "mix_norm": _gain(ks[2], (DEPTH_2, D_MODEL)),
        "w_in": _normal(ks[3], (DEPTH_2, D_MODEL, IN_COLS), D_MODEL),
        "q_a_norm": _gain(ks[4], (DEPTH_2, Q_RANK)),
        "w_q_b": _normal(ks[5], (DEPTH_2, Q_RANK, MLA_HEADS * (QK_NOPE + QK_ROPE)), Q_RANK),
        "kv_a_norm": _gain(ks[6], (DEPTH_2, KV_RANK)),
        "w_kv_b": _normal(ks[7], (DEPTH_2, KV_RANK, MLA_HEADS * (QK_NOPE + V_HEAD)), KV_RANK),
        "hg_lower_bounds": 0.5 * jax.random.normal(ks[8], (DEPTH_2, HG_FDIM), F32),
        "hg_out_norm": _gain(ks[9], (DEPTH_2, HG_VAL)),
        "w_out": _normal(ks[10], (DEPTH_2, MIX_WIDTH, D_MODEL), MIX_WIDTH),
        "ffn_norm": _gain(ks[11], (DEPTH_2, D_MODEL)),
        "dense_w_gate": _normal(ks[12], (N_DENSE, D_MODEL, DENSE_FF), D_MODEL),
        "dense_w_up": _normal(ks[13], (N_DENSE, D_MODEL, DENSE_FF), D_MODEL),
        "dense_w_down": _normal(ks[14], (N_DENSE, DENSE_FF, D_MODEL), DENSE_FF),
        "moe_router": _normal(ks[15], (N_MOE, D_MODEL, N_EXPERTS), D_MODEL),
        "moe_w_gate": _normal(ks[16], (N_MOE, N_EXPERTS, D_MODEL, EXPERT_FF), D_MODEL),
        "moe_w_up": _normal(ks[17], (N_MOE, N_EXPERTS, D_MODEL, EXPERT_FF), D_MODEL),
        "moe_w_down": _normal(ks[18], (N_MOE, N_EXPERTS, EXPERT_FF, D_MODEL), EXPERT_FF),
        "final_norm": _gain(ks[19], (D_MODEL,)),
    }

def second_block(x, positions, mix_norm, w_in, q_a_norm, w_q_b, kv_a_norm, w_kv_b, hg_lower_bounds, hg_out_norm, w_out, ffn_norm, dense_w_gate, dense_w_up, dense_w_down, moe_router, moe_w_gate, moe_w_up, moe_w_down, final_norm):
    lb_p = jax.nn.softmax(hg_lower_bounds.astype(F32), axis=0)
    lower = jnp.cumsum(lb_p, axis=0) - lb_p[0:1]
    splits = np.cumsum([Q_RANK, KV_RANK, QK_ROPE, HG_FDIM, HG_FDIM, HG_WIDTH]).tolist()
    for l in range(DEPTH_2):
        h = _rmsnorm(x, mix_norm[l])
        proj = h @ w_in[l]
        c_q, c_kv, k_pe, hq, hf, hi, hg = jnp.split(proj, splits, axis=-1)
        a = _mla(c_q, c_kv, k_pe, positions, q_a_norm[l], w_q_b[l], kv_a_norm[l], w_kv_b[l])
        r = _hgrn2(hq, hf, hi, hg, lower[l], hg_out_norm[l]).astype(x.dtype)
        x = x + jnp.concatenate([a, r], axis=-1) @ w_out[l]
        h = _rmsnorm(x, ffn_norm[l])
        if l % 2 == 0:
            j = l // 2
            x = x + _swiglu(h, dense_w_gate[j], dense_w_up[j], dense_w_down[j])
        else:
            j = l // 2
            x = x + _moe(h, moe_router[j], moe_w_gate[j], moe_w_up[j], moe_w_down[j])
    return _rmsnorm(x, final_norm)


def setup_inputs(seed=0):
    out = dict(first_inputs(seed))
    for name, value in second_inputs(seed + 1).items():
        if name != "x":
            out[name + "_2"] = value
    return out


def reference(
    x, norm_mix_g, w_in, gla_gate_up_fwd, gla_gate_bias_fwd, gla_gate_up_bwd, gla_gate_bias_bwd,
    gla_out_norm_g, w_o_gla, swa_q_norm_g, swa_k_norm_g, swa_sinks, w_o_swa, w_out, norm_ffn_g,
    w_ffn_in, w_ffn_out, positions_2, mix_norm_2, w_in_2, q_a_norm_2, w_q_b_2, kv_a_norm_2,
    w_kv_b_2, hg_lower_bounds_2, hg_out_norm_2, w_out_2, ffn_norm_2, dense_w_gate_2,
    dense_w_up_2, dense_w_down_2, moe_router_2, moe_w_gate_2, moe_w_up_2, moe_w_down_2,
    final_norm_2,
):
    x = first_block(
        x, norm_mix_g, w_in, gla_gate_up_fwd, gla_gate_bias_fwd, gla_gate_up_bwd,
        gla_gate_bias_bwd, gla_out_norm_g, w_o_gla, swa_q_norm_g, swa_k_norm_g, swa_sinks,
        w_o_swa, w_out, norm_ffn_g, w_ffn_in, w_ffn_out,
    )
    return second_block(
        x, positions_2, mix_norm_2, w_in_2, q_a_norm_2, w_q_b_2, kv_a_norm_2, w_kv_b_2,
        hg_lower_bounds_2, hg_out_norm_2, w_out_2, ffn_norm_2, dense_w_gate_2, dense_w_up_2,
        dense_w_down_2, moe_router_2, moe_w_gate_2, moe_w_up_2, moe_w_down_2, final_norm_2,
    )


_drawn_inputs = setup_inputs


def setup_inputs(seed=0):
    import zlib

    import numpy as np

    out = dict(_drawn_inputs(seed))
    spreads = {}
    factors = {'gla_gate_bias_fwd': 4.422,
     'gla_gate_bias_bwd': 2.817,
     'gla_out_norm_g': 3.125,
     'swa_q_norm_g': 3.329,
     'swa_k_norm_g': 4.454,
     'swa_sinks': 8.0,
     'q_a_norm_2': 5.192,
     'kv_a_norm_2': 4.609,
     'hg_lower_bounds_2': 8.0,
     'hg_out_norm_2': 4.821,
     'ffn_norm_2': 3.601}
    for name, (base, spread) in spreads.items():
        noise = np.random.default_rng([zlib.crc32(name.encode()), seed]).standard_normal(out[name].shape)
        drawn = base * np.exp(spread * noise) if base else spread * noise
        out[name] = __import__('jax').numpy.asarray(drawn.astype(out[name].dtype))
    for name, factor in factors.items():
        out[name] = (out[name] * factor).astype(out[name].dtype)
    return out
```

```python
from contextlib import ExitStack

import numpy as np

import concourse.bass as bass
from concourse import mybir

ALU = mybir.AluOpType
ACT = mybir.ActivationFunctionType
F32 = mybir.dt.float32
I32 = mybir.dt.int32
U32 = mybir.dt.uint32
AX_X = mybir.AxisListType.X

P = 128
TOKENS = 256
T = TOKENS // P
D = 1024
KD = D // P
EPS = 1e-6
MASKED = -1e30

GLA_HEADS, GLA_DK, GLA_DV, GLA_RANK = 4, 128, 256, 16
SWA_HEADS, SWA_KV, HD, WINDOW = 8, 2, 128, 128
D_FF = 2816
Q_RANK, KV_RANK, ROPE = 384, 256, 64
MLA_HEADS, NOPE, V_HEAD = 4, 128, 128
HG_HEADS = 4
EXPERTS, EXPERT_FF = 8, 3584
LEVELS = [64, 32, 16, 8, 4, 2, 1]
LN_F_FLOOR = float(np.log(1e-30))

SLOT = KD * 512
SLOTS = 7
DENSE_SLOTS = 4
CAP = 96
MAX_ROUNDS = -(-TOKENS // CAP)
FF_STEP = 512
MOE_STEPS = EXPERT_FF // FF_STEP
MOE_LOADS = 3 * MOE_STEPS
FFN_UNITS = D_FF // 256

CONSTS = [("le", P), ("ge", P), ("gt", P), ("lt", P), ("ident", P), ("ones", P),
          ("window", T * 256), ("swa_cos", T * HD), ("swa_sin", T * HD), ("causal", T * 256), ("iota", CAP),
          ("inv_freq", ROPE // 2)]
CONST_AT = {}
CONST_WORDS = 0
for _name, _width in CONSTS:
    CONST_AT[_name] = (CONST_WORDS, _width)
    CONST_WORDS += _width


def constants():
    r, c = np.arange(P)[:, None], np.arange(P)[None, :]
    key = np.arange(256)[None, :]
    query = [r + P * t for t in range(T)]
    half = HD // 2
    inv = (np.float32(10000.0) ** (-np.arange(half, dtype=np.float32) / np.float32(half))).astype(np.float32)
    ang = np.arange(TOKENS, dtype=np.float32)[:, None] * inv[None, :]
    cos, sin = np.cos(ang), np.sin(ang)
    tiles = lambda a: a.reshape(T, P, -1).transpose(1, 0, 2).reshape(P, -1)
    inv_pe = np.float32(10000.0) ** (-np.arange(0, ROPE, 2, dtype=np.float32) / np.float32(ROPE))
    parts = {
        "le": r <= c, "ge": r >= c, "gt": r > c, "lt": r < c, "ident": r == c, "ones": np.ones((P, P)),
        "window": np.concatenate([np.where(abs(q - key) <= WINDOW, 0.0, MASKED) for q in query], 1),
        "causal": np.concatenate([np.where(key <= q, 0.0, MASKED) for q in query], 1),
        "iota": np.broadcast_to(np.arange(CAP), (P, CAP)),
        "swa_cos": tiles(np.concatenate([cos, cos], 1)), "swa_sin": tiles(np.concatenate([-sin, sin], 1)),
        "inv_freq": np.broadcast_to(inv_pe, (P, ROPE // 2)),
    }
    table = np.concatenate([np.asarray(parts[n], np.float32).reshape(P, w) for n, w in CONSTS], 1)
    masks = [(r == c)]
    for h in LEVELS:
        masks.append((r // (2 * h) == c // (2 * h)) & (r % (2 * h) < h) & (c % (2 * h) >= h))
    return np.ascontiguousarray(table), np.ascontiguousarray(np.concatenate(masks, 1).astype(np.int32))


def counter():
    counts = {}

    def told(name):
        counts[name] = counts.get(name, 0) + 1
        return counts[name]

    return told


def gemm_plan():
    plan = []

    def add(name, weight, start, width, k=KD):
        plan.append((name, weight, start, width, k))

    add("gk", "w_in", 512, 512)
    add("gq", "w_in", 0, 512)
    add("lr", "w_in", 3072, 32)
    add("gv0", "w_in", 1024, 512)
    add("gv1", "w_in", 1536, 512)
    add("gr0", "w_in", 2048, 512)
    add("gr1", "w_in", 2560, 512)
    add("sq0", "w_in", 3104, 512)
    add("sq1", "w_in", 3616, 512)
    add("skv", "w_in", 4128, 512)
    add("ga0", "w_in", 4640, 512)
    add("ga1", "w_in", 5152, 512)
    add("gb0", "w_in", 5664, 512)
    add("gb1", "w_in", 6176, 512)
    for i in range(2):
        add(f"og{i}", "w_o_gla", 512 * i, 512)
    for i in range(2):
        add(f"os{i}", "w_o_swa", 512 * i, 512)
    for i in range(2):
        add(f"wo{i}", "w_out", 512 * i, 512)
    add("FFN", "f1", 0, 0)
    for layer in range(2):
        base = Q_RANK + KV_RANK + ROPE
        w = f"w_in_2_{layer}"
        add(f"hf_{layer}", w, base + 512, 512)
        add(f"c0_{layer}", w, 0, 512)
        add(f"c1_{layer}", w, 512, base - 512)
        add(f"hi_{layer}", w, base + 1024, 512)
        add(f"hq_{layer}", w, base, 512)
        add(f"hg_{layer}", w, base + 1536, 512)
        for i in range(2):
            add(f"qb{i}_{layer}", f"w_q_b_2_{layer}", 384 * i, 384, Q_RANK // P)
        for i in range(2):
            add(f"kvb{i}_{layer}", f"w_kv_b_2_{layer}", 512 * i, 512, KV_RANK // P)
        for i in range(2):
            add(f"wo{i}_{layer}", f"w_out_2_{layer}", 512 * i, 512)
        if layer == 0:
            add("FFN", "f2", 0, 0)
    return plan


def pair_plan():
    plan = [("hT_f0", 4), ("lrT", 1), ("z", 4), ("gqT", 2), ("gkT", 2), ("gb", 4), ("tail", 2), ("gsc", 4), ("gst", 4),
            ("go", 4), ("goT", 4), ("sT", 5), ("ssc", 8), ("sP", 8), ("so", 4), ("soT", 4), ("mT", 4), ("hT_f1", 4)]
    for layer in range(2):
        plan += [(f"hT_l{layer}", 4), (f"hkT_{layer}", 2), (f"hb_{layer}", 2), (f"ht_{layer}", 1),
                 (f"cT_{layer}", 3), (f"hqT_{layer}", 2)]
        plan += [(f"hlev_{layer}", T * (len(LEVELS) + 1)), (f"hst_{layer}", 1), (f"ho_{layer}", 2)]
        plan += [(f"mqT_{layer}", 2), (f"mkT_{layer}", 2), (f"mpT_{layer}", 3), (f"msc_{layer}", 4),
                 (f"mP_{layer}", 4), (f"mo_{layer}", 2), (f"mixT_{layer}", 4), (f"hT_g{layer}", 4)]
    plan += [("router", 1), ("ranks", 1)]
    return plan


def build(nc, A, out):
    gemms = [g for g in gemm_plan() if g[0] != "FFN"]
    gemm_at = {g[0]: T * i for i, g in enumerate(gemms)}
    pair_at, pair_end, n = {}, {}, 0
    for name, banks in pair_plan():
        pair_at[name], pair_end[name] = n, n + banks
        n += banks

    loads = []
    ffn_steps = [min(FF_STEP, D_FF - s) for s in range(0, D_FF, FF_STEP)]
    for name, weight, start, width, k in gemm_plan():
        if name != "FFN":
            src = A[weight].rearrange("(k p) n -> p k n", p=P)[:, :, start:start + width]
            loads.append((name, src, (k, width), ("gemm_done", gemm_at[name] + T)))
            continue
        units = 0
        for s, size in enumerate(ffn_steps):
            units += size // 256
            cols = slice(s * FF_STEP, s * FF_STEP + size)
            for kind in ("gate", "up"):
                src = A[f"{weight}_{kind}"].rearrange("(k p) n -> p k n", p=P)[:, :, cols]
                loads.append((f"{weight}_{kind}{s}", src, (KD, size), (f"{weight}_{kind}_done", units)))
            src = A[f"{weight}_down"][cols, :].rearrange("(k p) n -> p k n", p=P)
            loads.append((f"{weight}_down{s}", src, (size // P, D), (f"{weight}_down_done", units)))
    load_no = {ld[0]: i for i, ld in enumerate(loads)}
    slot_of = [(i - len(loads)) % DENSE_SLOTS for i in range(len(loads))]
    landed = [16 * slot_of[:i + 1].count(slot_of[i]) for i in range(len(loads))]

    with ExitStack() as ctx:
        sems = {}

        def sem(name):
            if name not in sems:
                sems[name] = ctx.enter_context(nc.semaphore(name))
            return sems[name]

        def sb(name, words):
            return ctx.enter_context(nc.sbuf_tensor(name, [P, words], F32))

        ring = sb("weight_ring", SLOTS * SLOT)
        x_sb = sb("x_sb", T * D)
        h_sb = sb("h_sb", T * D)
        hT_sb = sb("hT_sb", KD * TOKENS)
        const_sb = sb("const_sb", CONST_WORDS)
        level_masks = ctx.enter_context(nc.sbuf_tensor("level_masks", [P, (len(LEVELS) + 1) * P], I32))
        small = sb("small_sb", 320)
        work_sb = sb("work_sb", 13968)
        more = sb("more_sb", 256 + 256)
        bank = [ctx.enter_context(nc.psum_tensor(f"bank{i}", [P, 512], F32)) for i in range(8)]
        gemm_bank, pair_bank = bank[0:4], bank[4:8]

        def work(at, words):
            assert at + words <= 13968
            return work_sb[:, at:at + words]

        def scratch(at, words):
            assert at + words <= (SLOTS - DENSE_SLOTS) * SLOT
            return ring[:, DENSE_SLOTS * SLOT + at:DENSE_SLOTS * SLOT + at + words]

        def slot(i, k, n):
            return ring[:, i * SLOT:i * SLOT + k * n].rearrange("p (k n) -> p k n", k=k)

        small_used = [0]

        def tiny(words):
            at = small_used[0]
            small_used[0] += words
            assert small_used[0] <= 320
            return small[:, at:at + words]

        def const(name, *shape):
            at, w = CONST_AT[name]
            return const_sb[:, at:at + w]

        def tiles(ap, t=T):
            return ap.rearrange("p (t n) -> p t n", t=t)

        def over(ap, position, size):
            ap = ap.unsqueeze(position)
            shape = list(ap.shape)
            shape[position] = size
            return ap.to_broadcast(shape)

        le, ge, gt, lt, ident, ones = (const(c) for c in ("le", "ge", "gt", "lt", "ident", "ones"))
        window, causal = tiles(const("window")), tiles(const("causal"))
        swa_cos, swa_sin = tiles(const("swa_cos")), tiles(const("swa_sin"))
        lb_at = CONST_AT["window"][0]
        log_lb, log_rest = const_sb[:, lb_at:lb_at + 512], const_sb[:, lb_at + 512:lb_at + 1024]
        iota, inv_freq = const("iota"), const("inv_freq")
        x, h = tiles(x_sb[:, :]), tiles(h_sb[:, :])
        hT = tiles(hT_sb[:, :], KD)

        norms = ("f0", "f1", "l0", "g0", "l1", "g1")
        gain_T = {n: tiny(KD) for n in norms}
        c_gain = [tiny(5) for _ in range(2)]
        ss, ms, rinv = tiny(T), tiny(T), tiny(T)
        head_ms, head_rinv = tiny(20), tiny(20)
        row_max, sink_exp, row_sum, row_rec = tiny(16), tiny(16), tiny(16), tiny(16)
        sinks = tiny(SWA_HEADS)
        position = tiny(T).bitcast(I32)
        pos_f = tiny(T)
        router_w = tiles(tiny(KD * EXPERTS), KD)
        hg_gain = [more[:, 128 * i:128 * i + 128] for i in range(2)]
        rope_cos, rope_sin = tiles(more[:, 256:384]), tiles(more[:, 384:512])

        g_q, g_k, g_v = tiles(work(0, 1024)), tiles(work(1024, 1024)), tiles(work(2048, 2048))
        g_lg = work(4096, 2048).rearrange("p (a t n) -> p a t n", a=2, t=T)
        g_qT, g_kT = work(6144, 1024), work(7168, 1024)
        g_kt = tiles(work(8192, 1024))
        g_lrT = tiles(work(9216, 512)[0:GLA_RANK, :])
        g_lr = tiles(work(9728, 64))
        g_sr = h
        g_dec = [scratch(2048 * a, 1024) for a in range(2)]
        g_inv = [scratch(2048 * a + 1024, 1024) for a in range(2)]
        g_up = tiles(scratch(4096, 1024)[0:GLA_RANK, :])
        g_bias = tiles(scratch(6144, 1024)[0:1, :])
        g_sc = scratch(4096, 2048).rearrange("p (a t h c) -> p a t h c", a=2, t=T, h=GLA_HEADS)
        g_st = scratch(6144, 2048).rearrange("p (a h e) -> p a h e", a=2, h=GLA_HEADS)
        g_o = scratch(8192, 2048)
        g_tmp = scratch(0, 2048)
        g_gain = scratch(10240, 256)
        g_oT = tiles(work(4096, 2048), KD)
        s_qk = work(9856, 2560).rearrange("p (t h d) -> p t h d", t=T, h=10)
        s_qk_flat = tiles(work(9856, 2560))
        s_v = tiles(work(12416, 512))
        s_gain = tiles(work(12928, 256))
        s_a = scratch(0, 2560).rearrange("p (t h d) -> p t h d", t=T, h=10)
        s_b = scratch(2560, 2560).rearrange("p (t h d) -> p t h d", t=T, h=10)
        s_qkT = tiles(work(6144, 2560), 10)
        s_sc = scratch(4096, 4096).rearrange("p (t h k) -> p t h k", t=T, h=SWA_HEADS)
        s_pT = scratch(0, 4096).rearrange("p (t h b q) -> p t h b q", t=T, h=SWA_HEADS, b=2)
        s_o = tiles(scratch(8192, 2048))
        s_oT = tiles(scratch(10240, 2048), KD)
        gate_a, gate_b = tiles(work(0, 2048)), tiles(work(2048, 2048))
        y_gla, y_swa = tiles(work(9856, 2048)), tiles(work(4096, 2048))
        mT = hT
        f_silu = [work(512 * i, 512) for i in range(2)]
        f_hid = [work(1024 + 512 * i, 512) for i in range(2)]
        n_z, n_q, n_v, n_g, n_lf, n_k = (tiles(work(1024 * i, 1024)) for i in range(6))
        n_qT, n_kT, n_bT, n_at = (work(6144 + 1024 * i, 1024) for i in range(4))
        n_kt, n_st = work(10240, 512), work(10752, 512)
        n_c = tiles(work(11264, 1408))
        n_cT = tiles(work(12672, 1280), 5)
        n_tmp = [scratch(1024 * i, 1024) for i in range(4)]
        n_E, n_X = n_tmp[0:2], n_tmp[2:4]
        n_qd = scratch(4096, 512)
        n_qm, n_kvm = tiles(scratch(4608, 1536)), tiles(scratch(6144, 2048))
        n_mqT, n_mkT = tiles(scratch(8192, 1024), 4), tiles(scratch(9216, 1024), 4)
        n_pqT = tiles(scratch(10240, 1024)[0:ROPE, :], 4)
        n_pkT = scratch(11264, 256)[0:ROPE, :]
        n_sc = scratch(0, 2048).rearrange("p (t h k) -> p t h k", t=T, h=MLA_HEADS)
        n_pT = scratch(2048, 2048).rearrange("p (t h b q) -> p t h b q", t=T, h=MLA_HEADS, b=2)
        mix = h
        mixT = tiles(work(0, 2048), KD)
        e_logit, e_top, e_prob, e_mask, e_pos, e_oh0, e_oh1, e_idf = (tiles(work(16 * i, 16)) for i in range(8))
        e_idx = tiles(work(128, 16)).bitcast(U32)
        e_d, e_g0, e_g1, e_cnt, e_cntx = work(144, 2), work(146, 2), work(148, 2), work(150, 1), work(151, 2)
        e_rounds = work(153, 1).bitcast(I32)
        e_P, e_G = tiles(work(256, T * CAP)), tiles(work(448, T * CAP))
        e_GT = work(640, 256)[0:CAP, :]
        e_x = tiles(work(896, KD * CAP), KD)
        e_silu = [work(1664 + 384 * i, 384) for i in range(2)]
        e_hid = [tiles(work(2432 + 384 * i, 384), 4) for i in range(2)]
        e_y = work(3200, 1024)[0:CAP, :]
        fin_gain = work(4224, 1024)

        block = ctx.enter_context(nc.Block())
        dma = ctx.enter_context(nc.allow_non_contiguous_dma("vectors laid over partitions, small"))

        def expert_source(kind, e, s):
            cols = slice(s * FF_STEP, (s + 1) * FF_STEP)
            if kind == 2:
                return A["moe_w_down"][e, cols, :].rearrange("(k p) n -> p k n", p=P)
            w = A["moe_w_gate" if kind == 0 else "moe_w_up"]
            return w[e].rearrange("(k p) n -> p k n", p=P)[:, :, cols]

        EXPERT_DONE = ("expert_gate_done", "expert_up_done", "expert_down_done")

        @block.sync
        def _(sp):
            sp.dma_start(x, A["x"].rearrange("a (t p) d -> p (a t) d", p=P)).then_inc(sem("x_landed"), 16)
            for i, (name, src, (k, width), _) in enumerate(loads):
                if i >= DENSE_SLOTS:
                    sp.wait_ge(sem(loads[i - DENSE_SLOTS][3][0]), loads[i - DENSE_SLOTS][3][1])
                sp.dma_start(slot(slot_of[i], k, width), src).then_inc(sem(f"landed{slot_of[i]}"), 16)

            def load(e, i):
                k, width = ((KD, FF_STEP), (KD, FF_STEP), (FF_STEP // P, D))[i % 3]
                sp.dma_start(slot(i % SLOTS, k, width), expert_source(i % 3, e, i // 3)) \
                    .then_inc(sem(f"expert_landed{i % SLOTS}"), 16)

            def freed(it, i):
                sp.wait_ge(sem(EXPERT_DONE[i % 3]), it * MOE_STEPS + i // 3 + 1)

            def own(it, e):
                for i in range(SLOTS, MOE_LOADS):
                    freed(it, i - SLOTS)
                    load(e, i)

            def one_round(first):
                with sp.Fori(0, EXPERTS - 1) as e:
                    it = first + e
                    own(it, e)
                    for i in range(SLOTS):
                        freed(it, i + MOE_LOADS - SLOTS)
                        load(e + 1, i)
                own(first + EXPERTS - 1, EXPERTS - 1)

            for i in range(SLOTS):
                if i < DENSE_SLOTS:
                    last = len(loads) - DENSE_SLOTS + i
                    sp.wait_ge(sem(loads[last][3][0]), loads[last][3][1])
                else:
                    sp.wait_ge(sem("pair_read"), pair_end["mixT_1"])
                load(0, i)
            one_round(0)
            sp.wait_ge(sem("rounds_known"), 1)
            rounds = sp.value_load(e_rounds[0:1, 0:1], min_val=1, max_val=MAX_ROUNDS)
            with sp.If(rounds > 1):
                with sp.Fori(1, rounds) as r:
                    for i in range(SLOTS):
                        freed(r * EXPERTS - 1, i + MOE_LOADS - SLOTS)
                        load(0, i)
                    one_round(r * EXPERTS)
            sp.wait_ge(sem("result"), T)
            sp.dma_start(out.rearrange("a (t p) d -> p (a t) d", p=P), x).then_inc(sem("stored"), 16)
            sp.wait_ge(sem("stored"), 16)

        @block.gpsimd
        def _(pool):
            def column(dst, vec):
                pool.dma_start(dst, vec.rearrange("(k p) -> p k", p=P)).then_inc(sem("small_landed"), 16)

            def rows(dst, src, name="small_landed"):
                pool.dma_start(dst, src).then_inc(sem(name), 16)

            rows(const_sb[:, :], A["const_table"], "first_landed")
            rows(gain_T["f0"], A["norm_mix_g"][0].rearrange("(k p) -> p k", p=P), "first_landed")
            rows(level_masks[:, :], A["level_masks"])
            for a, d in enumerate(("fwd", "bwd")):
                rows(g_up[:, a, :], A[f"gla_gate_up_{d}"][0])
                rows(g_bias[:, a, :], A[f"gla_gate_bias_{d}"][0:1, :])
            rows(g_gain, A["gla_out_norm_g"].to_broadcast([P, GLA_DV]))
            rows(s_gain[:, 0, :], A["swa_q_norm_g"].to_broadcast([P, HD]))
            rows(s_gain[:, 1, :], A["swa_k_norm_g"].to_broadcast([P, HD]))
            rows(sinks, A["swa_sinks"].to_broadcast([P, SWA_HEADS]))
            column(gain_T["f1"], A["norm_ffn_g"][0])
            for l in range(2):
                column(gain_T[f"l{l}"], A["mix_norm_2"][l])
                column(gain_T[f"g{l}"], A["ffn_norm_2"][l])
                column(c_gain[l][:, 0:3], A["q_a_norm_2"][l])
                column(c_gain[l][:, 3:5], A["kv_a_norm_2"][l])
                rows(hg_gain[l], A["hg_out_norm_2"][l:l + 1, :].to_broadcast([P, P]))
            rows(position, A["positions_2"].rearrange("a (t p) -> p (a t)", p=P))
            rows(router_w, A["moe_router_2"][0].rearrange("(k p) e -> p k e", p=P))
            pool.wait_ge(sem("pair_read"), pair_end["so"])
            rows(log_lb, A["hg_lower_bounds_2"][0:1, :].to_broadcast([P, 512]), "bounds_landed")
            rows(log_rest, A["hg_lower_bounds_2"][1:2, :].to_broadcast([P, 512]), "bounds_landed")
            pool.wait_ge(sem("pair_read"), pair_end["hT_g1"])
            rows(fin_gain, A["final_norm_2"].rearrange("(a n) -> a n", a=1).to_broadcast([P, D]), "final_gain_landed")

        FIRST_LANDED = 32
        SMALL_LANDED = 16 * (1 + 4 + 1 + 2 + 1 + 1 + 10 + 2)

        @block.tensor
        def _(pe):
            def gemm(name, left):
                i = load_no[name]
                k_tiles, width = loads[i][2]
                w = slot(slot_of[i], k_tiles, width)
                pe.wait_ge(sem(f"landed{slot_of[i]}"), landed[i])
                for t in range(T):
                    j = gemm_at[name] + t
                    if j >= 4:
                        pe.wait_ge(sem("gemm_read"), j - 3)
                    for k in range(k_tiles):
                        mm = pe.matmul(gemm_bank[j % 4][:, 0:width], left(k, t), w[:, k, :],
                                       start=(k == 0), stop=(k == k_tiles - 1))
                    mm.then_inc(sem("gemm_done"), 1)

            def of(a):
                return lambda k, t: a[:, k, t * P:(t + 1) * P]

            def pair(name, i):
                j = pair_at[name] + i
                if j >= 4:
                    pe.wait_ge(sem("pair_read"), j - 3)
                return pair_bank[j % 4]

            def transpose_all(name, source, k_tiles, first=0):
                for i in range(-(-k_tiles // 2)):
                    b = pair(name, first + i)
                    for k in range(2 * i, min(2 * i + 2, k_tiles)):
                        for t in range(T):
                            at = (k % 2) * TOKENS + t * P
                            tr = pe.transpose(b[:, at:at + P], source(k, t), ident)
                    tr.then_inc(sem("pair_full"), 1)

            def natural(a):
                return lambda k, t: a[:, t, k * P:(k + 1) * P]

            def transpose_heads(name, a):
                for t in range(T):
                    b = pair(name, t)
                    for i in range(4):
                        tr = pe.transpose(b[:, i * P:(i + 1) * P], a[:, t, i * P:(i + 1) * P], ident)
                    tr.then_inc(sem("pair_full"), 1)

            def normed(tag):
                pe.wait_ge(sem(f"h_{tag}"), T)
                transpose_all(f"hT_{tag}", natural(h), KD)

            pe.wait_ge(sem("first_landed"), FIRST_LANDED)
            normed("f0")
            pe.wait_ge(sem("pair_read"), pair_end["hT_f0"])
            gemm("gk", of(hT))
            gemm("gq", of(hT))
            gemm("lr", of(hT))
            pe.wait_ge(sem("gemm_read"), gemm_at["lr"] + T)
            b = pair("lrT", 0)
            for a in range(2):
                for t in range(T):
                    at = a * TOKENS + t * P
                    tr = pe.transpose(b[0:GLA_RANK, at:at + P], g_lr[:, t, a * GLA_RANK:(a + 1) * GLA_RANK], ident)
            tr.then_inc(sem("pair_full"), 1)
            gemm("gv0", of(hT))
            pe.wait_ge(sem("small_landed"), SMALL_LANDED)
            pe.wait_ge(sem("pair_read"), pair_end["lrT"])
            for a in range(2):
                for t in range(T):
                    b = pair("z", 2 * a + t)
                    pe.matmul(b[:, :], g_lrT[:, a, t * P:(t + 1) * P], g_up[:, a, :], start=True, stop=False)
                    pe.matmul(b[:, :], ones[0:1, :], g_bias[:, a, :], start=False, stop=True) \
                        .then_inc(sem("pair_full"), 1)
            transpose_heads("gqT", g_q)
            transpose_heads("gkT", g_k)
            gemm("gv1", of(hT))
            pe.wait_ge(sem("g_lg_ready"), 2)
            for a in range(2):
                for t in range(T):
                    b = pair("gb", 2 * a + t)
                    for i in range(GLA_HEADS):
                        mm = pe.matmul(b[:, i * P:(i + 1) * P], g_lg[:, a, t, i * P:(i + 1) * P], (le, ge)[a],
                                       start=True, stop=True)
                    mm.then_inc(sem("pair_full"), 1)
            for a in range(2):
                pe.matmul(pair("tail", a)[:, :], (gt, lt)[a], g_lg[:, a, a, :], start=True, stop=True) \
                    .then_inc(sem("pair_full"), 1)
            gemm("gr0", of(hT))
            gemm("gr1", of(hT))
            for a in range(2):
                pe.wait_ge(sem("g_dec_ready"), a + 1)
                pe.wait_ge(sem("g_inv_ready"), a + 1)
                for t in range(T):
                    b = pair("gsc", 2 * a + t)
                    for i in range(GLA_HEADS):
                        at = (t * GLA_HEADS + i) * P
                        mm = pe.matmul(b[:, i * P:(i + 1) * P], g_inv[a][:, at:at + P], g_dec[a][:, at:at + P],
                                       start=True, stop=True)
                    mm.then_inc(sem("pair_full"), 1)
            pe.wait_ge(sem("g_kt_ready"), 2)
            for a in range(2):
                for half in range(2):
                    b = pair("gst", 2 * a + half)
                    for i in range(2):
                        head = 2 * half + i
                        mm = pe.matmul(b[:, i * GLA_DV:(i + 1) * GLA_DV], g_kt[:, a, head * P:(head + 1) * P],
                                       g_v[:, a, head * GLA_DV:(head + 1) * GLA_DV], start=True, stop=True)
                    mm.then_inc(sem("pair_full"), 1)
            gemm("sq0", of(hT))
            gemm("sq1", of(hT))
            pe.wait_ge(sem("pair_read"), pair_end["gst"])
            for t in range(T):
                for half in range(2):
                    b = pair("go", 2 * t + half)
                    for i in range(2):
                        head = 2 * half + i
                        values = g_v[:, t, head * GLA_DV:(head + 1) * GLA_DV]
                        o = b[:, i * GLA_DV:(i + 1) * GLA_DV]
                        a = 1 - t
                        at = (t * GLA_HEADS + head) * P
                        pe.matmul(o, g_sc[:, 0, t, head, :], values, start=True, stop=False)
                        pe.matmul(o, g_sc[:, 1, t, head, :], values, start=False, stop=False)
                        mm = pe.matmul(o, g_dec[a][:, at:at + P], g_st[:, a, head, :], start=False, stop=True)
                    mm.then_inc(sem("pair_full"), 1)
            gemm("skv", of(hT))
            gemm("ga0", of(hT))
            gemm("ga1", of(hT))
            pe.wait_ge(sem("g_out"), 1)
            transpose_all("goT", natural(tiles(g_o)), KD)
            pe.wait_ge(sem("s_rot"), T)
            transpose_all("sT", lambda k, t: s_a[:, t, k, :], 10)
            gemm("gb0", of(hT))
            gemm("gb1", of(hT))
            pe.wait_ge(sem("pair_read"), pair_end["sT"])
            for t in range(T):
                for i in range(SWA_HEADS // 2):
                    b = pair("ssc", 4 * t + i)
                    for j in range(2):
                        head = 2 * i + j
                        kv = SWA_HEADS + head // (SWA_HEADS // SWA_KV)
                        mm = pe.matmul(b[:, j * TOKENS:(j + 1) * TOKENS], s_qkT[:, head, t * P:(t + 1) * P],
                                       s_qkT[:, kv, :], start=True, stop=True)
                    mm.then_inc(sem("pair_full"), 1)
            gemm("og0", of(g_oT))
            gemm("og1", of(g_oT))

            def attend(names, scores, weightsT, values, heads):
                pe.wait_ge(sem(names[2]), T * heads)
                for t in range(T):
                    for i in range(heads // 2):
                        b = pair(names[0], t * heads // 2 + i)
                        for j in range(2):
                            for kt in range(2):
                                at = (2 * j + kt) * P
                                tr = pe.transpose(b[:, at:at + P], scores[:, t, 2 * i + j, kt * P:(kt + 1) * P], ident)
                        tr.then_inc(sem("pair_full"), 1)
                pe.wait_ge(sem("pair_read"), pair_end[names[0]])
                for t in range(T):
                    for i in range(heads // 4):
                        b = pair(names[1], t * heads // 4 + i)
                        for j in range(4):
                            for kt in range(2):
                                mm = pe.matmul(b[:, j * P:(j + 1) * P], weightsT[:, t, 4 * i + j, kt, :],
                                               values(kt, 4 * i + j), start=(kt == 0), stop=(kt == 1))
                        mm.then_inc(sem("pair_full"), 1)

            attend(("sP", "so", "s_exp"), s_sc, s_pT,
                   lambda kt, head: s_v[:, kt, (head // 4) * HD:(head // 4 + 1) * HD], SWA_HEADS)
            pe.wait_ge(sem("pair_read"), pair_end["so"])
            transpose_all("soT", natural(s_o), KD)
            pe.wait_ge(sem("pair_read"), pair_end["soT"])
            gemm("os0", of(s_oT))
            gemm("os1", of(s_oT))
            pe.wait_ge(sem("merged"), 1)
            transpose_all("mT", natural(y_gla), KD)
            pe.wait_ge(sem("pair_read"), pair_end["mT"])
            gemm("wo0", of(mT))
            gemm("wo1", of(mT))

            def ffn(tag, norm):
                def down(u, last):
                    s, i0 = divmod(u, 2)
                    size = ffn_steps[s]
                    i = load_no[f"{tag}_down{s}"]
                    pe.wait_ge(sem(f"landed{slot_of[i]}"), landed[i])
                    pe.wait_ge(sem(f"{tag}_hid"), u + 1)
                    w = slot(slot_of[i], size // P, D)
                    hid = tiles(f_hid[u % 2])
                    for j in range(2):
                        for t in range(T):
                            for half in range(2):
                                mm = pe.matmul(pair_bank[2 * t + half][:, :], hid[:, j, t * P:(t + 1) * P],
                                               w[:, 2 * i0 + j, half * 512:(half + 1) * 512],
                                               start=(u == 0 and j == 0), stop=(last and j == 1))
                    mm.then_inc(sem(f"{tag}_down_done"), 1)

                pe.wait_ge(sem("pair_read"), pair_end[f"hT_{norm}"])
                for u in range(FFN_UNITS):
                    s, i0 = divmod(u, 2)
                    for kind in range(2):
                        name = ("gate", "up")[kind]
                        i = load_no[f"{tag}_{name}{s}"]
                        w = slot(slot_of[i], KD, ffn_steps[s])
                        pe.wait_ge(sem(f"landed{slot_of[i]}"), landed[i])
                        if u >= 2:
                            pe.wait_ge(sem(f"{tag}_hid"), u - 1)
                        b = gemm_bank[2 * (u % 2) + kind]
                        for j in range(2):
                            at = (2 * i0 + j) * P
                            for k in range(KD):
                                mm = pe.matmul(b[:, j * TOKENS:(j + 1) * TOKENS], w[:, k, at:at + P], hT[:, k, :],
                                               start=(k == 0), stop=(k == KD - 1))
                        mm.then_inc(sem(f"{tag}_{name}_done"), 1)
                    if u >= 1:
                        down(u - 1, False)
                down(FFN_UNITS - 1, True)

            pe.wait_ge(sem("gemm_read"), gemm_at["wo1"] + T)
            normed("f1")
            ffn("f1", "f1")

            for l in range(2):
                if l == 1:
                    pe.wait_ge(sem("f2_hid"), FFN_UNITS)
                normed(f"l{l}")
                pe.wait_ge(sem("pair_read"), pair_end[f"hT_l{l}"])
                for name in ("hf", "c0", "c1", "hi", "hq", "hg"):
                    gemm(f"{name}_{l}", of(hT))
                pe.wait_ge(sem(f"n_k_ready_{l}"), 1)
                transpose_heads(f"hkT_{l}", n_k)
                pe.wait_ge(sem(f"n_lf_ready_{l}"), 1)
                for t in range(T):
                    b = pair(f"hb_{l}", t)
                    for i in range(HG_HEADS):
                        mm = pe.matmul(b[:, i * P:(i + 1) * P], n_lf[:, t, i * P:(i + 1) * P], le,
                                       start=True, stop=True)
                    mm.then_inc(sem("pair_full"), 1)
                pe.matmul(pair(f"ht_{l}", 0)[:, :], gt, n_lf[:, 0, :], start=True, stop=True) \
                    .then_inc(sem("pair_full"), 1)
                pe.wait_ge(sem(f"c_normed_{l}"), T * 2)
                transpose_all(f"cT_{l}", natural(n_c), 5)
                pe.wait_ge(sem("gemm_read"), gemm_at[f"hg_{l}"] + T)
                transpose_heads(f"hqT_{l}", n_q)
                pe.wait_ge(sem("pair_read"), pair_end[f"cT_{l}"])
                for i in range(2):
                    gemm(f"qb{i}_{l}", of(n_cT))
                for i in range(2):
                    gemm(f"kvb{i}_{l}", lambda k, t: n_cT[:, 3 + k, t * P:(t + 1) * P])
                pe.wait_ge(sem("pair_read"), pair_end[f"hqT_{l}"])
                for n in range(len(LEVELS) + 1):
                    if n:
                        pe.wait_ge(sem(f"level_ready_{l}"), 2 * n)
                    for t in range(T):
                        b = pair(f"hlev_{l}", T * n + t)
                        for i in range(HG_HEADS):
                            at = (t * HG_HEADS + i) * P
                            key, query = (n_X[n % 2], n_X[n % 2]) if n else (n_kT, n_qT)
                            mm = pe.matmul(b[:, i * P:(i + 1) * P], key[:, at:at + P], query[:, at:at + P],
                                           start=True, stop=True)
                        mm.then_inc(sem("pair_full"), 1)
                pe.wait_ge(sem(f"n_kt_ready_{l}"), 1)
                b = pair(f"hst_{l}", 0)
                for i in range(HG_HEADS):
                    mm = pe.matmul(b[:, i * P:(i + 1) * P], n_kt[:, i * P:(i + 1) * P], n_v[:, 0, i * P:(i + 1) * P],
                                   start=True, stop=True)
                mm.then_inc(sem("pair_full"), 1)
                pe.wait_ge(sem("pair_read"), pair_end[f"hst_{l}"])
                pe.wait_ge(sem(f"n_qd_ready_{l}"), 1)
                for t in range(T):
                    b = pair(f"ho_{l}", t)
                    for i in range(HG_HEADS):
                        at = (t * HG_HEADS + i) * P
                        mm = pe.matmul(b[:, i * P:(i + 1) * P], n_at[:, at:at + P], n_v[:, t, i * P:(i + 1) * P],
                                       start=True, stop=(t == 0))
                        if t == 1:
                            mm = pe.matmul(b[:, i * P:(i + 1) * P], n_qd[:, i * P:(i + 1) * P],
                                           n_st[:, i * P:(i + 1) * P], start=False, stop=True)
                    mm.then_inc(sem("pair_full"), 1)
                pe.wait_ge(sem(f"m_rot_{l}"), 2 * T)
                transpose_all(f"mqT_{l}", lambda k, t: n_qm[:, t, k * 192:k * 192 + NOPE], MLA_HEADS)
                transpose_all(f"mkT_{l}", lambda k, t: n_kvm[:, t, k * 256:k * 256 + NOPE], MLA_HEADS)
                for i in range(3):
                    b = pair(f"mpT_{l}", i)
                    for k in range(2 * i, min(2 * i + 2, MLA_HEADS + 1)):
                        for t in range(T):
                            src = n_qm[:, t, k * 192 + NOPE:(k + 1) * 192] if k < MLA_HEADS \
                                else n_c[:, t, Q_RANK + KV_RANK:Q_RANK + KV_RANK + ROPE]
                            at = (k % 2) * TOKENS + t * P
                            tr = pe.transpose(b[0:ROPE, at:at + P], src, ident)
                    tr.then_inc(sem("pair_full"), 1)
                pe.wait_ge(sem("pair_read"), pair_end[f"mpT_{l}"])
                for t in range(T):
                    for i in range(MLA_HEADS // 2):
                        b = pair(f"msc_{l}", 2 * t + i)
                        for j in range(2):
                            head = 2 * i + j
                            o = b[:, j * TOKENS:(j + 1) * TOKENS]
                            pe.matmul(o, n_mqT[:, head, t * P:(t + 1) * P], n_mkT[:, head, :], start=True, stop=False)
                            mm = pe.matmul(o, n_pqT[:, head, t * P:(t + 1) * P], n_pkT, start=False, stop=True)
                        mm.then_inc(sem("pair_full"), 1)
                attend((f"mP_{l}", f"mo_{l}", f"m_exp_{l}"), n_sc, n_pT,
                       lambda kt, head: n_kvm[:, kt, head * 256 + NOPE:(head + 1) * 256], MLA_HEADS)
                pe.wait_ge(sem(f"hg_mixed_{l}"), T)
                pe.wait_ge(sem("pair_read"), pair_end[f"mo_{l}"])
                transpose_all(f"mixT_{l}", natural(mix), KD)
                pe.wait_ge(sem("pair_read"), pair_end[f"mixT_{l}"])
                for i in range(2):
                    gemm(f"wo{i}_{l}", of(mixT))
                pe.wait_ge(sem("gemm_read"), gemm_at[f"wo1_{l}"] + T)
                normed(f"g{l}")
                if l == 0:
                    ffn("f2", "g0")

            pe.wait_ge(sem("pair_read"), pair_end["hT_g1"])
            b = pair("router", 0)
            for t in range(T):
                for k in range(KD):
                    mm = pe.matmul(b[:, t * EXPERTS:(t + 1) * EXPERTS], hT[:, k, t * P:(t + 1) * P], router_w[:, k, :],
                                   start=(k == 0), stop=(k == KD - 1))
            mm.then_inc(sem("pair_full"), 1)
            pe.wait_ge(sem("e_mask_ready"), 1)
            b = pair("ranks", 0)
            pe.matmul(b[:, 0:8], lt, e_mask[:, 0, :], start=True, stop=True)
            pe.matmul(b[:, 8:16], ones, e_mask[:, 0, :], start=True, stop=False)
            pe.matmul(b[:, 8:16], lt, e_mask[:, 1, :], start=False, stop=True)
            pe.matmul(b[:, 16:24], ones, e_mask[:, 0, :], start=True, stop=False)
            pe.matmul(b[:, 16:24], ones, e_mask[:, 1, :], start=False, stop=True).then_inc(sem("pair_full"), 1)
            pe.wait_ge(sem("pair_read"), pair_end["ranks"])

            def expert(it):
                y_bank, misc = pair_bank[0:2], pair_bank[2:4]
                pe.wait_ge(sem("e_placed"), 2 * T * it + 2 * T)
                for i in range(2):
                    for k in range(4 * i, 4 * i + 4):
                        for t in range(T):
                            mm = pe.matmul(misc[i][:, (k % 4) * CAP:(k % 4 + 1) * CAP], h[:, t, k * P:(k + 1) * P],
                                           e_P[:, t, :], start=(t == 0), stop=(t == T - 1))
                    mm.then_inc(sem("e_gathered"), 1)
                for t in range(T):
                    tr = pe.transpose(y_bank[0][0:CAP, t * P:(t + 1) * P], e_G[:, t, :], ident)
                tr.then_inc(sem("e_turned"), 1)
                pe.wait_ge(sem("e_x_ready"), 2 * it + 2)

                def down(s):
                    i = 3 * s + 2
                    w = slot(i % SLOTS, FF_STEP // P, D)
                    pe.wait_ge(sem(f"expert_landed{i % SLOTS}"), it * 48 + 16 * (i // SLOTS + 1))
                    pe.wait_ge(sem("e_hid_ready"), it * MOE_STEPS + s + 1)
                    if s == 0:
                        pe.wait_ge(sem("e_GT_ready"), it + 1)
                    for j in range(4):
                        for half in range(2):
                            mm = pe.matmul(y_bank[half][0:CAP, :], e_hid[s % 2][:, j, :],
                                           w[:, j, half * 512:(half + 1) * 512],
                                           start=(s == 0 and j == 0), stop=(s == MOE_STEPS - 1 and j == 3))
                    mm.then_inc(sem("expert_down_done"), 1)

                for s in range(MOE_STEPS):
                    for kind in range(2):
                        i = 3 * s + kind
                        w = slot(i % SLOTS, KD, FF_STEP)
                        pe.wait_ge(sem(f"expert_landed{i % SLOTS}"), it * 48 + 16 * (i // SLOTS + 1))
                        if s >= 2:
                            pe.wait_ge(sem("e_hid_ready"), it * MOE_STEPS + s - 1)
                        b = gemm_bank[2 * (s % 2) + kind]
                        for j in range(4):
                            for k in range(KD):
                                mm = pe.matmul(b[:, j * CAP:(j + 1) * CAP], w[:, k, j * P:(j + 1) * P], e_x[:, k, :],
                                               start=(k == 0), stop=(k == KD - 1))
                        mm.then_inc(sem(EXPERT_DONE[kind]), 1)
                    if s:
                        down(s - 1)
                down(MOE_STEPS - 1)
                pe.wait_ge(sem("e_y_ready"), 2 * it + 2)
                for q in range(4):
                    t, half = divmod(q, 2)
                    if q >= 2:
                        pe.wait_ge(sem("e_added"), 4 * it + q - 1)
                    pe.matmul(misc[q % 2][:, :], e_GT[:, t * P:(t + 1) * P], e_y[:, half * 512:(half + 1) * 512],
                              start=True, stop=True).then_inc(sem("e_scattered"), 1)
                pe.wait_ge(sem("e_added"), 4 * it + 4)

            with pe.Fori(0, EXPERTS) as e:
                expert(e)
            pe.wait_ge(sem("rounds_known"), 1)
            rounds = pe.value_load(e_rounds[0:1, 0:1], min_val=1, max_val=MAX_ROUNDS)
            with pe.If(rounds > 1):
                with pe.Fori(1, rounds) as r:
                    with pe.Fori(0, EXPERTS) as e:
                        expert(r * EXPERTS + e)

        @block.scalar
        def _(act):
            told = counter()

            def link(instruction):
                instruction.then_inc(sem("scalar_step"), 1)
                act.wait_ge(sem("scalar_step"), told("scalar_step"))

            def norm(tag, ready):
                act.wait_ge(sem(ready[0]), ready[1])
                for t in range(T):
                    act.activation(h[:, t, :], x[:, t, :], ACT.Square, accum_out=ss[:, t:t + 1]) \
                        .then_inc(sem(f"ss_{tag}"), 1)
                    act.wait_ge(sem(f"ss_{tag}"), told(f"ss_{tag}"))
                act.wait_ge(sem(f"ms_{tag}"), 1)
                link(act.activation(rinv, ms, ACT.Ln))
                act.activation(rinv, rinv, ACT.Exp, scale=-0.5).then_inc(sem(f"rinv_{tag}"), 1)
                act.wait_ge(sem(f"rinv_{tag}"), told(f"rinv_{tag}"))

            def evacuate(name, parts):
                for t in range(T):
                    j = gemm_at[name] + t
                    act.wait_ge(sem("gemm_done"), j + 1)
                    todo = parts(t)
                    for n, (dst, lo, hi, func, scale) in enumerate(todo):
                        ins = act.activation(dst, gemm_bank[j % 4][:, lo:hi], func, scale=scale)
                        if n == len(todo) - 1:
                            ins.then_inc(sem("gemm_read"), 1)

            def into(dst, at, width=512, func=ACT.Copy, scale=1.0):
                return lambda t: [(dst[:, t, at:at + width], 0, width, func, scale)]

            norm("f0", ("x_landed", 16))
            evacuate("gk", into(g_k, 0))
            evacuate("gq", into(g_q, 0, scale=GLA_DK ** -0.5))
            evacuate("lr", into(g_lr, 0, 2 * GLA_RANK))
            evacuate("gv0", into(g_v, 0))
            for d in range(2):
                act.wait_ge(sem("pair_read"), pair_at["z"] + 2 * d + 2)
                link(act.activation(g_lg[:, d, :, :], g_lg[:, d, :, :], ACT.Exp, scale=-1.0))
                act.activation(g_lg[:, d, :, :], g_lg[:, d, :, :], ACT.Ln, bias=1.0).then_inc(sem("g_soft"), 1)
                act.wait_ge(sem("g_soft"), told("g_soft"))
            evacuate("gv1", into(g_v, 512))
            for d in range(2):
                act.wait_ge(sem("pair_read"), pair_at["gb"] + 2 * d + 2)
                link(act.activation(g_inv[d], g_dec[d], ACT.Exp, scale=-1.0))
                act.activation(g_dec[d], g_dec[d], ACT.Exp).then_inc(sem("g_exp"), 1)
                act.wait_ge(sem("g_exp"), told("g_exp"))
            for d in range(2):
                act.wait_ge(sem("pair_read"), pair_at["tail"] + d + 1)
                act.activation(g_kt[:, d, :], g_kt[:, d, :], ACT.Exp).then_inc(sem("g_tail_exp"), 1)
                act.wait_ge(sem("g_tail_exp"), told("g_tail_exp"))
            for i in range(2):
                evacuate(f"gr{i}", into(g_sr, 512 * i, func=ACT.Silu))
            for i in range(2):
                evacuate(f"sq{i}", into(s_qk_flat, 512 * i))
            evacuate("skv", lambda t: [(s_qk_flat[:, t, 1024:1280], 0, 256, ACT.Copy, 1.0),
                                       (s_v[:, t, :], 256, 512, ACT.Copy, 1.0)])

            def head_norm(tag, n):
                act.wait_ge(sem(f"head_ms_{tag}"), 1)
                link(act.activation(head_rinv[:, 0:n], head_ms[:, 0:n], ACT.Ln))
                act.activation(head_rinv[:, 0:n], head_rinv[:, 0:n], ACT.Exp, scale=-0.5) \
                    .then_inc(sem(f"head_rinv_{tag}"), 1)
                act.wait_ge(sem(f"head_rinv_{tag}"), told(f"head_rinv_{tag}"))

            head_norm("g", 8)
            act.wait_ge(sem("g_out"), 1)
            for i in range(2):
                evacuate(f"ga{i}", into(gate_a, 512 * i, func=ACT.Sigmoid))
            head_norm("s", 20)
            for i in range(2):
                evacuate(f"gb{i}", into(gate_b, 512 * i, func=ACT.Sigmoid))

            def softmax(scores, heads, negmax, ready, done, sink=None):
                act.wait_ge(sem(ready), 1)
                if sink is not None:
                    link(act.activation(sink, sink, ACT.Exp))
                for t in range(T):
                    for i in range(heads):
                        at = t * heads + i
                        act.activation(scores[:, t, i, :], scores[:, t, i, :], ACT.Exp, bias=negmax[:, at:at + 1],
                                       accum_out=row_sum[:, at:at + 1]).then_inc(sem(done), 1)

            softmax(s_sc, SWA_HEADS, row_max, "s_max_ready", "s_exp", sink_exp)
            act.wait_ge(sem("pair_read"), pair_end["sT"])
            for i in range(2):
                evacuate(f"og{i}", into(y_gla, 512 * i))
            for i in range(2):
                evacuate(f"os{i}", into(y_swa, 512 * i))
            act.wait_ge(sem("merged"), 1)
            for i in range(2):
                evacuate(f"wo{i}", into(gate_a, 512 * i))

            def ffn(tag):
                for u in range(FFN_UNITS):
                    act.wait_ge(sem(f"{tag}_gate_done"), u + 1)
                    if u >= 2:
                        act.wait_ge(sem(f"{tag}_hid"), u - 1)
                    act.activation(f_silu[u % 2], gemm_bank[2 * (u % 2)][:, :], ACT.Silu) \
                        .then_inc(sem(f"{tag}_silu"), 1)

            norm("f1", ("x_mixed_f", T))
            ffn("f1")

            act.wait_ge(sem("angle_ready"), 2)
            link(act.activation(rope_sin[:, :, 32:64], rope_sin[:, :, 32:64], ACT.Sin))
            act.activation(rope_cos[:, :, 0:32], rope_cos[:, :, 0:32], ACT.Sin).then_inc(sem("sines"), 1)
            act.wait_ge(sem("sines"), told("sines"))

            for l in range(2):
                norm(f"l{l}", (f"x_ffn_{l}", 4))
                if l == 1:
                    act.wait_ge(sem("bound_abs"), 1)
                    link(act.activation(n_tmp[0][:, 0:512], n_tmp[0][:, 0:512], ACT.Exp, scale=-1.0))
                    act.activation(n_tmp[0][:, 0:512], n_tmp[0][:, 0:512], ACT.Ln, bias=1.0) \
                        .then_inc(sem("bound_soft"), 1)
                    act.wait_ge(sem("bound_soft"), told("bound_soft"))
                evacuate(f"hf_{l}", into(n_z, 0))
                act.wait_ge(sem(f"z_abs_{l}"), 1)
                link(act.activation(n_tmp[0], n_tmp[0], ACT.Exp, scale=-1.0))
                act.activation(n_tmp[0], n_tmp[0], ACT.Ln, bias=1.0).then_inc(sem(f"z_soft_{l}"), 1)
                act.wait_ge(sem(f"z_soft_{l}"), told(f"z_soft_{l}"))
                evacuate(f"c0_{l}", into(n_c, 0))
                evacuate(f"c1_{l}", into(n_c, 512, Q_RANK + KV_RANK + ROPE - 512))
                for t in range(T):
                    for n, (lo, hi) in enumerate(((0, Q_RANK), (Q_RANK, Q_RANK + KV_RANK))):
                        act.wait_ge(sem("gemm_read"), gemm_at[f"c1_{l}"] + T)
                        act.activation(n_tmp[3][:, lo:hi], n_c[:, t, lo:hi], ACT.Square,
                                       accum_out=head_ms[:, 8 + 2 * n + t:9 + 2 * n + t]) \
                                           .then_inc(sem(f"c_ss_{l}"), 1)
                        act.wait_ge(sem(f"c_ss_{l}"), told(f"c_ss_{l}"))
                if l == 1:
                    act.wait_ge(sem("mix_abs"), 1)
                    link(act.activation(n_tmp[1], n_tmp[1], ACT.Exp, scale=-1.0))
                    act.activation(n_tmp[1], n_tmp[1], ACT.Ln, bias=1.0).then_inc(sem("mix_soft"), 1)
                    act.wait_ge(sem("mix_soft"), told("mix_soft"))
                act.wait_ge(sem(f"ln_k_{l}"), 1)
                act.activation(n_k[:, :, :], n_k[:, :, :], ACT.Exp).then_inc(sem(f"n_k_ready_{l}"), 1)
                act.wait_ge(sem(f"n_k_ready_{l}"), told(f"n_k_ready_{l}"))
                act.wait_ge(sem(f"c_ms_{l}"), 1)
                link(act.activation(head_rinv[:, 8:12], head_ms[:, 8:12], ACT.Ln))
                act.activation(head_rinv[:, 8:12], head_rinv[:, 8:12], ACT.Exp, scale=-0.5) \
                    .then_inc(sem(f"c_rinv_{l}"), 1)
                act.wait_ge(sem(f"c_rinv_{l}"), told(f"c_rinv_{l}"))
                evacuate(f"hi_{l}", into(n_v, 0))
                evacuate(f"hq_{l}", into(n_q, 0, func=ACT.Silu))
                evacuate(f"hg_{l}", into(n_g, 0, func=ACT.Silu))
                act.wait_ge(sem("pair_read"), pair_end[f"ht_{l}"])
                act.activation(n_kt, n_kt, ACT.Exp).then_inc(sem(f"n_tail_exp_{l}"), 1)
                act.wait_ge(sem(f"n_tail_exp_{l}"), told(f"n_tail_exp_{l}"))
                act.activation(n_qd, n_bT[:, 512:1024], ACT.Exp).then_inc(sem(f"n_qd_exp_{l}"), 1)
                act.wait_ge(sem(f"n_qd_exp_{l}"), told(f"n_qd_exp_{l}"))
                for i in range(2):
                    evacuate(f"qb{i}_{l}", into(n_qm, 384 * i, 384))
                for i in range(2):
                    evacuate(f"kvb{i}_{l}", into(n_kvm, 512 * i))
                for n in range(1, len(LEVELS) + 1):
                    half = LEVELS[n - 1]
                    E = n_E[n % 2].rearrange("p (n s c) -> p n s c", s=2, c=half)
                    X = n_X[n % 2].rearrange("p (n s c) -> p n s c", s=2, c=half)
                    act.wait_ge(sem(f"level_diff_{l}"), n)
                    if n >= 3:
                        act.wait_ge(sem("pair_full"), pair_at[f"hlev_{l}"] + T * (n - 1))
                    act.activation(X[:, :, 0, :], E[:, :, 0, :], ACT.Exp, scale=-1.0) \
                        .then_inc(sem(f"level_exp_{l}"), 1)
                    act.wait_ge(sem(f"level_exp_{l}"), told(f"level_exp_{l}"))
                    act.activation(X[:, :, 1, :], E[:, :, 1, :], ACT.Exp).then_inc(sem(f"level_exp_{l}"), 1)
                    act.wait_ge(sem(f"level_exp_{l}"), told(f"level_exp_{l}"))
                head_norm(f"h{l}", 8)
                softmax(n_sc, MLA_HEADS, row_max, f"m_max_ready_{l}", f"m_exp_{l}")
                act.wait_ge(sem("pair_read"), pair_end[f"mixT_{l}"])
                for i in range(2):
                    evacuate(f"wo{i}_{l}", into(tiles(work(4096, 2048)), 512 * i))
                norm(f"g{l}", (f"x_mixed_{l}", T))
                if l == 0:
                    ffn("f2")

            act.wait_ge(sem("e_gap"), 1)
            act.activation(e_g1, e_d, ACT.Exp).then_inc(sem("e_odds"), 1)
            act.wait_ge(sem("e_odds"), told("e_odds"))

            def expert(it):
                for s in range(MOE_STEPS):
                    act.wait_ge(sem("expert_gate_done"), it * MOE_STEPS + s + 1)
                    if s >= 2:
                        act.wait_ge(sem("e_hid_ready"), it * MOE_STEPS + s - 1)
                    act.activation(e_silu[s % 2], gemm_bank[2 * (s % 2)][:, 0:4 * CAP], ACT.Silu) \
                        .then_inc(sem("e_silu_ready"), 1)

            with act.Fori(0, EXPERTS) as e:
                expert(e)
            act.wait_ge(sem("rounds_known"), 1)
            rounds = act.value_load(e_rounds[0:1, 0:1], min_val=1, max_val=MAX_ROUNDS)
            with act.If(rounds > 1):
                with act.Fori(1, rounds) as r:
                    with act.Fori(0, EXPERTS) as e:
                        expert(r * EXPERTS + e)
            act.wait_ge(sem("x_complete"), 1)
            for t in range(T):
                act.activation(h[:, t, :], x[:, t, :], ACT.Square, accum_out=ss[:, t:t + 1]) \
                    .then_inc(sem("ss_last"), 1)
                act.wait_ge(sem("ss_last"), told("ss_last"))
            act.wait_ge(sem("ms_last"), 1)
            link(act.activation(rinv, ms, ACT.Ln))
            act.activation(rinv, rinv, ACT.Exp, scale=-0.5).then_inc(sem("rinv_last"), 1)
            act.wait_ge(sem("rinv_last"), told("rinv_last"))

        @block.vector
        def _(dve):
            told = counter()

            def link(instruction):
                instruction.then_inc(sem("vector_step"), 1)
                dve.wait_ge(sem("vector_step"), told("vector_step"))
            TWO_PI = 2 * np.pi

            def bank_of(name, i):
                j = pair_at[name] + i
                dve.wait_ge(sem("pair_full"), j + 1)
                return pair_bank[j % 4]

            def copy_out(name, i, dst, rows=P, width=512):
                dve.tensor_copy(dst, bank_of(name, i)[0:rows, 0:width]).then_inc(sem("pair_read"), 1)
                dve.wait_ge(sem("pair_read"), told("pair_read"))

            def mul(dst, one, two, name="vector_step"):
                dve.tensor_tensor(dst, one, two, ALU.mult).then_inc(sem(name), 1)
                dve.wait_ge(sem(name), told(name))

            def mean(dst, src, count, name):
                dve.tensor_scalar(dst, src, 1.0 / count, EPS, ALU.mult, ALU.add).then_inc(sem(name), 1)
                dve.wait_ge(sem(name), told(name))

            def negate(dst, src, name="vector_step"):
                dve.tensor_scalar(dst, src, -1.0, None, ALU.mult).then_inc(sem(name), 1)
                dve.wait_ge(sem(name), told(name))

            def absolute(dst, src, name="vector_step"):
                dve.scalar_tensor_tensor(dst, src, -1.0, src, ALU.mult, ALU.max).then_inc(sem(name), 1)
                dve.wait_ge(sem(name), told(name))

            def norm(tag):
                dve.wait_ge(sem(f"ss_{tag}"), T)
                mean(ms, ss, D, f"ms_{tag}")
                dve.wait_ge(sem(f"rinv_{tag}"), 1)
                for t in range(T):
                    dve.tensor_scalar(h[:, t, :], x[:, t, :], rinv[:, t:t + 1], None, ALU.mult) \
                        .then_inc(sem(f"h_{tag}"), 1)
                    dve.wait_ge(sem(f"h_{tag}"), told(f"h_{tag}"))
                for i in range(KD // 2):
                    b = tiles(bank_of(f"hT_{tag}", i)[:, :], 2)
                    mul(hT[:, 2 * i:2 * i + 2, :], b, over(gain_T[tag][:, 2 * i:2 * i + 2], 2, TOKENS), "pair_read")

            dve.wait_ge(sem("first_landed"), FIRST_LANDED)
            norm("f0")
            copy_out("lrT", 0, g_lrT[:, :, :].rearrange("p a c -> p (a c)"), GLA_RANK)
            for a in range(2):
                for t in range(T):
                    b = bank_of("z", 2 * a + t)
                    dve.tensor_scalar(g_lg[:, a, t, :], b[:, :], -30.0, None, ALU.max).then_inc(sem("pair_read"), 1)
                    dve.wait_ge(sem("pair_read"), told("pair_read"))
            for t in range(T):
                copy_out("gqT", t, g_qT[:, t * 512:(t + 1) * 512])
            for t in range(T):
                copy_out("gkT", t, g_kT[:, t * 512:(t + 1) * 512])
            for a in range(2):
                dve.wait_ge(sem("g_soft"), a + 1)
                dve.tensor_scalar(g_lg[:, a, :, :], g_lg[:, a, :, :], -1.0 / 16, -0.5, ALU.mult, ALU.max) \
                    .then_inc(sem("g_lg_ready"), 1)
                dve.wait_ge(sem("g_lg_ready"), told("g_lg_ready"))
            for a in range(2):
                for t in range(T):
                    copy_out("gb", 2 * a + t, g_dec[a][:, t * 512:(t + 1) * 512])
            for a in range(2):
                copy_out("tail", a, g_kt[:, a, :])
            for a in range(2):
                dve.wait_ge(sem("g_exp"), a + 1)
                mul(g_inv[a], g_inv[a], g_kT, "g_inv_ready")
                mul(g_dec[a], g_dec[a], g_qT, "g_dec_ready")
            for a in range(2):
                dve.wait_ge(sem("g_tail_exp"), a + 1)
                mul(g_kt[:, a, :], g_kt[:, a, :], g_k[:, a, :], "g_kt_ready")
            for a in range(2):
                for t in range(T):
                    b = tiles(bank_of("gsc", 2 * a + t)[:, :], 4)
                    mul(g_sc[:, a, t, :, :], b, over((le, gt)[a], 1, 4), "pair_read")
            for i in range(4):
                copy_out("gst", i, g_st[:, i // 2, 2 * (i % 2):2 * (i % 2) + 2, :].rearrange("p h e -> p (h e)"))
            dve.wait_ge(sem("small_landed"), SMALL_LANDED)
            dve.wait_ge(sem("gemm_read"), gemm_at["gr1"] + T)
            for t in range(T):
                silu = g_sr[:, t, :].rearrange("p (h e) -> p h e", e=GLA_DV)
                mul(silu, silu, over(g_gain, 1, GLA_HEADS))
            for i in range(4):
                copy_out("go", i, g_o[:, i * 512:(i + 1) * 512])
            heads = g_o.rearrange("p (g e) -> p g e", e=GLA_DV)
            mul(g_tmp, g_o, g_o)
            link(dve.tensor_reduce(head_ms[:, 0:8], g_tmp.rearrange("p (g e) -> p g e", e=GLA_DV), AX_X, ALU.add))
            mean(head_ms[:, 0:8], head_ms[:, 0:8], GLA_DV, "head_ms_g")
            dve.wait_ge(sem("head_rinv_g"), 1)
            mul(heads, heads, over(head_rinv[:, 0:8], 2, GLA_DV))
            mul(g_o, g_o, h_sb[:, :], "g_out")
            for i in range(4):
                copy_out("goT", i, g_oT[:, 2 * i:2 * i + 2, :].rearrange("p k c -> p (k c)"))

            dve.wait_ge(sem("gemm_read"), gemm_at["skv"] + T)
            flat = lambda a: a[:, :, :, :].rearrange("p t h d -> p (t h) d")
            mul(flat(s_b), flat(s_qk), flat(s_qk))
            link(dve.tensor_reduce(head_ms[:, 0:20], flat(s_b), AX_X, ALU.add))
            mean(head_ms[:, 0:20], head_ms[:, 0:20], HD, "head_ms_s")
            dve.wait_ge(sem("head_rinv_s"), 1)
            mul(flat(s_qk), flat(s_qk), over(head_rinv[:, 0:20], 2, HD))
            for t in range(T):
                mul(s_qk[:, t, 0:8, :], s_qk[:, t, 0:8, :], over(s_gain[:, 0, :], 1, 8))
                mul(s_qk[:, t, 8:10, :], s_qk[:, t, 8:10, :], over(s_gain[:, 1, :], 1, 2))
                mul(s_a[:, t, :, :], s_qk[:, t, :, :], over(swa_cos[:, t, :], 1, 10))
                mul(s_b[:, t, :, 0:64], s_qk[:, t, :, 64:128], over(swa_sin[:, t, 0:64], 1, 10))
                mul(s_b[:, t, :, 64:128], s_qk[:, t, :, 0:64], over(swa_sin[:, t, 64:128], 1, 10))
                dve.tensor_tensor(s_a[:, t, :, :], s_a[:, t, :, :], s_b[:, t, :, :], ALU.add) \
                    .then_inc(sem("s_rot"), 1)
                dve.wait_ge(sem("s_rot"), told("s_rot"))
            for i in range(5):
                copy_out("sT", i, s_qkT[:, 2 * i:2 * i + 2, :].rearrange("p k c -> p (k c)"))

            def masked_scores(name, scores, n_heads, scale, mask):
                for t in range(T):
                    for i in range(n_heads // 2):
                        b = tiles(bank_of(name, t * n_heads // 2 + i)[:, :], 2)
                        dve.scalar_tensor_tensor(scores[:, t, 2 * i:2 * i + 2, :], b, scale,
                                                 over(mask[:, t, :], 1, 2), ALU.mult, ALU.add) \
                                                     .then_inc(sem("pair_read"), 1)
                        dve.wait_ge(sem("pair_read"), told("pair_read"))
                link(dve.tensor_reduce(row_max[:, 0:T * n_heads], scores[:, :, :, :].rearrange("p t h k -> p (t h) k"),
                                       AX_X, ALU.max))

            def attended(names, weightsT, n_heads, to):
                for t in range(T):
                    for i in range(n_heads // 2):
                        copy_out(names[0], t * n_heads // 2 + i,
                                 weightsT[:, t, 2 * i:2 * i + 2, :, :].rearrange("p h b q -> p (h b q)"))
                for t in range(T):
                    for i in range(n_heads // 4):
                        b = tiles(bank_of(names[1], t * n_heads // 4 + i)[:, :], 4)
                        at = t * n_heads + 4 * i
                        mul(to[:, t, 512 * i:512 * (i + 1)].rearrange("p (h d) -> p h d", h=4), b,
                            over(row_rec[:, at:at + 4], 2, P), "pair_read")

            masked_scores("ssc", s_sc, SWA_HEADS, HD ** -0.5, window)
            sink_all = over(sinks, 1, T)
            link(dve.tensor_tensor(tiles(row_max), tiles(row_max), sink_all, ALU.max))
            link(dve.tensor_tensor(tiles(sink_exp), sink_all, tiles(row_max), ALU.subtract))
            negate(row_max, row_max, "s_max_ready")
            dve.wait_ge(sem("s_exp"), T * SWA_HEADS)
            link(dve.tensor_tensor(row_sum, row_sum, sink_exp, ALU.add))
            link(dve.reciprocal(row_rec, row_sum))
            attended(("sP", "so"), s_pT, SWA_HEADS, s_o)
            for i in range(4):
                copy_out("soT", i, s_oT[:, 2 * i:2 * i + 2, :].rearrange("p k c -> p (k c)"))
            dve.wait_ge(sem("gemm_read"), gemm_at["os1"] + T)
            mul(y_gla, y_gla, gate_a)
            mul(y_swa, y_swa, gate_b)
            dve.tensor_tensor(y_gla, y_gla, y_swa, ALU.add).then_inc(sem("merged"), 1)
            dve.wait_ge(sem("merged"), told("merged"))
            for i in range(4):
                copy_out("mT", i, mT[:, 2 * i:2 * i + 2, :].rearrange("p k c -> p (k c)"))

            def residual(product, last_gemm, name):
                dve.wait_ge(sem("gemm_read"), gemm_at[last_gemm] + T)
                for t in range(T):
                    dve.tensor_tensor(x[:, t, :], x[:, t, :], product[:, t, :], ALU.add).then_inc(sem(name), 1)
                    dve.wait_ge(sem(name), told(name))

            def ffn(tag, done):
                for u in range(FFN_UNITS):
                    dve.wait_ge(sem(f"{tag}_silu"), u + 1)
                    dve.wait_ge(sem(f"{tag}_up_done"), u + 1)
                    if u >= 2:
                        dve.wait_ge(sem(f"{tag}_down_done"), u - 1)
                    mul(f_hid[u % 2], f_silu[u % 2], gemm_bank[2 * (u % 2) + 1][:, :], f"{tag}_hid")
                dve.wait_ge(sem(f"{tag}_down_done"), FFN_UNITS)
                for t in range(T):
                    for half in range(2):
                        part = x[:, t, half * 512:(half + 1) * 512]
                        dve.tensor_tensor(part, part, pair_bank[2 * t + half][:, :], ALU.add).then_inc(sem(done), 1)
                        dve.wait_ge(sem(done), told(done))

            residual(gate_a, "wo1", "x_mixed_f")
            norm("f1")
            ang, turns, rest = (tiles(scratch(64 * i, 64)) for i in range(3))
            link(dve.tensor_copy(pos_f, position))
            for t in range(T):
                link(dve.tensor_scalar(ang[:, t, :], inv_freq, pos_f[:, t:t + 1], None, ALU.mult))
            magic = float(1.5 * 2 ** 23)
            link(dve.tensor_scalar(turns, ang, 1.0 / TWO_PI, None, ALU.mult))
            link(dve.tensor_scalar(turns, turns, magic, None, ALU.add))
            link(dve.tensor_scalar(turns, turns, magic, None, ALU.subtract))
            part1 = 6.28125
            part2 = float(np.float32(round((TWO_PI - part1) * 2 ** 20) / 2 ** 20))
            for n, part in enumerate((part1, part2, TWO_PI - part1 - part2)):
                link(dve.scalar_tensor_tensor(rest, turns, -part, ang if n == 0 else rest, ALU.mult, ALU.add))
            edge = 3.1415925
            dve.tensor_scalar(rope_sin[:, :, 32:64], rest, edge, -edge, ALU.min, ALU.max) \
                .then_inc(sem("angle_ready"), 1)
            dve.wait_ge(sem("angle_ready"), told("angle_ready"))
            link(dve.tensor_scalar(rest, rest, np.pi / 2, None, ALU.add))
            link(dve.tensor_scalar(turns, rest, edge, -TWO_PI, ALU.is_gt, ALU.mult))
            link(dve.tensor_tensor(rest, rest, turns, ALU.add))
            dve.tensor_scalar(rope_cos[:, :, 0:32], rest, edge, -edge, ALU.min, ALU.max) \
                .then_inc(sem("angle_ready"), 1)
            dve.wait_ge(sem("angle_ready"), told("angle_ready"))
            ffn("f1", "x_ffn_0")
            dve.wait_ge(sem("sines"), 1)
            link(dve.tensor_copy(rope_cos[:, :, 32:64], rope_cos[:, :, 0:32]))
            negate(rope_sin[:, :, 0:32], rope_sin[:, :, 32:64])

            for l in range(2):
                norm(f"l{l}")
                if l == 1:
                    dve.wait_ge(sem("bounds_landed"), 32)
                    diff, soft = n_tmp[1][:, 0:512], n_tmp[0][:, 0:512]
                    link(dve.tensor_tensor(diff, log_rest, log_lb, ALU.subtract))
                    absolute(soft, diff, "bound_abs")
                    dve.wait_ge(sem("bound_soft"), 1)
                    link(dve.scalar_tensor_tensor(log_lb, diff, 0.0, soft, ALU.min, ALU.subtract))
                    link(dve.scalar_tensor_tensor(log_rest, diff, 0.0, soft, ALU.max, ALU.add))
                    negate(log_rest, log_rest)
                flat_z, flat_lf, flat_k = (a[:, :, :].rearrange("p t n -> p (t n)") for a in (n_z, n_lf, n_k))
                dve.wait_ge(sem("gemm_read"), gemm_at[f"hf_{l}"] + T)
                absolute(n_tmp[0], flat_z, f"z_abs_{l}")
                dve.wait_ge(sem(f"z_soft_{l}"), 1)
                link(dve.scalar_tensor_tensor(flat_lf, flat_z, 0.0, n_tmp[0], ALU.min, ALU.subtract))
                link(dve.scalar_tensor_tensor(flat_k, flat_z, 0.0, n_tmp[0], ALU.max, ALU.add))
                if l == 0:
                    negate(flat_k, flat_k, "ln_k_0")
                    dve.tensor_scalar(flat_lf, flat_lf, LN_F_FLOOR, None, ALU.max).then_inc(sem("n_lf_ready_0"), 1)
                    dve.wait_ge(sem("n_lf_ready_0"), told("n_lf_ready_0"))
                else:
                    link(dve.tensor_tensor(n_lf, n_lf, over(log_rest, 1, T), ALU.add))
                    link(dve.tensor_tensor(tiles(n_tmp[2]), over(log_lb, 1, T), n_lf, ALU.subtract))
                    absolute(n_tmp[1], n_tmp[2], "mix_abs")
                    link(dve.tensor_tensor(n_lf, n_lf, over(log_lb, 1, T), ALU.max))
                    dve.scalar_tensor_tensor(n_k, n_k, -1.0, over(log_rest, 1, T), ALU.mult, ALU.add) \
                        .then_inc(sem("ln_k_1"), 1)
                    dve.wait_ge(sem("ln_k_1"), told("ln_k_1"))
                    dve.wait_ge(sem("mix_soft"), 1)
                    link(dve.tensor_tensor(flat_lf, flat_lf, n_tmp[1], ALU.add))
                    dve.tensor_scalar(flat_lf, flat_lf, LN_F_FLOOR, None, ALU.max).then_inc(sem("n_lf_ready_1"), 1)
                    dve.wait_ge(sem("n_lf_ready_1"), told("n_lf_ready_1"))
                dve.wait_ge(sem(f"c_ss_{l}"), 2 * T)
                mean(head_ms[:, 8:10], head_ms[:, 8:10], Q_RANK, "vector_step")
                mean(head_ms[:, 10:12], head_ms[:, 10:12], KV_RANK, f"c_ms_{l}")
                dve.wait_ge(sem(f"c_rinv_{l}"), 1)
                for n, (lo, hi) in enumerate(((0, Q_RANK), (Q_RANK, Q_RANK + KV_RANK))):
                    for t in range(T):
                        at = 8 + 2 * n + t
                        dve.tensor_scalar(n_c[:, t, lo:hi], n_c[:, t, lo:hi], head_rinv[:, at:at + 1], None,
                                          ALU.mult).then_inc(sem(f"c_normed_{l}"), 1)
                        dve.wait_ge(sem(f"c_normed_{l}"), told(f"c_normed_{l}"))
                for t in range(T):
                    copy_out(f"hkT_{l}", t, n_kT[:, t * 512:(t + 1) * 512])
                for t in range(T):
                    copy_out(f"hb_{l}", t, n_bT[:, t * 512:(t + 1) * 512])
                copy_out(f"ht_{l}", 0, n_kt)
                for i in range(3):
                    n = min(2, 5 - 2 * i)
                    b = tiles(bank_of(f"cT_{l}", i)[:, 0:n * TOKENS], n)
                    mul(n_cT[:, 2 * i:2 * i + n, :], b, over(c_gain[l][:, 2 * i:2 * i + n], 2, TOKENS), "pair_read")
                for t in range(T):
                    copy_out(f"hqT_{l}", t, n_qT[:, t * 512:(t + 1) * 512])
                dve.wait_ge(sem(f"n_tail_exp_{l}"), 1)
                mul(n_kt, n_kt, n_k[:, 0, :], f"n_kt_ready_{l}")
                dve.wait_ge(sem(f"n_qd_exp_{l}"), 1)
                mul(n_qd, n_qd, n_qT[:, 512:1024], f"n_qd_ready_{l}")
                gains = n_g[:, :, :].rearrange("p t (g d) -> p (t g) d", d=P)
                dve.wait_ge(sem("gemm_read"), gemm_at[f"hg_{l}"] + T)
                mul(gains, gains, over(hg_gain[l], 1, 8))

                def blocks(a, half):
                    return a.rearrange("p (n c) -> p n c", c=2 * half)

                def halves(a, half):
                    return a.rearrange("p (n s c) -> p n s c", s=2, c=half)

                def level_diff(n):
                    half = LEVELS[n - 1]
                    if n >= 3:
                        dve.wait_ge(sem(f"level_exp_{l}"), 2 * (n - 2))
                    b = blocks(n_bT, half)
                    middle = b[:, :, half - 1]
                    dve.tensor_tensor(blocks(n_E[n % 2], half), b, over(middle, 2, 2 * half), ALU.subtract) \
                        .then_inc(sem(f"level_diff_{l}"), 1)
                    dve.wait_ge(sem(f"level_diff_{l}"), told(f"level_diff_{l}"))

                def level_scale(n):
                    half = LEVELS[n - 1]
                    dve.wait_ge(sem(f"level_exp_{l}"), 2 * n)
                    for side, other in enumerate((n_kT, n_qT)):
                        part = halves(n_X[n % 2], half)[:, :, side, :]
                        mul(part, part, halves(other, half)[:, :, side, :], f"level_ready_{l}")

                def level_take(n):
                    for t in range(T):
                        b = tiles(bank_of(f"hlev_{l}", T * n + t)[:, :], 4)
                        to = tiles(n_at[:, t * 512:(t + 1) * 512], 4)
                        if n == 0:
                            mul(to, b, over(ident, 1, 4), "pair_read")
                        else:
                            mask = over(level_masks[:, n * P:(n + 1) * P], 1, 4)
                            dve.copy_predicated(to, mask, b).then_inc(sem("pair_read"), 1)
                            dve.wait_ge(sem("pair_read"), told("pair_read"))

                level_diff(1)
                level_diff(2)
                level_take(0)
                for n in range(1, len(LEVELS) + 1):
                    level_scale(n)
                    if n + 2 <= len(LEVELS):
                        level_diff(n + 2)
                    if n >= 2:
                        level_take(n - 1)
                level_take(len(LEVELS))

                dve.wait_ge(sem("gemm_read"), gemm_at[f"kvb1_{l}"] + T)
                ra, rb = scratch(11520, 256), scratch(11776, 256)
                for t in range(T):
                    q_pe = n_qm[:, t, :].rearrange("p (h d) -> p h d", h=MLA_HEADS)[:, :, NOPE:192]
                    k_pe = n_c[:, t, Q_RANK + KV_RANK:Q_RANK + KV_RANK + ROPE].rearrange("p (h d) -> p h d", h=1)
                    for pe_part, n in ((q_pe, MLA_HEADS), (k_pe, 1)):
                        a_, b_ = (r[:, 0:n * ROPE].rearrange("p (h d) -> p h d", h=n) for r in (ra, rb))
                        mul(a_, pe_part, over(rope_cos[:, t, :], 1, n))
                        mul(b_[:, :, 0:32], pe_part[:, :, 32:64], over(rope_sin[:, t, 0:32], 1, n))
                        mul(b_[:, :, 32:64], pe_part[:, :, 0:32], over(rope_sin[:, t, 32:64], 1, n))
                        dve.tensor_tensor(pe_part, a_, b_, ALU.add).then_inc(sem(f"m_rot_{l}"), 1)
                        dve.wait_ge(sem(f"m_rot_{l}"), told(f"m_rot_{l}"))

                copy_out(f"hst_{l}", 0, n_st)
                for t in range(T):
                    copy_out(f"ho_{l}", t, mix[:, t, 512:1024])
                for t in range(T):
                    mul(tiles(n_tmp[0])[:, t, :], mix[:, t, 512:1024], mix[:, t, 512:1024])
                link(dve.tensor_reduce(head_ms[:, 0:8], n_tmp[0].rearrange("p (g d) -> p g d", d=P), AX_X, ALU.add))
                mean(head_ms[:, 0:8], head_ms[:, 0:8], P, f"head_ms_h{l}")
                dve.wait_ge(sem(f"head_rinv_h{l}"), 1)
                for t in range(T):
                    o = mix[:, t, 512:1024].rearrange("p (g d) -> p g d", d=P)
                    mul(o, o, over(head_rinv[:, 4 * t:4 * t + 4], 2, P))
                for t in range(T):
                    mul(mix[:, t, 512:1024], mix[:, t, 512:1024], n_g[:, t, :], f"hg_mixed_{l}")

                for name, to in ((f"mqT_{l}", n_mqT), (f"mkT_{l}", n_mkT)):
                    for i in range(2):
                        copy_out(name, i, to[:, 2 * i:2 * i + 2, :].rearrange("p k c -> p (k c)"))
                for i in range(2):
                    copy_out(f"mpT_{l}", i, n_pqT[:, 2 * i:2 * i + 2, :].rearrange("p k c -> p (k c)"), ROPE)
                copy_out(f"mpT_{l}", 2, n_pkT, ROPE, TOKENS)
                masked_scores(f"msc_{l}", n_sc, MLA_HEADS, (NOPE + ROPE) ** -0.5, causal)
                negate(row_max[:, 0:8], row_max[:, 0:8], f"m_max_ready_{l}")
                dve.wait_ge(sem(f"m_exp_{l}"), T * MLA_HEADS)
                link(dve.reciprocal(row_rec[:, 0:8], row_sum[:, 0:8]))
                attended((f"mP_{l}", f"mo_{l}"), n_pT, MLA_HEADS, mix)
                for i in range(4):
                    copy_out(f"mixT_{l}", i, mixT[:, 2 * i:2 * i + 2, :].rearrange("p k c -> p (k c)"))
                residual(tiles(work(4096, 2048)), f"wo1_{l}", f"x_mixed_{l}")
                norm(f"g{l}")
                if l == 0:
                    ffn("f2", "x_ffn_1")

            dve.tensor_copy(work(0, 16), bank_of("router", 0)[:, 0:16]).then_inc(sem("pair_read"), 1)
            dve.wait_ge(sem("pair_read"), told("pair_read"))
            for t in range(T):
                link(dve.max(e_top[:, t, :], e_logit[:, t, :]))
                link(dve.max_index(e_idx[:, t, :], e_top[:, t, :], e_logit[:, t, :]))
            link(dve.tensor_copy(e_idf, e_idx))
            dve.tensor_tensor(e_d, e_top[:, :, 1], e_top[:, :, 0], ALU.subtract).then_inc(sem("e_gap"), 1)
            dve.wait_ge(sem("e_gap"), told("e_gap"))
            for t in range(T):
                for n, one_hot in enumerate((e_oh0, e_oh1)):
                    link(dve.tensor_scalar(one_hot[:, t, :], iota[:, 0:EXPERTS], e_idf[:, t, n:n + 1], None, ALU.is_equal))
            dve.tensor_tensor(e_mask, e_oh0, e_oh1, ALU.add).then_inc(sem("e_mask_ready"), 1)
            dve.wait_ge(sem("e_mask_ready"), told("e_mask_ready"))
            dve.wait_ge(sem("e_odds"), 1)
            link(dve.tensor_scalar(e_g0, e_g1, 1.0, None, ALU.add))
            link(dve.reciprocal(e_g0, e_g0))
            mul(e_g1, e_g1, e_g0)
            for t in range(T):
                link(dve.tensor_scalar(e_prob[:, t, :], e_oh0[:, t, :], e_g0[:, t:t + 1], None, ALU.mult))
                link(dve.scalar_tensor_tensor(e_prob[:, t, :], e_oh1[:, t, :], e_g1[:, t:t + 1], e_prob[:, t, :],
                                              ALU.mult, ALU.add))
            b = bank_of("ranks", 0)
            far = float(4 * TOKENS)
            link(dve.tensor_reduce(e_cnt, b[:, 16:24], AX_X, ALU.max))
            dve.scalar_tensor_tensor(e_pos, e_mask, -far, tiles(b[:, 0:16]), ALU.mult, ALU.add) \
                .then_inc(sem("pair_read"), 1)
            dve.wait_ge(sem("pair_read"), told("pair_read"))
            link(dve.tensor_scalar(e_pos, e_pos, far, None, ALU.add))
            link(dve.tensor_scalar(e_cntx[:, 0:1], e_cnt, float(CAP), 1.0, ALU.is_gt, ALU.add))
            for n in range(2, MAX_ROUNDS):
                link(dve.tensor_scalar(e_cntx[:, 1:2], e_cnt, float(n * CAP), None, ALU.is_gt))
                link(dve.tensor_tensor(e_cntx[:, 0:1], e_cntx[:, 0:1], e_cntx[:, 1:2], ALU.add))
            dve.tensor_copy(e_rounds, e_cntx[:, 0:1]).then_inc(sem("rounds_known"), 1)
            dve.wait_ge(sem("rounds_known"), told("rounds_known"))

            def expert(it, e):
                for t in range(T):
                    dve.tensor_scalar(e_P[:, t, :], iota, e_pos[:, t, bass.ds(e, 1)], None, ALU.is_equal) \
                        .then_inc(sem("e_placed"), 1)
                    dve.wait_ge(sem("e_placed"), 2 * T * it + 2 * t + 1)
                    dve.tensor_scalar(e_G[:, t, :], e_P[:, t, :], e_prob[:, t, bass.ds(e, 1)], None, ALU.mult) \
                        .then_inc(sem("e_placed"), 1)
                    dve.wait_ge(sem("e_placed"), 2 * T * it + 2 * t + 2)
                for i in range(2):
                    dve.wait_ge(sem("e_gathered"), 2 * it + i + 1)
                    b = tiles(pair_bank[2 + i][:, 0:4 * CAP], 4)
                    dve.tensor_tensor(e_x[:, 4 * i:4 * i + 4, :], b, over(gain_T["g1"][:, 4 * i:4 * i + 4], 2, CAP),
                                      ALU.mult).then_inc(sem("e_x_ready"), 1)
                    dve.wait_ge(sem("e_x_ready"), 2 * it + i + 1)
                dve.wait_ge(sem("e_turned"), it + 1)
                dve.tensor_copy(e_GT, pair_bank[0][0:CAP, 0:TOKENS]).then_inc(sem("e_GT_ready"), 1)
                dve.wait_ge(sem("e_GT_ready"), it + 1)
                for s in range(MOE_STEPS):
                    dve.wait_ge(sem("e_silu_ready"), it * MOE_STEPS + s + 1)
                    dve.wait_ge(sem("expert_up_done"), it * MOE_STEPS + s + 1)
                    if s >= 2:
                        dve.wait_ge(sem("expert_down_done"), it * MOE_STEPS + s - 1)
                    dve.tensor_tensor(e_hid[s % 2][:, :, :].rearrange("p j c -> p (j c)"), e_silu[s % 2],
                                      gemm_bank[2 * (s % 2) + 1][:, 0:4 * CAP], ALU.mult) \
                                          .then_inc(sem("e_hid_ready"), 1)
                    dve.wait_ge(sem("e_hid_ready"), it * MOE_STEPS + s + 1)
                dve.wait_ge(sem("expert_down_done"), it * MOE_STEPS + MOE_STEPS)
                for half in range(2):
                    dve.tensor_copy(e_y[:, half * 512:(half + 1) * 512], pair_bank[half][0:CAP, :]) \
                        .then_inc(sem("e_y_ready"), 1)
                    dve.wait_ge(sem("e_y_ready"), 2 * it + half + 1)
                for q in range(4):
                    t, half = divmod(q, 2)
                    dve.wait_ge(sem("e_scattered"), 4 * it + q + 1)
                    part = x[:, t, half * 512:(half + 1) * 512]
                    dve.tensor_tensor(part, part, pair_bank[2 + q % 2][:, :], ALU.add).then_inc(sem("e_added"), 1)
                    dve.wait_ge(sem("e_added"), 4 * it + q + 1)

            with dve.Fori(0, EXPERTS) as e:
                expert(e, e)
            rounds = dve.value_load(e_rounds[0:1, 0:1], min_val=1, max_val=MAX_ROUNDS)
            with dve.If(rounds > 1):
                with dve.Fori(1, rounds) as r:
                    dve.tensor_scalar(e_pos, e_pos, float(CAP), None, ALU.subtract).then_inc(sem("e_shifted"), 1)
                    with dve.Fori(0, EXPERTS) as e:
                        dve.wait_ge(sem("e_shifted"), r)
                        expert(r * EXPERTS + e, e)
            dve.memset(ss, 0.0).then_inc(sem("x_complete"), 1)
            dve.wait_ge(sem("x_complete"), told("x_complete"))
            dve.wait_ge(sem("ss_last"), T)
            mean(ms, ss, D, "ms_last")
            dve.wait_ge(sem("rinv_last"), 1)
            dve.wait_ge(sem("final_gain_landed"), 16)
            for t in range(T):
                link(dve.tensor_scalar(x[:, t, :], x[:, t, :], rinv[:, t:t + 1], None, ALU.mult))
                mul(x[:, t, :], x[:, t, :], fin_gain, "result")


_OUTS = [((1, TOKENS, D), "float32")]


def kernel(**inputs):
    import concourse.bacc as _bacc
    from concourse.bass_utils import run_bass_kernel_spmd as _run

    nc = _bacc.Bacc("TRN2", target_bir_lowering=False, num_devices=1)
    table, masks = constants()
    arrays, A = {}, {}
    for name, value in {**inputs, "const_table": table, "level_masks": masks}.items():
        a = np.ascontiguousarray(value)
        arrays[f"in_{name}"] = a
        A[name] = nc.dram_tensor(f"in_{name}", a.shape, mybir.dt.from_np(a.dtype), kind="ExternalInput").ap()
    out = nc.dram_tensor("out_0", _OUTS[0][0], F32, kind="ExternalOutput").ap()
    for name in ("w_in", "w_o_gla", "w_o_swa", "w_out"):
        A[name] = A[name][0]
    A["f1_gate"], A["f1_up"] = A["w_ffn_in"][0][:, 0:D_FF], A["w_ffn_in"][0][:, D_FF:2 * D_FF]
    A["f1_down"] = A["w_ffn_out"][0]
    for part in ("gate", "up", "down"):
        A[f"f2_{part}"] = A[f"dense_w_{part}_2"][0]
        A[f"moe_w_{part}"] = A[f"moe_w_{part}_2"][0]
    for l in range(2):
        for name in ("w_in", "w_q_b", "w_kv_b", "w_out"):
            A[f"{name}_2_{l}"] = A[f"{name}_2"][l]
    build(nc, A, out)
    r = _run(nc, [arrays], core_ids=[0])
    return r.results[0]["out_0"]
```

```python
from contextlib import ExitStack

import numpy as np

import concourse.bass as bass
from concourse import mybir

ALU = mybir.AluOpType
ACT = mybir.ActivationFunctionType
F32 = mybir.dt.float32
F32R = mybir.dt.float32r
I32 = mybir.dt.int32
U32 = mybir.dt.uint32
AX_X = mybir.AxisListType.X

P = 128
TOKENS = 256
T = TOKENS // P
D = 1024
KD = D // P
EPS = 1e-6
MASKED = -1e30

GLA_HEADS, GLA_DK, GLA_DV, GLA_RANK = 4, 128, 256, 16
SWA_HEADS, SWA_KV, HD, WINDOW = 8, 2, 128, 128
D_FF = 2816
Q_RANK, KV_RANK, ROPE = 384, 256, 64
MLA_HEADS, NOPE, V_HEAD = 4, 128, 128
HG_HEADS = 4
EXPERTS, EXPERT_FF = 8, 3584
LEVELS = [64, 32, 16, 8, 4, 2, 1]
LN_F_FLOOR = float(np.log(1e-30))

SLOT = 2048
SUB = 1024
BUFFERS = 4
SLOTS = 7
DENSE_SLOTS = 4
CAP = 128
MAX_ROUNDS = -(-TOKENS // CAP)
FF_STEP = 512
MOE_STEPS = EXPERT_FF // FF_STEP
MOE_LOADS = 3 * MOE_STEPS * 2
MOE_SUBS = 2 * MOE_LOADS
FF_UNIT = 256
FFN_UNITS = D_FF // FF_UNIT
SCRATCH = 4 * SLOT
WORK = 13968

CONSTS = [("le", P), ("ge", P), ("gt", P), ("lt", P), ("ident", P), ("ones", P),
          ("window", T * 256), ("swa_cos", T * HD), ("swa_sin", T * HD), ("causal", T * 256), ("iota", CAP),
          ("inv_freq", ROPE // 2)]
CONST_AT = {}
CONST_WORDS = 0
for _name, _width in CONSTS:
    CONST_AT[_name] = (CONST_WORDS, _width)
    CONST_WORDS += _width


def constants():
    r, c = np.arange(P)[:, None], np.arange(P)[None, :]
    key = np.arange(256)[None, :]
    query = [r + P * t for t in range(T)]
    half = HD // 2
    inv = (np.float32(10000.0) ** (-np.arange(half, dtype=np.float32) / np.float32(half))).astype(np.float32)
    ang = np.arange(TOKENS, dtype=np.float32)[:, None] * inv[None, :]
    cos, sin = np.cos(ang), np.sin(ang)
    tiles = lambda a: a.reshape(T, P, -1).transpose(1, 0, 2).reshape(P, -1)
    inv_pe = np.float32(10000.0) ** (-np.arange(0, ROPE, 2, dtype=np.float32) / np.float32(ROPE))
    parts = {
        "le": r <= c, "ge": r >= c, "gt": r > c, "lt": r < c, "ident": r == c, "ones": np.ones((P, P)),
        "window": np.concatenate([np.where(abs(q - key) <= WINDOW, 0.0, MASKED) for q in query], 1),
        "causal": np.concatenate([np.where(key <= q, 0.0, MASKED) for q in query], 1),
        "iota": np.broadcast_to(np.arange(CAP), (P, CAP)),
        "swa_cos": tiles(np.concatenate([cos, cos], 1)), "swa_sin": tiles(np.concatenate([-sin, sin], 1)),
        "inv_freq": np.broadcast_to(inv_pe, (P, ROPE // 2)),
    }
    table = np.concatenate([np.asarray(parts[n], np.float32).reshape(P, w) for n, w in CONSTS], 1)
    masks = [(r == c)]
    for h in LEVELS:
        masks.append((r // (2 * h) == c // (2 * h)) & (r % (2 * h) < h) & (c % (2 * h) >= h))
    return np.ascontiguousarray(table), np.ascontiguousarray(np.concatenate(masks, 1).astype(np.int32))


def counter():
    counts = {}

    def told(name):
        counts[name] = counts.get(name, 0) + 1
        return counts[name]

    return told


def gemm_plan():
    plan = []

    def add(name, weight, start, width, k=KD):
        plan.append((name, weight, start, width, k))

    add("gk", "w_in", 512, 512)
    add("gq", "w_in", 0, 512)
    add("lr", "w_in", 3072, 32)
    add("gv0", "w_in", 1024, 512)
    add("gv1", "w_in", 1536, 512)
    add("gr0", "w_in", 2048, 512)
    add("gr1", "w_in", 2560, 512)
    add("sq0", "w_in", 3104, 512)
    add("sq1", "w_in", 3616, 512)
    add("skv", "w_in", 4128, 512)
    add("ga0", "w_in", 4640, 512)
    add("ga1", "w_in", 5152, 512)
    add("gb0", "w_in", 5664, 512)
    add("gb1", "w_in", 6176, 512)
    for i in range(2):
        add(f"og{i}", "w_o_gla", 512 * i, 512)
    for i in range(2):
        add(f"os{i}", "w_o_swa", 512 * i, 512)
    for i in range(2):
        add(f"wo{i}", "w_out", 512 * i, 512)
    add("FFN", "f1", 0, 0)
    for layer in range(2):
        base = Q_RANK + KV_RANK + ROPE
        w = f"w_in_2_{layer}"
        add(f"hf_{layer}", w, base + 512, 512)
        add(f"c0_{layer}", w, 0, 512)
        add(f"c1_{layer}", w, 512, base - 512)
        add(f"hi_{layer}", w, base + 1024, 512)
        add(f"hq_{layer}", w, base, 512)
        add(f"hg_{layer}", w, base + 1536, 512)
        for i in range(2):
            add(f"qb{i}_{layer}", f"w_q_b_2_{layer}", 384 * i, 384, Q_RANK // P)
        for i in range(2):
            add(f"kvb{i}_{layer}", f"w_kv_b_2_{layer}", 512 * i, 512, KV_RANK // P)
        for i in range(2):
            add(f"wo{i}_{layer}", f"w_out_2_{layer}", 512 * i, 512)
        if layer == 0:
            add("FFN", "f2", 0, 0)
    return plan


def pair_plan():
    plan = [("hT_f0", 4), ("lrT", 1), ("z", 4), ("gqT", 2), ("gkT", 2), ("gb", 4), ("tail", 2), ("gsc", 4), ("gst", 4),
            ("go", 4), ("sT", 5), ("ssc", 8), ("goT", 4), ("sP", 8), ("so", 4), ("soT", 4), ("mT", 4), ("hT_f1", 4)]
    for layer in range(2):
        plan += [(f"hT_l{layer}", 4), (f"hkT_{layer}", 2), (f"hb_{layer}", 2), (f"ht_{layer}", 1),
                 (f"cT_{layer}", 3), (f"hqT_{layer}", 2)]
        plan += [(f"hlev_{layer}", T * (len(LEVELS) + 1)), (f"hst_{layer}", 1), (f"ho_{layer}", 2)]
        plan += [(f"mqT_{layer}", 2), (f"mkT_{layer}", 2), (f"mpT_{layer}", 3), (f"msc_{layer}", 4),
                 (f"mP_{layer}", 4), (f"mo_{layer}", 2), (f"mixT_{layer}", 4), (f"hT_g{layer}", 4)]
    plan += [("router", 1), ("ranks", 1)]
    return plan


def build(nc, A, out):
    gemms = [g for g in gemm_plan() if g[0] != "FFN"]
    gemm_at = {g[0]: T * i for i, g in enumerate(gemms)}
    pair_at, pair_end, n = {}, {}, 0
    for name, banks in pair_plan():
        pair_at[name], pair_end[name] = n, n + banks
        n += banks

    loads, subs, span = [], [], {}

    def stream(name, src, k_tiles, width, cuts):
        for n, piece in enumerate(cuts):
            subs.append((len(loads), n == 0, piece))
        loads.append((src, k_tiles, width))
        span[name] = (span.get(name, (len(subs) - len(cuts), 0))[0], len(subs))

    ffn_range = {}
    for name, weight, start, width, k in gemm_plan():
        if name != "FFN":
            src = A[weight].rearrange("(k p) n -> p k n", p=P)[:, :, start:start + width]
            if k < KD:
                stream(name, src, k, width, [None])
            elif width == 512:
                for k0 in (0, 4):
                    stream(name, src[:, k0:k0 + 4, :], 4, width, [("k", 0, 2), ("k", 2, 2)])
            else:
                n = KD if KD * width <= SUB else KD // 2
                stream(name, src, KD, width, [("k", k0, n) for k0 in range(0, KD, n)])
            continue
        ffn_range[weight] = [len(subs), 0]
        down = A[f"{weight}_down"].rearrange("(k p) n -> p k n", p=P)
        for u in range(FFN_UNITS + 1):
            if u < FFN_UNITS:
                for kind in ("gate", "up"):
                    src = A[f"{weight}_{kind}"].rearrange("(k p) n -> p k n", p=P)
                    stream(f"{weight}_{kind}{u}", src[:, :, u * FF_UNIT:(u + 1) * FF_UNIT], KD, FF_UNIT,
                           [("n", j * P, P) for j in range(2)])
            if u >= 1:
                stream(f"{weight}_down{u - 1}", down[:, 2 * (u - 1):2 * u, :], 2, D, [("k", 0, 1), ("k", 1, 1)])
        ffn_range[weight][1] = len(subs)
    slot_of = [i % DENSE_SLOTS for i in range(len(loads))]
    landed = [16 * (i // DENSE_SLOTS + 1) for i in range(len(loads))]
    hi_count, lo_count, made = [], [], {"w_hi_ready": 0, "w_lo_by_vector": 0, "w_lo_by_gpsimd": 0}
    for j, (_, _, piece) in enumerate(subs):
        by_vector = any(lo + BUFFERS <= j < hi for lo, hi in ffn_range.values())
        maker = "w_lo_by_vector" if by_vector else "w_lo_by_gpsimd"
        if piece is not None:
            made["w_hi_ready"] += 1
            made[maker] += 1
        hi_count.append(made["w_hi_ready"])
        lo_count.append((maker, made[maker]))
    USED0, HI0, LO0 = len(subs), made["w_hi_ready"], made["w_lo_by_vector"]
    load_freed = {}
    for j, (i, _, piece) in enumerate(subs):
        load_freed[i] = lo_count[j] if piece is not None else ("w_used", j + 1)

    with ExitStack() as ctx:
        sems = {}

        def sem(name):
            if name not in sems:
                sems[name] = ctx.enter_context(nc.semaphore(name))
            return sems[name]

        def sb(name, words, dtype=F32):
            return ctx.enter_context(nc.sbuf_tensor(name, [P, words], dtype))

        arena = sb("arena", DENSE_SLOTS * SLOT + SCRATCH + WORK)
        x_sb = sb("x_sb", T * D)
        h_sb = sb("h_sb", T * D)
        left_hi_sb, left_lo_sb = (sb(f"left_{n}_sb", KD * TOKENS, F32R) for n in ("hi", "lo"))
        w_hi_sb, w_lo_sb = (sb(f"w_{n}_sb", BUFFERS * SUB, F32R) for n in ("hi", "lo"))
        hid_hi_sb, hid_lo_sb = (sb(f"hid_{n}_sb", 2 * 512, F32R) for n in ("hi", "lo"))
        const_sb = sb("const_sb", CONST_WORDS)
        level_masks = ctx.enter_context(nc.sbuf_tensor("level_masks", [P, (len(LEVELS) + 1) * P], I32))
        small = sb("small_sb", 320)
        more = sb("more_sb", 256 + 256)
        bank = [ctx.enter_context(nc.psum_tensor(f"bank{i}", [P, 512], F32)) for i in range(8)]
        gemm_bank, pair_bank = bank[0:4], bank[4:8]

        def work(at, words):
            assert at + words <= WORK
            at += DENSE_SLOTS * SLOT + SCRATCH
            return arena[:, at:at + words]

        def scratch(at, words):
            assert at + words <= SCRATCH
            return arena[:, DENSE_SLOTS * SLOT + at:DENSE_SLOTS * SLOT + at + words]

        def slot(i, k, n):
            return arena[:, i * SLOT:i * SLOT + k * n].rearrange("p (k n) -> p k n", k=k)

        def piece_of(view, piece):
            axis, start, size = piece
            return view[:, start:start + size, :] if axis == "k" else view[:, :, start:start + size]

        def raw(j):
            i, _, piece = subs[j]
            return piece_of(slot(slot_of[i], *loads[i][1:]), piece)

        def buffer(store, j, k, n):
            at = (j % BUFFERS) * SUB
            return store[:, at:at + k * n].rearrange("p (k n) -> p k n", k=k)

        small_used = [0]

        def tiny(words):
            at = small_used[0]
            small_used[0] += words
            assert small_used[0] <= 320
            return small[:, at:at + words]

        def const(name, *shape):
            at, w = CONST_AT[name]
            return const_sb[:, at:at + w]

        def tiles(ap, t=T):
            return ap.rearrange("p (t n) -> p t n", t=t)

        def over(ap, position, size):
            ap = ap.unsqueeze(position)
            shape = list(ap.shape)
            shape[position] = size
            return ap.to_broadcast(shape)

        le, ge, gt, lt, ident, ones = (const(c) for c in ("le", "ge", "gt", "lt", "ident", "ones"))
        window, causal = tiles(const("window")), tiles(const("causal"))
        swa_cos, swa_sin = tiles(const("swa_cos")), tiles(const("swa_sin"))
        lb_at = CONST_AT["window"][0]
        log_lb, log_rest = const_sb[:, lb_at:lb_at + 512], const_sb[:, lb_at + 512:lb_at + 1024]
        iota, inv_freq = const("iota"), const("inv_freq")
        x, h = tiles(x_sb[:, :]), tiles(h_sb[:, :])
        left_hi, left_lo = tiles(left_hi_sb[:, :], KD), tiles(left_lo_sb[:, :], KD)

        norms = ("f0", "f1", "l0", "g0", "l1", "g1")
        gain_T = {n: tiny(KD) for n in norms}
        c_gain = [tiny(5) for _ in range(2)]
        ss, ms, rinv = tiny(T), tiny(T), tiny(T)
        head_ms, head_rinv = tiny(20), tiny(20)
        row_max, sink_exp, row_sum, row_rec = tiny(16), tiny(16), tiny(16), tiny(16)
        sinks = tiny(SWA_HEADS)
        position = tiny(T).bitcast(I32)
        pos_f = tiny(T)
        router_w = tiles(tiny(KD * EXPERTS), KD)
        hg_gain = [more[:, 128 * i:128 * i + 128] for i in range(2)]
        rope_cos, rope_sin = tiles(more[:, 256:384]), tiles(more[:, 384:512])

        g_q, g_k, g_v = tiles(work(0, 1024)), tiles(work(1024, 1024)), tiles(work(2048, 2048))
        g_lg = work(4096, 2048).rearrange("p (a t n) -> p a t n", a=2, t=T)
        g_qT, g_kT = work(6144, 1024), work(7168, 1024)
        g_kt = tiles(work(8192, 1024))
        g_lrT = tiles(work(9216, 512)[0:GLA_RANK, :])
        g_lr = tiles(work(9728, 64))
        g_sr = h
        g_dec = [scratch(2048 * a, 1024) for a in range(2)]
        g_inv = [scratch(2048 * a + 1024, 1024) for a in range(2)]
        g_up = tiles(scratch(4096, 1024)[0:GLA_RANK, :])
        g_bias = tiles(scratch(6144, 1024)[0:1, :])
        g_sc = scratch(4096, 2048).rearrange("p (a t h c) -> p a t h c", a=2, t=T, h=GLA_HEADS)
        g_st = scratch(6144, 2048).rearrange("p (a h e) -> p a h e", a=2, h=GLA_HEADS)
        g_o = work(4096, 2048)
        g_tmp = scratch(0, 2048)
        g_gain = work(13184, 256)
        s_qk = work(9856, 2560).rearrange("p (t h d) -> p t h d", t=T, h=10)
        s_qk_flat = tiles(work(9856, 2560))
        s_v = tiles(work(12416, 512))
        s_gain = tiles(work(12928, 256))
        s_a = scratch(0, 2560).rearrange("p (t h d) -> p t h d", t=T, h=10)
        s_b = scratch(2560, 2560).rearrange("p (t h d) -> p t h d", t=T, h=10)
        s_qkT = tiles(work(6144, 2560), 10)
        s_sc = scratch(4096, 4096).rearrange("p (t h k) -> p t h k", t=T, h=SWA_HEADS)
        s_pT = scratch(0, 4096).rearrange("p (t h b q) -> p t h b q", t=T, h=SWA_HEADS, b=2)
        s_o = tiles(work(4096, 2048))
        gate_a, gate_b = tiles(work(0, 2048)), tiles(work(2048, 2048))
        y_gla, y_swa = tiles(work(9856, 2048)), tiles(work(4096, 2048))
        f_silu = [work(512 * i, 512) for i in range(2)]
        f_hid = work(1024, 512)
        hid_hi, hid_lo = ([a[:, 512 * i:512 * i + 512] for i in range(2)] for a in (hid_hi_sb, hid_lo_sb))
        n_z, n_q, n_v, n_g, n_lf, n_k = (tiles(work(1024 * i, 1024)) for i in range(6))
        n_qT, n_kT, n_bT, n_at = (work(6144 + 1024 * i, 1024) for i in range(4))
        n_kt, n_st = work(10240, 512), work(10752, 512)
        n_c = tiles(work(11264, 1408))
        n_cT = tiles(work(12672, 1280), 5)
        n_tmp = [scratch(1024 * i, 1024) for i in range(4)]
        n_E, n_X = n_tmp[0:2], n_tmp[2:4]
        n_qd = scratch(4096, 512)
        n_qm, n_kvm = tiles(scratch(4608, 1536)), tiles(scratch(6144, 2048))
        n_mqT, n_mkT = tiles(work(4096, 1024), 4), tiles(work(5120, 1024), 4)
        n_pqT = tiles(work(0, 1024)[0:ROPE, :], 4)
        n_pkT = work(1024, 256)[0:ROPE, :]
        n_sc = scratch(0, 2048).rearrange("p (t h k) -> p t h k", t=T, h=MLA_HEADS)
        n_pT = scratch(2048, 2048).rearrange("p (t h b q) -> p t h b q", t=T, h=MLA_HEADS, b=2)
        mix = h
        e_logit, e_top, e_prob, e_mask, e_pos, e_oh0, e_oh1, e_idf = (tiles(work(16 * i, 16)) for i in range(8))
        e_idx = tiles(work(128, 16)).bitcast(U32)
        e_d, e_g0, e_g1, e_cnt, e_cntx = work(144, 2), work(146, 2), work(148, 2), work(150, 1), work(151, 2)
        e_rounds = work(153, 1).bitcast(I32)
        e_P, e_G = tiles(work(256, T * CAP)), tiles(work(512, T * CAP))
        e_GT = work(768, 256)[0:CAP, :]
        e_hi, e_lo = left_hi[:, :, 0:CAP], left_lo[:, :, 0:CAP]
        e_silu, e_hid = ([work(1024 * n + 512 * i, 512)[0:CAP, :] for i in range(2)] for n in (1, 2))
        e_y = work(3072, 1024)[0:CAP, :]
        fin_gain, e_gain = work(4096, 1024), work(5120, 1024)

        block = ctx.enter_context(nc.Block())
        dma = ctx.enter_context(nc.allow_non_contiguous_dma("vectors laid over partitions, small"))

        expert_parts = [("gate", 0), ("up", 0)]
        for s in range(1, MOE_STEPS):
            expert_parts += [("gate", s), ("up", s), ("down", s - 1)]
        expert_parts.append(("down", MOE_STEPS - 1))
        part_end = {part: 4 * n + 4 for n, part in enumerate(expert_parts)}

        def expert_source(i, e):
            (kind, s), second = expert_parts[i // 2], i % 2
            if kind == "down":
                at = s * FF_STEP + second * 2 * P
                return A["moe_w_down"][e, at:at + 2 * P, :].rearrange("(k p) n -> p k n", p=P)
            w = A[f"moe_w_{kind}"][e].rearrange("(k p) n -> p k n", p=P)
            return w[:, 4 * second:4 * second + 4, s * FF_STEP:(s + 1) * FF_STEP]

        def expert_shape(i):
            return (2, D) if expert_parts[i // 2][0] == "down" else (4, FF_STEP)

        def expert_piece(j):
            i = j // 2
            k, n = expert_shape(i)
            half = k // 2
            return slot(i % SLOTS, k, n)[:, (j % 2) * half:(j % 2 + 1) * half, :]

        def expert_buffer(store, j):
            k, n = expert_shape((j % MOE_SUBS) // 2)
            return buffer(store, USED0 + j, k // 2, n)

        @block.sync
        def _(sp):
            sp.dma_start(x, A["x"].rearrange("a (t p) d -> p (a t) d", p=P)).then_inc(sem("x_landed"), 16)
            for i, (src, k, width) in enumerate(loads):
                if i >= DENSE_SLOTS:
                    sp.wait_ge(sem(load_freed[i - DENSE_SLOTS][0]), load_freed[i - DENSE_SLOTS][1])
                sp.dma_start(slot(slot_of[i], k, width), src).then_inc(sem(f"landed{slot_of[i]}"), 16)

            def load(e, i):
                sp.dma_start(slot(i % SLOTS, *expert_shape(i)), expert_source(i, e)) \
                    .then_inc(sem(f"expert_landed{i % SLOTS}"), 16)

            def freed(it, i):
                sp.wait_ge(sem("w_lo_by_vector"), it * MOE_SUBS + (LO0 + 2 * i + 2))

            def own(it, e):
                freed(it, 1)
                load(e, SLOTS)
                load(e, SLOTS + 1)
                for i in range(SLOTS + 2, MOE_LOADS):
                    freed(it, i - SLOTS)
                    load(e, i)

            def one_round(first):
                with sp.Fori(0, EXPERTS - 1) as e:
                    it = first + e
                    own(it, e)
                    for i in range(SLOTS):
                        freed(it, i + MOE_LOADS - SLOTS)
                        load(e + 1, i)
                own(first + EXPERTS - 1, EXPERTS - 1)

            for i in range(SLOTS):
                if i < DENSE_SLOTS:
                    last = max(n for n in range(len(loads)) if slot_of[n] == i)
                    sp.wait_ge(sem(load_freed[last][0]), load_freed[last][1])
                else:
                    sp.wait_ge(sem("pair_read"), pair_end["mixT_1"])
                load(0, i)
            one_round(0)
            sp.wait_ge(sem("rounds_known"), 1)
            rounds = sp.value_load(e_rounds[0:1, 0:1], min_val=1, max_val=MAX_ROUNDS)
            with sp.If(rounds > 1):
                with sp.Fori(1, rounds) as r:
                    for i in range(SLOTS):
                        freed(r * EXPERTS - 1, i + MOE_LOADS - SLOTS)
                        load(0, i)
                    one_round(r * EXPERTS)
            sp.wait_ge(sem("result"), T)
            sp.dma_start(out.rearrange("a (t p) d -> p (a t) d", p=P), x).then_inc(sem("stored"), 16)
            sp.wait_ge(sem("stored"), 16)

        @block.gpsimd
        def _(pool):
            def column(dst, vec):
                pool.dma_start(dst, vec.rearrange("(k p) -> p k", p=P)).then_inc(sem("small_landed"), 16)

            def rows(dst, src, name="small_landed"):
                pool.dma_start(dst, src).then_inc(sem(name), 16)

            rows(const_sb[:, :], A["const_table"], "first_landed")
            rows(gain_T["f0"], A["norm_mix_g"][0].rearrange("(k p) -> p k", p=P), "first_landed")
            rows(level_masks[:, :], A["level_masks"])
            for a, d in enumerate(("fwd", "bwd")):
                rows(g_up[:, a, :], A[f"gla_gate_up_{d}"][0])
                rows(g_bias[:, a, :], A[f"gla_gate_bias_{d}"][0:1, :])
            rows(g_gain, A["gla_out_norm_g"].to_broadcast([P, GLA_DV]))
            rows(s_gain[:, 0, :], A["swa_q_norm_g"].to_broadcast([P, HD]))
            rows(s_gain[:, 1, :], A["swa_k_norm_g"].to_broadcast([P, HD]))
            rows(sinks, A["swa_sinks"].to_broadcast([P, SWA_HEADS]))
            column(gain_T["f1"], A["norm_ffn_g"][0])
            for l in range(2):
                column(gain_T[f"l{l}"], A["mix_norm_2"][l])
                column(gain_T[f"g{l}"], A["ffn_norm_2"][l])
                column(c_gain[l][:, 0:3], A["q_a_norm_2"][l])
                column(c_gain[l][:, 3:5], A["kv_a_norm_2"][l])
                rows(hg_gain[l], A["hg_out_norm_2"][l:l + 1, :].to_broadcast([P, P]))
            rows(position, A["positions_2"].rearrange("a (t p) -> p (a t)", p=P))
            rows(router_w, A["moe_router_2"][0].rearrange("(k p) e -> p k e", p=P))
            for j, (_, _, piece) in enumerate(subs):
                if piece is not None and lo_count[j][0] == "w_lo_by_gpsimd":
                    w = raw(j)
                    k, n = w.shape[1:]
                    pool.wait_ge(sem("w_hi_ready"), hi_count[j])
                    pool.tensor_tensor(buffer(w_lo_sb, j, k, n), w, buffer(w_hi_sb, j, k, n).bitcast(F32),
                                       ALU.subtract).then_inc(sem("w_lo_by_gpsimd"), 1)

        FIRST_LANDED = 32
        SMALL_LANDED = 16 * (1 + 4 + 1 + 2 + 1 + 1 + 10 + 2)

        @block.tensor
        def _(pe):
            def three_passes(out, still, moving, start, stop):
                pe.matmul(out, still[0], moving[0], start=start, stop=False)
                pe.matmul(out, still[0], moving[1], start=False, stop=False)
                return pe.matmul(out, still[1], moving[0], start=False, stop=stop)

            def gemm(name, left=None):
                first, end = span[name]
                k = 0
                for j in range(first, end):
                    size, width = raw(j).shape[1:]
                    pe.wait_ge(sem(lo_count[j][0]), lo_count[j][1])
                    if left is not None:
                        pe.wait_ge(sem("pair_read"), pair_at[left] + (k + size) // 2)
                    w = [buffer(a, j, size, width) for a in (w_hi_sb, w_lo_sb)]
                    for t in range(T):
                        job = gemm_at[name] + t
                        if j == first and job >= 4:
                            pe.wait_ge(sem("gemm_read"), job - 3)
                        for i in range(size):
                            still = [a[:, k + i, t * P:(t + 1) * P] for a in (left_hi, left_lo)]
                            mm = three_passes(gemm_bank[job % 4][:, 0:width], still, [a[:, i, :] for a in w],
                                              k + i == 0, k + i == KD - 1)
                    mm.then_inc(sem("w_used"), 1)
                    k += size

            def whole_gemm(name, left):
                i = subs[span[name][0]][0]
                _, k_tiles, width = loads[i]
                w = slot(slot_of[i], k_tiles, width)
                pe.wait_ge(sem(f"landed{slot_of[i]}"), landed[i])
                for t in range(T):
                    job = gemm_at[name] + t
                    pe.wait_ge(sem("gemm_read"), job - 3)
                    for k in range(k_tiles):
                        mm = pe.matmul(gemm_bank[job % 4][:, 0:width], left(k, t), w[:, k, :],
                                       start=(k == 0), stop=(k == k_tiles - 1))
                mm.then_inc(sem("w_used"), 1)

            def pair(name, i):
                j = pair_at[name] + i
                if j >= 4:
                    pe.wait_ge(sem("pair_read"), j - 3)
                return pair_bank[j % 4]

            def transpose_all(name, source, k_tiles, first=0):
                for i in range(-(-k_tiles // 2)):
                    b = pair(name, first + i)
                    for k in range(2 * i, min(2 * i + 2, k_tiles)):
                        for t in range(T):
                            at = (k % 2) * TOKENS + t * P
                            tr = pe.transpose(b[:, at:at + P], source(k, t), ident)
                    tr.then_inc(sem("pair_full"), 1)

            def natural(a):
                return lambda k, t: a[:, t, k * P:(k + 1) * P]

            def transpose_heads(name, a):
                for t in range(T):
                    b = pair(name, t)
                    for i in range(4):
                        tr = pe.transpose(b[:, i * P:(i + 1) * P], a[:, t, i * P:(i + 1) * P], ident)
                    tr.then_inc(sem("pair_full"), 1)

            def normed(tag):
                pe.wait_ge(sem(f"h_{tag}"), T)
                transpose_all(f"hT_{tag}", natural(h), KD)

            pe.wait_ge(sem("first_landed"), FIRST_LANDED)
            normed("f0")
            gemm("gk", "hT_f0")
            gemm("gq")
            gemm("lr")
            pe.wait_ge(sem("gemm_read"), gemm_at["lr"] + T)
            b = pair("lrT", 0)
            for a in range(2):
                for t in range(T):
                    at = a * TOKENS + t * P
                    tr = pe.transpose(b[0:GLA_RANK, at:at + P], g_lr[:, t, a * GLA_RANK:(a + 1) * GLA_RANK], ident)
            tr.then_inc(sem("pair_full"), 1)
            gemm("gv0")
            pe.wait_ge(sem("small_landed"), SMALL_LANDED)
            pe.wait_ge(sem("pair_read"), pair_end["lrT"])
            for a in range(2):
                for t in range(T):
                    b = pair("z", 2 * a + t)
                    pe.matmul(b[:, :], g_lrT[:, a, t * P:(t + 1) * P], g_up[:, a, :], start=True, stop=False)
                    pe.matmul(b[:, :], ones[0:1, :], g_bias[:, a, :], start=False, stop=True) \
                        .then_inc(sem("pair_full"), 1)
            transpose_heads("gqT", g_q)
            transpose_heads("gkT", g_k)
            gemm("gv1")
            pe.wait_ge(sem("g_lg_ready"), 2)
            for a in range(2):
                for t in range(T):
                    b = pair("gb", 2 * a + t)
                    for i in range(GLA_HEADS):
                        mm = pe.matmul(b[:, i * P:(i + 1) * P], g_lg[:, a, t, i * P:(i + 1) * P], (le, ge)[a],
                                       start=True, stop=True)
                    mm.then_inc(sem("pair_full"), 1)
            for a in range(2):
                pe.matmul(pair("tail", a)[:, :], (gt, lt)[a], g_lg[:, a, a, :], start=True, stop=True) \
                    .then_inc(sem("pair_full"), 1)
            gemm("gr0")
            gemm("gr1")
            for a in range(2):
                pe.wait_ge(sem("g_dec_ready"), a + 1)
                pe.wait_ge(sem("g_inv_ready"), a + 1)
                for t in range(T):
                    b = pair("gsc", 2 * a + t)
                    for i in range(GLA_HEADS):
                        at = (t * GLA_HEADS + i) * P
                        mm = pe.matmul(b[:, i * P:(i + 1) * P], g_inv[a][:, at:at + P], g_dec[a][:, at:at + P],
                                       start=True, stop=True)
                    mm.then_inc(sem("pair_full"), 1)
            pe.wait_ge(sem("g_kt_ready"), 2)
            for a in range(2):
                for half in range(2):
                    b = pair("gst", 2 * a + half)
                    for i in range(2):
                        head = 2 * half + i
                        mm = pe.matmul(b[:, i * GLA_DV:(i + 1) * GLA_DV], g_kt[:, a, head * P:(head + 1) * P],
                                       g_v[:, a, head * GLA_DV:(head + 1) * GLA_DV], start=True, stop=True)
                    mm.then_inc(sem("pair_full"), 1)
            gemm("sq0")
            gemm("sq1")
            pe.wait_ge(sem("pair_read"), pair_end["gst"])
            for t in range(T):
                for half in range(2):
                    b = pair("go", 2 * t + half)
                    for i in range(2):
                        head = 2 * half + i
                        values = g_v[:, t, head * GLA_DV:(head + 1) * GLA_DV]
                        o = b[:, i * GLA_DV:(i + 1) * GLA_DV]
                        a = 1 - t
                        at = (t * GLA_HEADS + head) * P
                        pe.matmul(o, g_sc[:, 0, t, head, :], values, start=True, stop=False)
                        pe.matmul(o, g_sc[:, 1, t, head, :], values, start=False, stop=False)
                        mm = pe.matmul(o, g_dec[a][:, at:at + P], g_st[:, a, head, :], start=False, stop=True)
                    mm.then_inc(sem("pair_full"), 1)
            gemm("skv")
            gemm("ga0")
            gemm("ga1")
            gemm("gb0")
            pe.wait_ge(sem("s_rot"), T)
            transpose_all("sT", lambda k, t: s_a[:, t, k, :], 10)
            gemm("gb1")
            pe.wait_ge(sem("pair_read"), pair_end["sT"])
            for t in range(T):
                for i in range(SWA_HEADS // 2):
                    b = pair("ssc", 4 * t + i)
                    for j in range(2):
                        head = 2 * i + j
                        kv = SWA_HEADS + head // (SWA_HEADS // SWA_KV)
                        mm = pe.matmul(b[:, j * TOKENS:(j + 1) * TOKENS], s_qkT[:, head, t * P:(t + 1) * P],
                                       s_qkT[:, kv, :], start=True, stop=True)
                    mm.then_inc(sem("pair_full"), 1)
            pe.wait_ge(sem("g_out"), 1)
            transpose_all("goT", natural(tiles(g_o)), KD)
            gemm("og0", "goT")
            gemm("og1")

            def attend(names, scores, weightsT, values, heads):
                pe.wait_ge(sem(names[2]), T * heads)
                for t in range(T):
                    for i in range(heads // 2):
                        b = pair(names[0], t * heads // 2 + i)
                        for j in range(2):
                            for kt in range(2):
                                at = (2 * j + kt) * P
                                tr = pe.transpose(b[:, at:at + P], scores[:, t, 2 * i + j, kt * P:(kt + 1) * P], ident)
                        tr.then_inc(sem("pair_full"), 1)
                pe.wait_ge(sem("pair_read"), pair_end[names[0]])
                for t in range(T):
                    for i in range(heads // 4):
                        b = pair(names[1], t * heads // 4 + i)
                        for j in range(4):
                            for kt in range(2):
                                mm = pe.matmul(b[:, j * P:(j + 1) * P], weightsT[:, t, 4 * i + j, kt, :],
                                               values(kt, 4 * i + j), start=(kt == 0), stop=(kt == 1))
                        mm.then_inc(sem("pair_full"), 1)

            attend(("sP", "so", "s_exp"), s_sc, s_pT,
                   lambda kt, head: s_v[:, kt, (head // 4) * HD:(head // 4 + 1) * HD], SWA_HEADS)
            pe.wait_ge(sem("pair_read"), pair_end["so"])
            transpose_all("soT", natural(s_o), KD)
            gemm("os0", "soT")
            gemm("os1")
            pe.wait_ge(sem("merged"), 1)
            transpose_all("mT", natural(y_gla), KD)
            gemm("wo0", "mT")
            gemm("wo1")

            def ffn(tag, norm):
                def down(u, last):
                    pe.wait_ge(sem(f"{tag}_hid"), u + 1)
                    hid = [tiles(a[u % 2]) for a in (hid_hi, hid_lo)]
                    first = span[f"{tag}_down{u}"][0]
                    for i in range(2):
                        pe.wait_ge(sem(lo_count[first + i][0]), lo_count[first + i][1])
                        w = [buffer(a, first + i, 1, D) for a in (w_hi_sb, w_lo_sb)]
                        for t in range(T):
                            for half in range(2):
                                mm = three_passes(pair_bank[2 * t + half][:, :],
                                                  [a[:, i, t * P:(t + 1) * P] for a in hid],
                                                  [a[:, 0, half * 512:(half + 1) * 512] for a in w],
                                                  u == 0 and i == 0, last and i == 1)
                        mm.then_inc(sem("w_used"), 1)

                for u in range(FFN_UNITS):
                    for kind in range(2):
                        if u >= 2:
                            pe.wait_ge(sem(f"{tag}_hid"), u - 1)
                        b = gemm_bank[2 * (u % 2) + kind]
                        first = span[f"{tag}_{('gate', 'up')[kind]}{u}"][0]
                        for i in range(2):
                            pe.wait_ge(sem(lo_count[first + i][0]), lo_count[first + i][1])
                            w = [buffer(a, first + i, KD, P) for a in (w_hi_sb, w_lo_sb)]
                            for k in range(KD):
                                if u + kind + i == 0 and k % 2 == 0:
                                    pe.wait_ge(sem("pair_read"), pair_at[f"hT_{norm}"] + k // 2 + 1)
                                mm = three_passes(b[:, i * TOKENS:(i + 1) * TOKENS], [a[:, k, :] for a in w],
                                                  (left_hi[:, k, :], left_lo[:, k, :]), k == 0, k == KD - 1)
                            mm.then_inc(sem("w_used"), 1)
                    if u >= 1:
                        down(u - 1, False)
                down(FFN_UNITS - 1, True)

            pe.wait_ge(sem("gemm_read"), gemm_at["wo1"] + T)
            normed("f1")
            ffn("f1", "f1")

            for l in range(2):
                if l == 1:
                    pe.wait_ge(sem("f2_hid"), FFN_UNITS)
                normed(f"l{l}")
                for name in ("hf", "c0", "c1", "hi", "hq", "hg"):
                    gemm(f"{name}_{l}", f"hT_l{l}" if name == "hf" else None)
                pe.wait_ge(sem(f"n_k_ready_{l}"), 1)
                transpose_heads(f"hkT_{l}", n_k)
                pe.wait_ge(sem(f"n_lf_ready_{l}"), 1)
                for t in range(T):
                    b = pair(f"hb_{l}", t)
                    for i in range(HG_HEADS):
                        mm = pe.matmul(b[:, i * P:(i + 1) * P], n_lf[:, t, i * P:(i + 1) * P], le,
                                       start=True, stop=True)
                    mm.then_inc(sem("pair_full"), 1)
                pe.matmul(pair(f"ht_{l}", 0)[:, :], gt, n_lf[:, 0, :], start=True, stop=True) \
                    .then_inc(sem("pair_full"), 1)
                pe.wait_ge(sem(f"c_normed_{l}"), T * 2)
                transpose_all(f"cT_{l}", natural(n_c), 5)
                pe.wait_ge(sem("gemm_read"), gemm_at[f"hg_{l}"] + T)
                transpose_heads(f"hqT_{l}", n_q)
                pe.wait_ge(sem("pair_read"), pair_end[f"cT_{l}"])
                for i in range(2):
                    whole_gemm(f"qb{i}_{l}", lambda k, t: n_cT[:, k, t * P:(t + 1) * P])
                for i in range(2):
                    whole_gemm(f"kvb{i}_{l}", lambda k, t: n_cT[:, 3 + k, t * P:(t + 1) * P])
                pe.wait_ge(sem("pair_read"), pair_end[f"hqT_{l}"])
                for n in range(len(LEVELS) + 1):
                    if n:
                        pe.wait_ge(sem(f"level_ready_{l}"), 2 * n)
                    for t in range(T):
                        b = pair(f"hlev_{l}", T * n + t)
                        for i in range(HG_HEADS):
                            at = (t * HG_HEADS + i) * P
                            key, query = (n_X[n % 2], n_X[n % 2]) if n else (n_kT, n_qT)
                            mm = pe.matmul(b[:, i * P:(i + 1) * P], key[:, at:at + P], query[:, at:at + P],
                                           start=True, stop=True)
                        mm.then_inc(sem("pair_full"), 1)
                pe.wait_ge(sem(f"n_kt_ready_{l}"), 1)
                b = pair(f"hst_{l}", 0)
                for i in range(HG_HEADS):
                    mm = pe.matmul(b[:, i * P:(i + 1) * P], n_kt[:, i * P:(i + 1) * P], n_v[:, 0, i * P:(i + 1) * P],
                                   start=True, stop=True)
                mm.then_inc(sem("pair_full"), 1)
                pe.wait_ge(sem("pair_read"), pair_end[f"hst_{l}"])
                pe.wait_ge(sem(f"n_qd_ready_{l}"), 1)
                for t in range(T):
                    b = pair(f"ho_{l}", t)
                    for i in range(HG_HEADS):
                        at = (t * HG_HEADS + i) * P
                        mm = pe.matmul(b[:, i * P:(i + 1) * P], n_at[:, at:at + P], n_v[:, t, i * P:(i + 1) * P],
                                       start=True, stop=(t == 0))
                        if t == 1:
                            mm = pe.matmul(b[:, i * P:(i + 1) * P], n_qd[:, i * P:(i + 1) * P],
                                           n_st[:, i * P:(i + 1) * P], start=False, stop=True)
                    mm.then_inc(sem("pair_full"), 1)
                pe.wait_ge(sem(f"m_rot_{l}"), 2 * T)
                transpose_all(f"mqT_{l}", lambda k, t: n_qm[:, t, k * 192:k * 192 + NOPE], MLA_HEADS)
                transpose_all(f"mkT_{l}", lambda k, t: n_kvm[:, t, k * 256:k * 256 + NOPE], MLA_HEADS)
                for i in range(3):
                    b = pair(f"mpT_{l}", i)
                    for k in range(2 * i, min(2 * i + 2, MLA_HEADS + 1)):
                        for t in range(T):
                            src = n_qm[:, t, k * 192 + NOPE:(k + 1) * 192] if k < MLA_HEADS \
                                else n_c[:, t, Q_RANK + KV_RANK:Q_RANK + KV_RANK + ROPE]
                            at = (k % 2) * TOKENS + t * P
                            tr = pe.transpose(b[0:ROPE, at:at + P], src, ident)
                    tr.then_inc(sem("pair_full"), 1)
                pe.wait_ge(sem("pair_read"), pair_end[f"mpT_{l}"])
                for t in range(T):
                    for i in range(MLA_HEADS // 2):
                        b = pair(f"msc_{l}", 2 * t + i)
                        for j in range(2):
                            head = 2 * i + j
                            o = b[:, j * TOKENS:(j + 1) * TOKENS]
                            pe.matmul(o, n_mqT[:, head, t * P:(t + 1) * P], n_mkT[:, head, :], start=True, stop=False)
                            mm = pe.matmul(o, n_pqT[:, head, t * P:(t + 1) * P], n_pkT, start=False, stop=True)
                        mm.then_inc(sem("pair_full"), 1)
                attend((f"mP_{l}", f"mo_{l}", f"m_exp_{l}"), n_sc, n_pT,
                       lambda kt, head: n_kvm[:, kt, head * 256 + NOPE:(head + 1) * 256], MLA_HEADS)
                pe.wait_ge(sem(f"hg_mixed_{l}"), T)
                pe.wait_ge(sem("pair_read"), pair_end[f"mo_{l}"])
                transpose_all(f"mixT_{l}", natural(mix), KD)
                gemm(f"wo0_{l}", f"mixT_{l}")
                gemm(f"wo1_{l}")
                pe.wait_ge(sem("gemm_read"), gemm_at[f"wo1_{l}"] + T)
                normed(f"g{l}")
                if l == 0:
                    ffn("f2", "g0")

            pe.wait_ge(sem("pair_read"), pair_end["hT_g1"])
            b = pair("router", 0)
            for t in range(T):
                for n, part in enumerate((left_hi, left_lo)):
                    for k in range(KD):
                        mm = pe.matmul(b[:, t * EXPERTS:(t + 1) * EXPERTS], part[:, k, t * P:(t + 1) * P].bitcast(F32),
                                       router_w[:, k, :], start=(n == 0 and k == 0), stop=(n == 1 and k == KD - 1))
            mm.then_inc(sem("pair_full"), 1)
            pe.wait_ge(sem("e_mask_ready"), 1)
            b = pair("ranks", 0)
            pe.matmul(b[:, 0:8], lt, e_mask[:, 0, :], start=True, stop=True)
            pe.matmul(b[:, 8:16], ones, e_mask[:, 0, :], start=True, stop=False)
            pe.matmul(b[:, 8:16], lt, e_mask[:, 1, :], start=False, stop=True)
            pe.matmul(b[:, 16:24], ones, e_mask[:, 0, :], start=True, stop=False)
            pe.matmul(b[:, 16:24], ones, e_mask[:, 1, :], start=False, stop=True).then_inc(sem("pair_full"), 1)
            pe.wait_ge(sem("pair_read"), pair_end["ranks"])

            y_bank, misc = pair_bank[0:2], pair_bank[2:4]

            def gather(number):
                pe.wait_ge(sem("e_placed"), T * number + T)
                for i in range(2):
                    for k in range(4 * i, 4 * i + 4):
                        for t in range(T):
                            mm = pe.matmul(gemm_bank[2 + i][:, (k % 4) * CAP:(k % 4 + 1) * CAP],
                                           h[:, t, k * P:(k + 1) * P], e_P[:, t, :], start=(t == 0), stop=(t == T - 1))
                    mm.then_inc(sem("e_gathered"), 1)

            def expert(it, more):
                def piece(j):
                    pe.wait_ge(sem("w_lo_by_vector"), it * MOE_SUBS + (LO0 + j + 1))
                    return [expert_buffer(a, j) for a in (w_hi_sb, w_lo_sb)]

                def into_hidden(kind, s):
                    b = gemm_bank[2 * (s % 2) + (kind == "up")]
                    for i in range(4):
                        w = piece(part_end[kind, s] - 4 + i)
                        for k in range(2 * i, 2 * i + 2):
                            mm = three_passes(b[0:CAP, :], (e_hi[:, k, :], e_lo[:, k, :]), [a[:, k % 2, :] for a in w],
                                              k == 0, k == KD - 1)
                        mm.then_inc(sem("w_used"), 1)

                def turn(s):
                    pe.wait_ge(sem("e_hid_ready"), it * MOE_STEPS + s + 1)
                    if s == 0:
                        pe.wait_ge(sem("e_added"), it * 4 + 4)
                    for i in range(4):
                        tr = pe.transpose(misc[s % 2][:, i * CAP:(i + 1) * CAP], e_hid[s % 2][:, i * P:(i + 1) * P],
                                          ident[0:CAP, 0:CAP])
                    tr.then_inc(sem("e_hid_turned"), 1)

                def down(s):
                    pe.wait_ge(sem("e_hid_split"), it * MOE_STEPS + s + 1)
                    hid = [tiles(a[s % 2], 4) for a in (hid_hi, hid_lo)]
                    for i in range(4):
                        w = piece(part_end["down", s] - 4 + i)
                        for half in range(2):
                            mm = three_passes(y_bank[half][0:CAP, :], [a[:, i, :] for a in hid],
                                              [a[:, 0, half * 512:(half + 1) * 512] for a in w],
                                              s == 0 and i == 0, s == MOE_STEPS - 1 and i == 3)
                        mm.then_inc(sem("w_used"), 1)

                pe.wait_ge(sem("e_x_ready"), it * 2 + 2)
                into_hidden("gate", 0)
                into_hidden("up", 0)
                for s in range(MOE_STEPS - 1):
                    into_hidden("gate", s + 1)
                    turn(s)
                    into_hidden("up", s + 1)
                    down(s)
                if more:
                    gather(it + 1)
                turn(MOE_STEPS - 1)
                pe.wait_ge(sem("e_weighted"), it * T + T)
                for t in range(T):
                    tr = pe.transpose(misc[1][0:CAP, t * P:(t + 1) * P], e_G[:, t, :], ident)
                tr.then_inc(sem("e_turned"), 1)
                down(MOE_STEPS - 1)
                pe.wait_ge(sem("e_GT_ready"), it + 1)
                pe.wait_ge(sem("e_y0_ready"), it + 1)
                for half in range(2):
                    if half == 1:
                        pe.wait_ge(sem("e_y1_ready"), it + 1)
                    for t in range(T):
                        pe.matmul((misc, y_bank)[half][t][:, :], e_GT[:, t * P:(t + 1) * P],
                                  e_y[:, half * 512:(half + 1) * 512], start=True, stop=True) \
                            .then_inc(sem("e_scattered"), 1)

            def one_round(r):
                gather(r * EXPERTS)
                with pe.Fori(0, EXPERTS - 1) as e:
                    expert(r * EXPERTS + e, True)
                expert(r * EXPERTS + (EXPERTS - 1), False)

            one_round(0)
            pe.wait_ge(sem("rounds_known"), 1)
            rounds = pe.value_load(e_rounds[0:1, 0:1], min_val=1, max_val=MAX_ROUNDS)
            with pe.If(rounds > 1):
                with pe.Fori(1, rounds) as r:
                    one_round(r)

        @block.scalar
        def _(act):
            told = counter()

            def link(instruction):
                instruction.then_inc(sem("scalar_step"), 1)
                act.wait_ge(sem("scalar_step"), told("scalar_step"))

            def norm(tag, ready):
                act.wait_ge(sem(ready[0]), ready[1])
                for t in range(T):
                    act.activation(h[:, t, :], x[:, t, :], ACT.Square, accum_out=ss[:, t:t + 1]) \
                        .then_inc(sem(f"ss_{tag}"), 1)
                    act.wait_ge(sem(f"ss_{tag}"), told(f"ss_{tag}"))
                act.wait_ge(sem(f"ms_{tag}"), 1)
                link(act.activation(rinv, ms, ACT.Ln))
                act.activation(rinv, rinv, ACT.Exp, scale=-0.5).then_inc(sem(f"rinv_{tag}"), 1)
                act.wait_ge(sem(f"rinv_{tag}"), told(f"rinv_{tag}"))

            split = [0]
            misc_bank = pair_bank[2:4]

            def expert_split(it, pieces):
                for j in pieces:
                    i = j // 2
                    if j % 2 == 0:
                        act.wait_ge(sem(f"expert_landed{i % SLOTS}"),
                                    it * (16 * MOE_LOADS // SLOTS) + 16 * (i // SLOTS + 1))
                    act.wait_ge(sem("w_used"), it * MOE_SUBS + (USED0 + j - BUFFERS + 1))
                    act.activation(expert_buffer(w_hi_sb, j), expert_piece(j % MOE_SUBS), ACT.Copy) \
                        .then_inc(sem("w_hi_ready"), 1)

            def gathered_hi(number):
                for i in range(2):
                    act.wait_ge(sem("e_gathered"), number * 2 + i + 1)
                    act.activation(e_hi[:, 4 * i:4 * i + 4, :], tiles(gemm_bank[2 + i][:, 0:4 * CAP], 4), ACT.Copy) \
                        .then_inc(sem("e_hi_ready"), 1)

            def split_to(end):
                for j in range(split[0], min(end, len(subs))):
                    i, first_of_load, piece = subs[j]
                    if piece is not None:
                        w = raw(j)
                        if first_of_load:
                            act.wait_ge(sem(f"landed{slot_of[i]}"), landed[i])
                        if j >= BUFFERS:
                            act.wait_ge(sem("w_used"), j - BUFFERS + 1)
                        act.activation(buffer(w_hi_sb, j, *w.shape[1:]), w, ACT.Copy).then_inc(sem("w_hi_ready"), 1)
                    split[0] = j + 1

            def evacuate(name, parts):
                split_to(span[name][1] + BUFFERS)
                act.wait_ge(sem("w_used"), span[name][1])
                for t in range(T):
                    j = gemm_at[name] + t
                    todo = parts(t)
                    for n, (dst, lo, hi, func, scale) in enumerate(todo):
                        ins = act.activation(dst, gemm_bank[j % 4][:, lo:hi], func, scale=scale)
                        if n == len(todo) - 1:
                            ins.then_inc(sem("gemm_read"), 1)

            def into(dst, at, width=512, func=ACT.Copy, scale=1.0):
                return lambda t: [(dst[:, t, at:at + width], 0, width, func, scale)]

            norm("f0", ("x_landed", 16))
            split_to(BUFFERS)
            evacuate("gk", into(g_k, 0))
            evacuate("gq", into(g_q, 0, scale=GLA_DK ** -0.5))
            evacuate("lr", into(g_lr, 0, 2 * GLA_RANK))
            evacuate("gv0", into(g_v, 0))
            for d in range(2):
                act.wait_ge(sem("pair_read"), pair_at["z"] + 2 * d + 2)
                link(act.activation(g_lg[:, d, :, :], g_lg[:, d, :, :], ACT.Exp, scale=-1.0))
                act.activation(g_lg[:, d, :, :], g_lg[:, d, :, :], ACT.Ln, bias=1.0).then_inc(sem("g_soft"), 1)
                act.wait_ge(sem("g_soft"), told("g_soft"))
            evacuate("gv1", into(g_v, 512))
            for d in range(2):
                act.wait_ge(sem("pair_read"), pair_at["gb"] + 2 * d + 2)
                link(act.activation(g_inv[d], g_dec[d], ACT.Exp, scale=-1.0))
                act.activation(g_dec[d], g_dec[d], ACT.Exp).then_inc(sem("g_exp"), 1)
                act.wait_ge(sem("g_exp"), told("g_exp"))
            for d in range(2):
                act.wait_ge(sem("pair_read"), pair_at["tail"] + d + 1)
                act.activation(g_kt[:, d, :], g_kt[:, d, :], ACT.Exp).then_inc(sem("g_tail_exp"), 1)
                act.wait_ge(sem("g_tail_exp"), told("g_tail_exp"))
            for i in range(2):
                evacuate(f"gr{i}", into(g_sr, 512 * i, func=ACT.Silu))
            for i in range(2):
                evacuate(f"sq{i}", into(s_qk_flat, 512 * i))
            evacuate("skv", lambda t: [(s_qk_flat[:, t, 1024:1280], 0, 256, ACT.Copy, 1.0),
                                       (s_v[:, t, :], 256, 512, ACT.Copy, 1.0)])

            def head_norm(tag, n):
                act.wait_ge(sem(f"head_ms_{tag}"), 1)
                link(act.activation(head_rinv[:, 0:n], head_ms[:, 0:n], ACT.Ln))
                act.activation(head_rinv[:, 0:n], head_rinv[:, 0:n], ACT.Exp, scale=-0.5) \
                    .then_inc(sem(f"head_rinv_{tag}"), 1)
                act.wait_ge(sem(f"head_rinv_{tag}"), told(f"head_rinv_{tag}"))

            head_norm("g", 8)
            act.wait_ge(sem("g_out"), 1)
            for i in range(2):
                evacuate(f"ga{i}", into(gate_a, 512 * i, func=ACT.Sigmoid))
            head_norm("s", 20)
            for i in range(2):
                evacuate(f"gb{i}", into(gate_b, 512 * i, func=ACT.Sigmoid))

            def softmax(scores, heads, negmax, ready, done, sink=None):
                act.wait_ge(sem(ready), 1)
                if sink is not None:
                    link(act.activation(sink, sink, ACT.Exp))
                for t in range(T):
                    for i in range(heads):
                        at = t * heads + i
                        act.activation(scores[:, t, i, :], scores[:, t, i, :], ACT.Exp, bias=negmax[:, at:at + 1],
                                       accum_out=row_sum[:, at:at + 1]).then_inc(sem(done), 1)

            act.wait_ge(sem("pair_read"), pair_end["sT"])
            evacuate("og0", into(y_gla, 0))
            softmax(s_sc, SWA_HEADS, row_max, "s_max_ready", "s_exp", sink_exp)
            evacuate("og1", into(y_gla, 512))
            for i in range(2):
                evacuate(f"os{i}", into(y_swa, 512 * i))
            act.wait_ge(sem("merged"), 1)
            for i in range(2):
                evacuate(f"wo{i}", into(gate_a, 512 * i))

            def ffn(tag):
                for u in range(FFN_UNITS):
                    gate_end = span[f"{tag}_gate{u}"][1]
                    split_to(gate_end + BUFFERS)
                    act.wait_ge(sem("w_used"), gate_end)
                    if u >= 2:
                        act.wait_ge(sem(f"{tag}_hid"), u - 1)
                    act.activation(f_silu[u % 2], gemm_bank[2 * (u % 2)][:, :], ACT.Silu) \
                        .then_inc(sem(f"{tag}_silu"), 1)
                split_to(ffn_range[tag][1] + BUFFERS)

            norm("f1", ("x_mixed_f", T))
            act.wait_ge(sem("pair_read"), pair_end["so"])
            act.dma_start(log_lb, A["hg_lower_bounds_2"][0:1, :].to_broadcast([P, 512])) \
                .then_inc(sem("bounds_landed"), 16)
            act.dma_start(log_rest, A["hg_lower_bounds_2"][1:2, :].to_broadcast([P, 512])) \
                .then_inc(sem("bounds_landed"), 16)
            ffn("f1")

            act.wait_ge(sem("angle_ready"), 2)
            link(act.activation(rope_sin[:, :, 32:64], rope_sin[:, :, 32:64], ACT.Sin))
            act.activation(rope_cos[:, :, 0:32], rope_cos[:, :, 0:32], ACT.Sin).then_inc(sem("sines"), 1)
            act.wait_ge(sem("sines"), told("sines"))

            for l in range(2):
                norm(f"l{l}", (f"x_ffn_{l}", 4))
                if l == 1:
                    act.wait_ge(sem("bound_abs"), 1)
                    link(act.activation(n_tmp[0][:, 0:512], n_tmp[0][:, 0:512], ACT.Exp, scale=-1.0))
                    act.activation(n_tmp[0][:, 0:512], n_tmp[0][:, 0:512], ACT.Ln, bias=1.0) \
                        .then_inc(sem("bound_soft"), 1)
                    act.wait_ge(sem("bound_soft"), told("bound_soft"))
                evacuate(f"hf_{l}", into(n_z, 0))
                act.wait_ge(sem(f"z_abs_{l}"), 1)
                link(act.activation(n_tmp[0], n_tmp[0], ACT.Exp, scale=-1.0))
                act.activation(n_tmp[0], n_tmp[0], ACT.Ln, bias=1.0).then_inc(sem(f"z_soft_{l}"), 1)
                act.wait_ge(sem(f"z_soft_{l}"), told(f"z_soft_{l}"))
                evacuate(f"c0_{l}", into(n_c, 0))
                evacuate(f"c1_{l}", into(n_c, 512, Q_RANK + KV_RANK + ROPE - 512))
                for t in range(T):
                    for n, (lo, hi) in enumerate(((0, Q_RANK), (Q_RANK, Q_RANK + KV_RANK))):
                        act.wait_ge(sem("gemm_read"), gemm_at[f"c1_{l}"] + T)
                        act.activation(n_tmp[3][:, lo:hi], n_c[:, t, lo:hi], ACT.Square,
                                       accum_out=head_ms[:, 8 + 2 * n + t:9 + 2 * n + t]) \
                                           .then_inc(sem(f"c_ss_{l}"), 1)
                        act.wait_ge(sem(f"c_ss_{l}"), told(f"c_ss_{l}"))
                if l == 1:
                    act.wait_ge(sem("mix_abs"), 1)
                    link(act.activation(n_tmp[1], n_tmp[1], ACT.Exp, scale=-1.0))
                    act.activation(n_tmp[1], n_tmp[1], ACT.Ln, bias=1.0).then_inc(sem("mix_soft"), 1)
                    act.wait_ge(sem("mix_soft"), told("mix_soft"))
                act.wait_ge(sem(f"ln_k_{l}"), 1)
                act.activation(n_k[:, :, :], n_k[:, :, :], ACT.Exp).then_inc(sem(f"n_k_ready_{l}"), 1)
                act.wait_ge(sem(f"n_k_ready_{l}"), told(f"n_k_ready_{l}"))
                act.wait_ge(sem(f"c_ms_{l}"), 1)
                link(act.activation(head_rinv[:, 8:12], head_ms[:, 8:12], ACT.Ln))
                act.activation(head_rinv[:, 8:12], head_rinv[:, 8:12], ACT.Exp, scale=-0.5) \
                    .then_inc(sem(f"c_rinv_{l}"), 1)
                act.wait_ge(sem(f"c_rinv_{l}"), told(f"c_rinv_{l}"))
                evacuate(f"hi_{l}", into(n_v, 0))
                evacuate(f"hq_{l}", into(n_q, 0, func=ACT.Silu))
                evacuate(f"hg_{l}", into(n_g, 0, func=ACT.Silu))
                act.wait_ge(sem("pair_read"), pair_end[f"ht_{l}"])
                act.activation(n_kt, n_kt, ACT.Exp).then_inc(sem(f"n_tail_exp_{l}"), 1)
                act.wait_ge(sem(f"n_tail_exp_{l}"), told(f"n_tail_exp_{l}"))
                act.activation(n_qd, n_bT[:, 512:1024], ACT.Exp).then_inc(sem(f"n_qd_exp_{l}"), 1)
                act.wait_ge(sem(f"n_qd_exp_{l}"), told(f"n_qd_exp_{l}"))
                for i in range(2):
                    evacuate(f"qb{i}_{l}", into(n_qm, 384 * i, 384))
                for i in range(2):
                    evacuate(f"kvb{i}_{l}", into(n_kvm, 512 * i))
                for n in range(1, len(LEVELS) + 1):
                    half = LEVELS[n - 1]
                    E = n_E[n % 2].rearrange("p (n s c) -> p n s c", s=2, c=half)
                    X = n_X[n % 2].rearrange("p (n s c) -> p n s c", s=2, c=half)
                    act.wait_ge(sem(f"level_diff_{l}"), n)
                    if n >= 3:
                        act.wait_ge(sem("pair_full"), pair_at[f"hlev_{l}"] + T * (n - 1))
                    act.activation(X[:, :, 0, :], E[:, :, 0, :], ACT.Exp, scale=-1.0) \
                        .then_inc(sem(f"level_exp_{l}"), 1)
                    act.wait_ge(sem(f"level_exp_{l}"), told(f"level_exp_{l}"))
                    act.activation(X[:, :, 1, :], E[:, :, 1, :], ACT.Exp).then_inc(sem(f"level_exp_{l}"), 1)
                    act.wait_ge(sem(f"level_exp_{l}"), told(f"level_exp_{l}"))
                head_norm(f"h{l}", 8)
                softmax(n_sc, MLA_HEADS, row_max, f"m_max_ready_{l}", f"m_exp_{l}")
                act.wait_ge(sem("pair_read"), pair_end[f"mixT_{l}"])
                for i in range(2):
                    evacuate(f"wo{i}_{l}", into(tiles(work(4096, 2048)), 512 * i))
                if l == 1:
                    expert_split(0, range(BUFFERS))
                norm(f"g{l}", (f"x_mixed_{l}", T))
                if l == 0:
                    ffn("f2")

            act.dma_start(e_gain, A["ffn_norm_2"][1:2, :].to_broadcast([P, D])).then_inc(sem("expert_gain_landed"), 16)
            act.dma_start(fin_gain, A["final_norm_2"].rearrange("(a n) -> a n", a=1).to_broadcast([P, D])) \
                .then_inc(sem("final_gain_landed"), 16)
            act.wait_ge(sem("e_gap"), 1)
            act.activation(e_g1, e_d, ACT.Exp).then_inc(sem("e_odds"), 1)
            act.wait_ge(sem("e_odds"), told("e_odds"))

            def expert(it, e, more):
                def finished(part):
                    act.wait_ge(sem("w_used"), it * MOE_SUBS + (USED0 + part_end[part]))

                def silu(s):
                    finished(("gate", s))
                    act.activation(e_silu[s % 2], gemm_bank[2 * (s % 2)][0:CAP, :], ACT.Silu) \
                        .then_inc(sem("e_silu_ready"), 1)

                def hidden_hi(s):
                    act.wait_ge(sem("e_hid_turned"), it * MOE_STEPS + s + 1)
                    act.activation(hid_hi[s % 2], misc_bank[s % 2][:, 0:4 * CAP], ACT.Copy) \
                        .then_inc(sem("e_hid_hi"), 1)

                at = BUFFERS
                for s in range(MOE_STEPS):
                    until = part_end["gate", s] + BUFFERS
                    expert_split(it, range(at, until))
                    silu(s)
                    if s >= 1:
                        expert_split(it, range(until, until + 1))
                        until += 1
                        hidden_hi(s - 1)
                    at = until
                expert_split(it, range(at, MOE_SUBS))
                hidden_hi(MOE_STEPS - 1)
                if more:
                    gathered_hi(it + 1)
                    expert_split(it, range(MOE_SUBS, MOE_SUBS + BUFFERS))
                finished(("down", MOE_STEPS - 1))
                act.activation(e_y[:, 0:512], pair_bank[0][0:CAP, :], ACT.Copy).then_inc(sem("e_y0_ready"), 1)

            def one_round(r, again):
                if again:
                    expert_split(r * EXPERTS, range(BUFFERS))
                gathered_hi(r * EXPERTS)
                with act.Fori(0, EXPERTS - 1) as e:
                    expert(r * EXPERTS + e, e, True)
                expert(r * EXPERTS + (EXPERTS - 1), EXPERTS - 1, False)

            one_round(0, False)
            act.wait_ge(sem("rounds_known"), 1)
            rounds = act.value_load(e_rounds[0:1, 0:1], min_val=1, max_val=MAX_ROUNDS)
            with act.If(rounds > 1):
                with act.Fori(1, rounds) as r:
                    one_round(r, True)
            act.wait_ge(sem("x_complete"), 1)
            for t in range(T):
                act.activation(h[:, t, :], x[:, t, :], ACT.Square, accum_out=ss[:, t:t + 1]) \
                    .then_inc(sem("ss_last"), 1)
                act.wait_ge(sem("ss_last"), told("ss_last"))
            act.wait_ge(sem("ms_last"), 1)
            link(act.activation(rinv, ms, ACT.Ln))
            act.activation(rinv, rinv, ACT.Exp, scale=-0.5).then_inc(sem("rinv_last"), 1)
            act.wait_ge(sem("rinv_last"), told("rinv_last"))

        @block.vector
        def _(dve):
            told = counter()

            def link(instruction):
                instruction.then_inc(sem("vector_step"), 1)
                dve.wait_ge(sem("vector_step"), told("vector_step"))
            TWO_PI = 2 * np.pi

            def bank_of(name, i):
                j = pair_at[name] + i
                dve.wait_ge(sem("pair_full"), j + 1)
                return pair_bank[j % 4]

            def copy_out(name, i, dst, rows=P, width=512):
                dve.tensor_copy(dst, bank_of(name, i)[0:rows, 0:width]).then_inc(sem("pair_read"), 1)
                dve.wait_ge(sem("pair_read"), told("pair_read"))

            def mul(dst, one, two, name="vector_step"):
                dve.tensor_tensor(dst, one, two, ALU.mult).then_inc(sem(name), 1)
                dve.wait_ge(sem(name), told(name))

            def mean(dst, src, count, name):
                dve.tensor_scalar(dst, src, 1.0 / count, EPS, ALU.mult, ALU.add).then_inc(sem(name), 1)
                dve.wait_ge(sem(name), told(name))

            def negate(dst, src, name="vector_step"):
                dve.tensor_scalar(dst, src, -1.0, None, ALU.mult).then_inc(sem(name), 1)
                dve.wait_ge(sem(name), told(name))

            def absolute(dst, src, name="vector_step"):
                dve.scalar_tensor_tensor(dst, src, -1.0, src, ALU.mult, ALU.max).then_inc(sem(name), 1)
                dve.wait_ge(sem(name), told(name))

            def split_out(name, gain=None):
                for i in range(KD // 2):
                    b = tiles(bank_of(name, i)[:, :], 2)
                    k = slice(2 * i, 2 * i + 2)
                    hi, lo = left_hi[:, k, :], left_lo[:, k, :]
                    if gain is None:
                        link(dve.tensor_copy(hi, b))
                        dve.tensor_tensor(lo, b, hi.bitcast(F32), ALU.subtract).then_inc(sem("pair_read"), 1)
                    else:
                        mul(hi, b, over(gain[:, k], 2, TOKENS))
                        for n in range(2):
                            ins = dve.scalar_tensor_tensor(lo[:, n, :], b[:, n, :], gain[:, 2 * i + n:2 * i + n + 1],
                                                           hi[:, n, :].bitcast(F32), ALU.mult, ALU.subtract)
                        ins.then_inc(sem("pair_read"), 1)
                    dve.wait_ge(sem("pair_read"), told("pair_read"))

            def expert_lo(it, pieces):
                for j in pieces:
                    dve.wait_ge(sem("w_hi_ready"), it * MOE_SUBS + (HI0 + j + 1))
                    dve.tensor_tensor(expert_buffer(w_lo_sb, j), expert_piece(j % MOE_SUBS),
                                      expert_buffer(w_hi_sb, j).bitcast(F32), ALU.subtract) \
                        .then_inc(sem("w_lo_by_vector"), 1)

            low = [0]

            def lo_to(end):
                for j in range(low[0], end):
                    if subs[j][2] is not None and lo_count[j][0] == "w_lo_by_vector":
                        w = raw(j)
                        dve.wait_ge(sem("w_hi_ready"), hi_count[j])
                        dve.tensor_tensor(buffer(w_lo_sb, j, *w.shape[1:]), w,
                                          buffer(w_hi_sb, j, *w.shape[1:]).bitcast(F32), ALU.subtract) \
                            .then_inc(sem("w_lo_by_vector"), 1)
                    low[0] = j + 1

            def norm(tag):
                dve.wait_ge(sem(f"ss_{tag}"), T)
                mean(ms, ss, D, f"ms_{tag}")
                dve.wait_ge(sem(f"rinv_{tag}"), 1)
                for t in range(T):
                    dve.tensor_scalar(h[:, t, :], x[:, t, :], rinv[:, t:t + 1], None, ALU.mult) \
                        .then_inc(sem(f"h_{tag}"), 1)
                    dve.wait_ge(sem(f"h_{tag}"), told(f"h_{tag}"))
                split_out(f"hT_{tag}", gain_T[tag])

            dve.wait_ge(sem("first_landed"), FIRST_LANDED)
            norm("f0")
            copy_out("lrT", 0, g_lrT[:, :, :].rearrange("p a c -> p (a c)"), GLA_RANK)
            for a in range(2):
                for t in range(T):
                    b = bank_of("z", 2 * a + t)
                    dve.tensor_scalar(g_lg[:, a, t, :], b[:, :], -30.0, None, ALU.max).then_inc(sem("pair_read"), 1)
                    dve.wait_ge(sem("pair_read"), told("pair_read"))
            for t in range(T):
                copy_out("gqT", t, g_qT[:, t * 512:(t + 1) * 512])
            for t in range(T):
                copy_out("gkT", t, g_kT[:, t * 512:(t + 1) * 512])
            for a in range(2):
                dve.wait_ge(sem("g_soft"), a + 1)
                dve.tensor_scalar(g_lg[:, a, :, :], g_lg[:, a, :, :], -1.0 / 16, -0.5, ALU.mult, ALU.max) \
                    .then_inc(sem("g_lg_ready"), 1)
                dve.wait_ge(sem("g_lg_ready"), told("g_lg_ready"))
            for a in range(2):
                for t in range(T):
                    copy_out("gb", 2 * a + t, g_dec[a][:, t * 512:(t + 1) * 512])
            for a in range(2):
                copy_out("tail", a, g_kt[:, a, :])
            for a in range(2):
                dve.wait_ge(sem("g_exp"), a + 1)
                mul(g_inv[a], g_inv[a], g_kT, "g_inv_ready")
                mul(g_dec[a], g_dec[a], g_qT, "g_dec_ready")
            for a in range(2):
                dve.wait_ge(sem("g_tail_exp"), a + 1)
                mul(g_kt[:, a, :], g_kt[:, a, :], g_k[:, a, :], "g_kt_ready")
            for a in range(2):
                for t in range(T):
                    b = tiles(bank_of("gsc", 2 * a + t)[:, :], 4)
                    mul(g_sc[:, a, t, :, :], b, over((le, gt)[a], 1, 4), "pair_read")
            for i in range(4):
                copy_out("gst", i, g_st[:, i // 2, 2 * (i % 2):2 * (i % 2) + 2, :].rearrange("p h e -> p (h e)"))
            dve.wait_ge(sem("small_landed"), SMALL_LANDED)
            dve.wait_ge(sem("gemm_read"), gemm_at["gr1"] + T)
            for t in range(T):
                silu = g_sr[:, t, :].rearrange("p (h e) -> p h e", e=GLA_DV)
                mul(silu, silu, over(g_gain, 1, GLA_HEADS))
            for i in range(4):
                copy_out("go", i, g_o[:, i * 512:(i + 1) * 512])
            heads = g_o.rearrange("p (g e) -> p g e", e=GLA_DV)
            mul(g_tmp, g_o, g_o)
            link(dve.tensor_reduce(head_ms[:, 0:8], g_tmp.rearrange("p (g e) -> p g e", e=GLA_DV), AX_X, ALU.add))
            mean(head_ms[:, 0:8], head_ms[:, 0:8], GLA_DV, "head_ms_g")
            dve.wait_ge(sem("head_rinv_g"), 1)
            mul(heads, heads, over(head_rinv[:, 0:8], 2, GLA_DV))
            mul(g_o, g_o, h_sb[:, :], "g_out")
            dve.wait_ge(sem("gemm_read"), gemm_at["skv"] + T)
            flat = lambda a: a[:, :, :, :].rearrange("p t h d -> p (t h) d")
            mul(flat(s_b), flat(s_qk), flat(s_qk))
            link(dve.tensor_reduce(head_ms[:, 0:20], flat(s_b), AX_X, ALU.add))
            mean(head_ms[:, 0:20], head_ms[:, 0:20], HD, "head_ms_s")
            dve.wait_ge(sem("head_rinv_s"), 1)
            mul(flat(s_qk), flat(s_qk), over(head_rinv[:, 0:20], 2, HD))
            for t in range(T):
                mul(s_qk[:, t, 0:8, :], s_qk[:, t, 0:8, :], over(s_gain[:, 0, :], 1, 8))
                mul(s_qk[:, t, 8:10, :], s_qk[:, t, 8:10, :], over(s_gain[:, 1, :], 1, 2))
                mul(s_a[:, t, :, :], s_qk[:, t, :, :], over(swa_cos[:, t, :], 1, 10))
                mul(s_b[:, t, :, 0:64], s_qk[:, t, :, 64:128], over(swa_sin[:, t, 0:64], 1, 10))
                mul(s_b[:, t, :, 64:128], s_qk[:, t, :, 0:64], over(swa_sin[:, t, 64:128], 1, 10))
                dve.tensor_tensor(s_a[:, t, :, :], s_a[:, t, :, :], s_b[:, t, :, :], ALU.add) \
                    .then_inc(sem("s_rot"), 1)
                dve.wait_ge(sem("s_rot"), told("s_rot"))
            for i in range(5):
                copy_out("sT", i, s_qkT[:, 2 * i:2 * i + 2, :].rearrange("p k c -> p (k c)"))

            def masked_scores(name, scores, n_heads, scale, mask):
                for t in range(T):
                    for i in range(n_heads // 2):
                        b = tiles(bank_of(name, t * n_heads // 2 + i)[:, :], 2)
                        dve.scalar_tensor_tensor(scores[:, t, 2 * i:2 * i + 2, :], b, scale,
                                                 over(mask[:, t, :], 1, 2), ALU.mult, ALU.add) \
                                                     .then_inc(sem("pair_read"), 1)
                        dve.wait_ge(sem("pair_read"), told("pair_read"))

            def row_maxima(scores, n_heads):
                link(dve.tensor_reduce(row_max[:, 0:T * n_heads], scores[:, :, :, :].rearrange("p t h k -> p (t h) k"),
                                       AX_X, ALU.max))

            def attended(names, weightsT, n_heads, to):
                for t in range(T):
                    for i in range(n_heads // 2):
                        copy_out(names[0], t * n_heads // 2 + i,
                                 weightsT[:, t, 2 * i:2 * i + 2, :, :].rearrange("p h b q -> p (h b q)"))
                for t in range(T):
                    for i in range(n_heads // 4):
                        b = tiles(bank_of(names[1], t * n_heads // 4 + i)[:, :], 4)
                        at = t * n_heads + 4 * i
                        mul(to[:, t, 512 * i:512 * (i + 1)].rearrange("p (h d) -> p h d", h=4), b,
                            over(row_rec[:, at:at + 4], 2, P), "pair_read")

            masked_scores("ssc", s_sc, SWA_HEADS, HD ** -0.5, window)
            split_out("goT")
            row_maxima(s_sc, SWA_HEADS)
            sink_all = over(sinks, 1, T)
            link(dve.tensor_tensor(tiles(row_max), tiles(row_max), sink_all, ALU.max))
            link(dve.tensor_tensor(tiles(sink_exp), sink_all, tiles(row_max), ALU.subtract))
            negate(row_max, row_max, "s_max_ready")
            dve.wait_ge(sem("s_exp"), T * SWA_HEADS)
            link(dve.tensor_tensor(row_sum, row_sum, sink_exp, ALU.add))
            link(dve.reciprocal(row_rec, row_sum))
            attended(("sP", "so"), s_pT, SWA_HEADS, s_o)
            split_out("soT")
            dve.wait_ge(sem("gemm_read"), gemm_at["os1"] + T)
            mul(y_gla, y_gla, gate_a)
            mul(y_swa, y_swa, gate_b)
            dve.tensor_tensor(y_gla, y_gla, y_swa, ALU.add).then_inc(sem("merged"), 1)
            dve.wait_ge(sem("merged"), told("merged"))
            split_out("mT")

            def residual(product, last_gemm, name):
                dve.wait_ge(sem("gemm_read"), gemm_at[last_gemm] + T)
                for t in range(T):
                    dve.tensor_tensor(x[:, t, :], x[:, t, :], product[:, t, :], ALU.add).then_inc(sem(name), 1)
                    dve.wait_ge(sem(name), told(name))

            def ffn(tag, done):
                for u in range(FFN_UNITS):
                    up_end = span[f"{tag}_up{u}"][1]
                    lo_to(min(up_end + BUFFERS, ffn_range[tag][1]))
                    dve.wait_ge(sem(f"{tag}_silu"), u + 1)
                    dve.wait_ge(sem("w_used"), up_end)
                    mul(f_hid, f_silu[u % 2], gemm_bank[2 * (u % 2) + 1][:, :])
                    link(dve.tensor_copy(hid_hi[u % 2], f_hid))
                    dve.tensor_tensor(hid_lo[u % 2], f_hid, hid_hi[u % 2].bitcast(F32), ALU.subtract) \
                        .then_inc(sem(f"{tag}_hid"), 1)
                    dve.wait_ge(sem(f"{tag}_hid"), told(f"{tag}_hid"))
                lo_to(ffn_range[tag][1])
                dve.wait_ge(sem("w_used"), ffn_range[tag][1])
                for t in range(T):
                    for half in range(2):
                        part = x[:, t, half * 512:(half + 1) * 512]
                        dve.tensor_tensor(part, part, pair_bank[2 * t + half][:, :], ALU.add).then_inc(sem(done), 1)
                        dve.wait_ge(sem(done), told(done))

            residual(gate_a, "wo1", "x_mixed_f")
            norm("f1")
            ang, turns, rest = (tiles(scratch(64 * i, 64)) for i in range(3))
            link(dve.tensor_copy(pos_f, position))
            for t in range(T):
                link(dve.tensor_scalar(ang[:, t, :], inv_freq, pos_f[:, t:t + 1], None, ALU.mult))
            magic = float(1.5 * 2 ** 23)
            link(dve.tensor_scalar(turns, ang, 1.0 / TWO_PI, None, ALU.mult))
            link(dve.tensor_scalar(turns, turns, magic, None, ALU.add))
            link(dve.tensor_scalar(turns, turns, magic, None, ALU.subtract))
            part1 = 6.28125
            part2 = float(np.float32(round((TWO_PI - part1) * 2 ** 20) / 2 ** 20))
            for n, part in enumerate((part1, part2, TWO_PI - part1 - part2)):
                link(dve.scalar_tensor_tensor(rest, turns, -part, ang if n == 0 else rest, ALU.mult, ALU.add))
            edge = 3.1415925
            dve.tensor_scalar(rope_sin[:, :, 32:64], rest, edge, -edge, ALU.min, ALU.max) \
                .then_inc(sem("angle_ready"), 1)
            dve.wait_ge(sem("angle_ready"), told("angle_ready"))
            link(dve.tensor_scalar(rest, rest, np.pi / 2, None, ALU.add))
            link(dve.tensor_scalar(turns, rest, edge, -TWO_PI, ALU.is_gt, ALU.mult))
            link(dve.tensor_tensor(rest, rest, turns, ALU.add))
            dve.tensor_scalar(rope_cos[:, :, 0:32], rest, edge, -edge, ALU.min, ALU.max) \
                .then_inc(sem("angle_ready"), 1)
            dve.wait_ge(sem("angle_ready"), told("angle_ready"))
            ffn("f1", "x_ffn_0")
            dve.wait_ge(sem("sines"), 1)
            link(dve.tensor_copy(rope_cos[:, :, 32:64], rope_cos[:, :, 0:32]))
            negate(rope_sin[:, :, 0:32], rope_sin[:, :, 32:64])

            for l in range(2):
                norm(f"l{l}")
                if l == 1:
                    dve.wait_ge(sem("bounds_landed"), 32)
                    diff, soft = n_tmp[1][:, 0:512], n_tmp[0][:, 0:512]
                    link(dve.tensor_tensor(diff, log_rest, log_lb, ALU.subtract))
                    absolute(soft, diff, "bound_abs")
                    dve.wait_ge(sem("bound_soft"), 1)
                    link(dve.scalar_tensor_tensor(log_lb, diff, 0.0, soft, ALU.min, ALU.subtract))
                    link(dve.scalar_tensor_tensor(log_rest, diff, 0.0, soft, ALU.max, ALU.add))
                    negate(log_rest, log_rest)
                flat_z, flat_lf, flat_k = (a[:, :, :].rearrange("p t n -> p (t n)") for a in (n_z, n_lf, n_k))
                dve.wait_ge(sem("gemm_read"), gemm_at[f"hf_{l}"] + T)
                absolute(n_tmp[0], flat_z, f"z_abs_{l}")
                dve.wait_ge(sem(f"z_soft_{l}"), 1)
                link(dve.scalar_tensor_tensor(flat_lf, flat_z, 0.0, n_tmp[0], ALU.min, ALU.subtract))
                link(dve.scalar_tensor_tensor(flat_k, flat_z, 0.0, n_tmp[0], ALU.max, ALU.add))
                if l == 0:
                    negate(flat_k, flat_k, "ln_k_0")
                    dve.tensor_scalar(flat_lf, flat_lf, LN_F_FLOOR, None, ALU.max).then_inc(sem("n_lf_ready_0"), 1)
                    dve.wait_ge(sem("n_lf_ready_0"), told("n_lf_ready_0"))
                else:
                    link(dve.tensor_tensor(n_lf, n_lf, over(log_rest, 1, T), ALU.add))
                    link(dve.tensor_tensor(tiles(n_tmp[2]), over(log_lb, 1, T), n_lf, ALU.subtract))
                    absolute(n_tmp[1], n_tmp[2], "mix_abs")
                    link(dve.tensor_tensor(n_lf, n_lf, over(log_lb, 1, T), ALU.max))
                    dve.scalar_tensor_tensor(n_k, n_k, -1.0, over(log_rest, 1, T), ALU.mult, ALU.add) \
                        .then_inc(sem("ln_k_1"), 1)
                    dve.wait_ge(sem("ln_k_1"), told("ln_k_1"))
                    dve.wait_ge(sem("mix_soft"), 1)
                    link(dve.tensor_tensor(flat_lf, flat_lf, n_tmp[1], ALU.add))
                    dve.tensor_scalar(flat_lf, flat_lf, LN_F_FLOOR, None, ALU.max).then_inc(sem("n_lf_ready_1"), 1)
                    dve.wait_ge(sem("n_lf_ready_1"), told("n_lf_ready_1"))
                dve.wait_ge(sem(f"c_ss_{l}"), 2 * T)
                mean(head_ms[:, 8:10], head_ms[:, 8:10], Q_RANK, "vector_step")
                mean(head_ms[:, 10:12], head_ms[:, 10:12], KV_RANK, f"c_ms_{l}")
                dve.wait_ge(sem(f"c_rinv_{l}"), 1)
                for n, (lo, hi) in enumerate(((0, Q_RANK), (Q_RANK, Q_RANK + KV_RANK))):
                    for t in range(T):
                        at = 8 + 2 * n + t
                        dve.tensor_scalar(n_c[:, t, lo:hi], n_c[:, t, lo:hi], head_rinv[:, at:at + 1], None,
                                          ALU.mult).then_inc(sem(f"c_normed_{l}"), 1)
                        dve.wait_ge(sem(f"c_normed_{l}"), told(f"c_normed_{l}"))
                for t in range(T):
                    copy_out(f"hkT_{l}", t, n_kT[:, t * 512:(t + 1) * 512])
                for t in range(T):
                    copy_out(f"hb_{l}", t, n_bT[:, t * 512:(t + 1) * 512])
                copy_out(f"ht_{l}", 0, n_kt)
                for i in range(3):
                    n = min(2, 5 - 2 * i)
                    b = tiles(bank_of(f"cT_{l}", i)[:, 0:n * TOKENS], n)
                    mul(n_cT[:, 2 * i:2 * i + n, :], b, over(c_gain[l][:, 2 * i:2 * i + n], 2, TOKENS), "pair_read")
                for t in range(T):
                    copy_out(f"hqT_{l}", t, n_qT[:, t * 512:(t + 1) * 512])
                dve.wait_ge(sem(f"n_tail_exp_{l}"), 1)
                mul(n_kt, n_kt, n_k[:, 0, :], f"n_kt_ready_{l}")
                dve.wait_ge(sem(f"n_qd_exp_{l}"), 1)
                mul(n_qd, n_qd, n_qT[:, 512:1024], f"n_qd_ready_{l}")
                gains = n_g[:, :, :].rearrange("p t (g d) -> p (t g) d", d=P)
                dve.wait_ge(sem("gemm_read"), gemm_at[f"hg_{l}"] + T)
                mul(gains, gains, over(hg_gain[l], 1, 8))

                def blocks(a, half):
                    return a.rearrange("p (n c) -> p n c", c=2 * half)

                def halves(a, half):
                    return a.rearrange("p (n s c) -> p n s c", s=2, c=half)

                def level_diff(n):
                    half = LEVELS[n - 1]
                    if n >= 3:
                        dve.wait_ge(sem(f"level_exp_{l}"), 2 * (n - 2))
                    b = blocks(n_bT, half)
                    middle = b[:, :, half - 1]
                    dve.tensor_tensor(blocks(n_E[n % 2], half), b, over(middle, 2, 2 * half), ALU.subtract) \
                        .then_inc(sem(f"level_diff_{l}"), 1)
                    dve.wait_ge(sem(f"level_diff_{l}"), told(f"level_diff_{l}"))

                def level_scale(n):
                    half = LEVELS[n - 1]
                    dve.wait_ge(sem(f"level_exp_{l}"), 2 * n)
                    for side, other in enumerate((n_kT, n_qT)):
                        part = halves(n_X[n % 2], half)[:, :, side, :]
                        mul(part, part, halves(other, half)[:, :, side, :], f"level_ready_{l}")

                def level_take(n):
                    for t in range(T):
                        b = tiles(bank_of(f"hlev_{l}", T * n + t)[:, :], 4)
                        to = tiles(n_at[:, t * 512:(t + 1) * 512], 4)
                        if n == 0:
                            mul(to, b, over(ident, 1, 4), "pair_read")
                        else:
                            mask = over(level_masks[:, n * P:(n + 1) * P], 1, 4)
                            dve.copy_predicated(to, mask, b).then_inc(sem("pair_read"), 1)
                            dve.wait_ge(sem("pair_read"), told("pair_read"))

                level_diff(1)
                level_diff(2)
                level_take(0)
                for n in range(1, len(LEVELS) + 1):
                    level_scale(n)
                    if n + 2 <= len(LEVELS):
                        level_diff(n + 2)
                    if n >= 2:
                        level_take(n - 1)
                level_take(len(LEVELS))

                dve.wait_ge(sem("gemm_read"), gemm_at[f"kvb1_{l}"] + T)
                ra, rb = work(1280, 256), work(1536, 256)
                for t in range(T):
                    q_pe = n_qm[:, t, :].rearrange("p (h d) -> p h d", h=MLA_HEADS)[:, :, NOPE:192]
                    k_pe = n_c[:, t, Q_RANK + KV_RANK:Q_RANK + KV_RANK + ROPE].rearrange("p (h d) -> p h d", h=1)
                    for pe_part, n in ((q_pe, MLA_HEADS), (k_pe, 1)):
                        a_, b_ = (r[:, 0:n * ROPE].rearrange("p (h d) -> p h d", h=n) for r in (ra, rb))
                        mul(a_, pe_part, over(rope_cos[:, t, :], 1, n))
                        mul(b_[:, :, 0:32], pe_part[:, :, 32:64], over(rope_sin[:, t, 0:32], 1, n))
                        mul(b_[:, :, 32:64], pe_part[:, :, 0:32], over(rope_sin[:, t, 32:64], 1, n))
                        dve.tensor_tensor(pe_part, a_, b_, ALU.add).then_inc(sem(f"m_rot_{l}"), 1)
                        dve.wait_ge(sem(f"m_rot_{l}"), told(f"m_rot_{l}"))

                copy_out(f"hst_{l}", 0, n_st)
                for t in range(T):
                    copy_out(f"ho_{l}", t, mix[:, t, 512:1024])
                for t in range(T):
                    mul(tiles(n_tmp[0])[:, t, :], mix[:, t, 512:1024], mix[:, t, 512:1024])
                link(dve.tensor_reduce(head_ms[:, 0:8], n_tmp[0].rearrange("p (g d) -> p g d", d=P), AX_X, ALU.add))
                mean(head_ms[:, 0:8], head_ms[:, 0:8], P, f"head_ms_h{l}")
                dve.wait_ge(sem(f"head_rinv_h{l}"), 1)
                for t in range(T):
                    o = mix[:, t, 512:1024].rearrange("p (g d) -> p g d", d=P)
                    mul(o, o, over(head_rinv[:, 4 * t:4 * t + 4], 2, P))
                for t in range(T):
                    mul(mix[:, t, 512:1024], mix[:, t, 512:1024], n_g[:, t, :], f"hg_mixed_{l}")

                for name, to in ((f"mqT_{l}", n_mqT), (f"mkT_{l}", n_mkT)):
                    for i in range(2):
                        copy_out(name, i, to[:, 2 * i:2 * i + 2, :].rearrange("p k c -> p (k c)"))
                for i in range(2):
                    copy_out(f"mpT_{l}", i, n_pqT[:, 2 * i:2 * i + 2, :].rearrange("p k c -> p (k c)"), ROPE)
                copy_out(f"mpT_{l}", 2, n_pkT, ROPE, TOKENS)
                masked_scores(f"msc_{l}", n_sc, MLA_HEADS, (NOPE + ROPE) ** -0.5, causal)
                row_maxima(n_sc, MLA_HEADS)
                negate(row_max[:, 0:8], row_max[:, 0:8], f"m_max_ready_{l}")
                dve.wait_ge(sem(f"m_exp_{l}"), T * MLA_HEADS)
                link(dve.reciprocal(row_rec[:, 0:8], row_sum[:, 0:8]))
                attended((f"mP_{l}", f"mo_{l}"), n_pT, MLA_HEADS, mix)
                split_out(f"mixT_{l}")
                residual(tiles(work(4096, 2048)), f"wo1_{l}", f"x_mixed_{l}")
                norm(f"g{l}")
                if l == 0:
                    ffn("f2", "x_ffn_1")

            expert_lo(0, range(BUFFERS))
            dve.wait_ge(sem("expert_gain_landed"), 16)
            mul(h, h, over(e_gain, 1, T))
            dve.tensor_copy(work(0, 16), bank_of("router", 0)[:, 0:16]).then_inc(sem("pair_read"), 1)
            dve.wait_ge(sem("pair_read"), told("pair_read"))
            for t in range(T):
                link(dve.max(e_top[:, t, :], e_logit[:, t, :]))
                link(dve.max_index(e_idx[:, t, :], e_top[:, t, :], e_logit[:, t, :]))
            link(dve.tensor_copy(e_idf, e_idx))
            dve.tensor_tensor(e_d, e_top[:, :, 1], e_top[:, :, 0], ALU.subtract).then_inc(sem("e_gap"), 1)
            dve.wait_ge(sem("e_gap"), told("e_gap"))
            for t in range(T):
                for n, one_hot in enumerate((e_oh0, e_oh1)):
                    link(dve.tensor_scalar(one_hot[:, t, :], iota[:, 0:EXPERTS], e_idf[:, t, n:n + 1], None, ALU.is_equal))
            dve.tensor_tensor(e_mask, e_oh0, e_oh1, ALU.add).then_inc(sem("e_mask_ready"), 1)
            dve.wait_ge(sem("e_mask_ready"), told("e_mask_ready"))
            dve.wait_ge(sem("e_odds"), 1)
            link(dve.tensor_scalar(e_g0, e_g1, 1.0, None, ALU.add))
            link(dve.reciprocal(e_g0, e_g0))
            mul(e_g1, e_g1, e_g0)
            for t in range(T):
                link(dve.tensor_scalar(e_prob[:, t, :], e_oh0[:, t, :], e_g0[:, t:t + 1], None, ALU.mult))
                link(dve.scalar_tensor_tensor(e_prob[:, t, :], e_oh1[:, t, :], e_g1[:, t:t + 1], e_prob[:, t, :],
                                              ALU.mult, ALU.add))
            b = bank_of("ranks", 0)
            far = float(4 * TOKENS)
            link(dve.tensor_reduce(e_cnt, b[:, 16:24], AX_X, ALU.max))
            dve.scalar_tensor_tensor(e_pos, e_mask, -far, tiles(b[:, 0:16]), ALU.mult, ALU.add) \
                .then_inc(sem("pair_read"), 1)
            dve.wait_ge(sem("pair_read"), told("pair_read"))
            dve.tensor_scalar(e_pos, e_pos, far, None, ALU.add).then_inc(sem("e_added"), 4)
            dve.wait_ge(sem("e_added"), 4)
            link(dve.tensor_scalar(e_cntx[:, 0:1], e_cnt, float(CAP), 1.0, ALU.is_gt, ALU.add))
            for n in range(2, MAX_ROUNDS):
                link(dve.tensor_scalar(e_cntx[:, 1:2], e_cnt, float(n * CAP), None, ALU.is_gt))
                link(dve.tensor_tensor(e_cntx[:, 0:1], e_cntx[:, 0:1], e_cntx[:, 1:2], ALU.add))
            dve.tensor_copy(e_rounds, e_cntx[:, 0:1]).then_inc(sem("rounds_known"), 1)
            dve.wait_ge(sem("rounds_known"), told("rounds_known"))

            def place(number, e):
                for t in range(T):
                    dve.tensor_scalar(e_P[:, t, :], iota, e_pos[:, t, bass.ds(e, 1)], None, ALU.is_equal) \
                        .then_inc(sem("e_placed"), 1)
                    dve.wait_ge(sem("e_placed"), T * number + t + 1)

            def gathered_lo(number):
                for i in range(2):
                    dve.wait_ge(sem("e_hi_ready"), number * 2 + i + 1)
                    k = slice(4 * i, 4 * i + 4)
                    dve.tensor_tensor(e_lo[:, k, :], tiles(gemm_bank[2 + i][:, 0:4 * CAP], 4),
                                      e_hi[:, k, :].bitcast(F32), ALU.subtract).then_inc(sem("e_x_ready"), 1)

            def expert(it, e, more):
                def multiply(s):
                    dve.wait_ge(sem("e_silu_ready"), it * MOE_STEPS + s + 1)
                    dve.wait_ge(sem("w_used"), it * MOE_SUBS + (USED0 + part_end["up", s]))
                    dve.tensor_tensor(e_hid[s % 2], e_silu[s % 2], gemm_bank[2 * (s % 2) + 1][0:CAP, :], ALU.mult) \
                        .then_inc(sem("e_hid_ready"), 1)

                def hidden_lo(s):
                    dve.wait_ge(sem("e_hid_hi"), it * MOE_STEPS + s + 1)
                    dve.tensor_tensor(hid_lo[s % 2], pair_bank[2 + s % 2][:, 0:4 * CAP], hid_hi[s % 2].bitcast(F32),
                                      ALU.subtract).then_inc(sem("e_hid_split"), 1)

                at = BUFFERS
                for s in range(MOE_STEPS):
                    if s >= 1:
                        until = part_end["gate", s] + BUFFERS + 1
                        expert_lo(it, range(at, until))
                        hidden_lo(s - 1)
                        at = until
                    until = part_end["up", s] + BUFFERS
                    expert_lo(it, range(at, until))
                    multiply(s)
                    at = until
                    if s == 2:
                        for t in range(T):
                            dve.tensor_scalar(e_G[:, t, :], e_P[:, t, :], e_prob[:, t, bass.ds(e, 1)], None, ALU.mult) \
                                .then_inc(sem("e_weighted"), 1)
                            dve.wait_ge(sem("e_weighted"), T * it + t + 1)
                        if more:
                            place(it + 1, e + 1)
                expert_lo(it, range(at, MOE_SUBS))
                hidden_lo(MOE_STEPS - 1)
                dve.wait_ge(sem("e_turned"), it + 1)
                dve.tensor_copy(e_GT, pair_bank[3][0:CAP, 0:TOKENS]).then_inc(sem("e_GT_ready"), 1)
                if more:
                    gathered_lo(it + 1)
                    expert_lo(it, range(MOE_SUBS, MOE_SUBS + BUFFERS))
                dve.wait_ge(sem("w_used"), it * MOE_SUBS + (USED0 + MOE_SUBS))
                dve.tensor_copy(e_y[:, 512:1024], pair_bank[1][0:CAP, :]).then_inc(sem("e_y1_ready"), 1)
                for half in range(2):
                    for t in range(T):
                        q = 2 * half + t
                        dve.wait_ge(sem("e_scattered"), 4 * it + q + 1)
                        part = x[:, t, half * 512:(half + 1) * 512]
                        b = pair_bank[(2, 0)[half] + t]
                        dve.tensor_tensor(part, part, b[:, :], ALU.add).then_inc(sem("e_added"), 1)
                dve.wait_ge(sem("e_added"), 4 * it + 8)

            def one_round(r, again):
                if again:
                    expert_lo(r * EXPERTS, range(BUFFERS))
                place(r * EXPERTS, 0)
                gathered_lo(r * EXPERTS)
                with dve.Fori(0, EXPERTS - 1) as e:
                    expert(r * EXPERTS + e, e, True)
                expert(r * EXPERTS + (EXPERTS - 1), EXPERTS - 1, False)

            one_round(0, False)
            rounds = dve.value_load(e_rounds[0:1, 0:1], min_val=1, max_val=MAX_ROUNDS)
            with dve.If(rounds > 1):
                with dve.Fori(1, rounds) as r:
                    dve.tensor_scalar(e_pos, e_pos, float(CAP), None, ALU.subtract).then_inc(sem("e_shifted"), 1)
                    dve.wait_ge(sem("e_shifted"), r)
                    one_round(r, True)
            dve.memset(ss, 0.0).then_inc(sem("x_complete"), 1)
            dve.wait_ge(sem("x_complete"), told("x_complete"))
            dve.wait_ge(sem("ss_last"), T)
            mean(ms, ss, D, "ms_last")
            dve.wait_ge(sem("rinv_last"), 1)
            dve.wait_ge(sem("final_gain_landed"), 16)
            for t in range(T):
                link(dve.tensor_scalar(x[:, t, :], x[:, t, :], rinv[:, t:t + 1], None, ALU.mult))
                mul(x[:, t, :], x[:, t, :], fin_gain, "result")


_OUTS = [((1, TOKENS, D), "float32")]


def kernel(**inputs):
    import concourse.bacc as _bacc
    from concourse.bass_utils import run_bass_kernel_spmd as _run

    nc = _bacc.Bacc("TRN2", target_bir_lowering=False, num_devices=1)
    table, masks = constants()
    arrays, A = {}, {}
    for name, value in {**inputs, "const_table": table, "level_masks": masks}.items():
        a = np.ascontiguousarray(value)
        arrays[f"in_{name}"] = a
        A[name] = nc.dram_tensor(f"in_{name}", a.shape, mybir.dt.from_np(a.dtype), kind="ExternalInput").ap()
    out = nc.dram_tensor("out_0", _OUTS[0][0], F32, kind="ExternalOutput").ap()
    for name in ("w_in", "w_o_gla", "w_o_swa", "w_out"):
        A[name] = A[name][0]
    A["f1_gate"], A["f1_up"] = A["w_ffn_in"][0][:, 0:D_FF], A["w_ffn_in"][0][:, D_FF:2 * D_FF]
    A["f1_down"] = A["w_ffn_out"][0]
    for part in ("gate", "up", "down"):
        A[f"f2_{part}"] = A[f"dense_w_{part}_2"][0]
        A[f"moe_w_{part}"] = A[f"moe_w_{part}_2"][0]
    for l in range(2):
        for name in ("w_in", "w_q_b", "w_kv_b", "w_out"):
            A[f"{name}_2_{l}"] = A[f"{name}_2"][l]
    build(nc, A, out)
    r = _run(nc, [arrays], core_ids=[0])
    return r.results[0]["out_0"]
```

```python
from contextlib import ExitStack

import numpy as np

import concourse.bass as bass
from concourse import mybir

ALU = mybir.AluOpType
ACT = mybir.ActivationFunctionType
F32 = mybir.dt.float32
F32R = mybir.dt.float32r
I32 = mybir.dt.int32
U32 = mybir.dt.uint32
AX_X = mybir.AxisListType.X

P = 128
TOKENS = 256
T = TOKENS // P
D = 1024
KD = D // P
EPS = 1e-6
MASKED = -1e30

GLA_HEADS, GLA_DK, GLA_DV, GLA_RANK = 4, 128, 256, 16
SWA_HEADS, SWA_KV, HD, WINDOW = 8, 2, 128, 128
D_FF = 2816
Q_RANK, KV_RANK, ROPE = 384, 256, 64
MLA_HEADS, NOPE, V_HEAD = 4, 128, 128
HG_HEADS = 4
EXPERTS, EXPERT_FF = 8, 3584
LEVELS = [64, 32, 16, 8, 4, 2, 1]
LN_F_FLOOR = float(np.log(1e-30))

SLOT = 2048
SUB = 1024
BUFFERS = 4
SLOTS = 7
DENSE_SLOTS = 4
CAP = 128
MAX_ROUNDS = -(-TOKENS // CAP)
FF_STEP = 512
MOE_STEPS = EXPERT_FF // FF_STEP
MOE_LOADS = 3 * MOE_STEPS * 2
MOE_SUBS = 2 * MOE_LOADS
FF_UNIT = 256
FFN_UNITS = D_FF // FF_UNIT
SCRATCH = 4 * SLOT
WORK = 13952

CONSTS = [("ident", P), ("le", P), ("ge", P), ("gt", P), ("lt", P), ("ones", P),
          ("window", T * 256), ("swa_cos", T * HD), ("swa_sin", T * HD), ("causal", T * 256), ("iota", CAP),
          ("inv_freq", ROPE // 2)]
CONST_AT = {}
CONST_WORDS = 0
for _name, _width in CONSTS:
    CONST_AT[_name] = (CONST_WORDS, _width)
    CONST_WORDS += _width


def constants():
    r, c = np.arange(P)[:, None], np.arange(P)[None, :]
    key = np.arange(256)[None, :]
    query = [r + P * t for t in range(T)]
    half = HD // 2
    inv = (np.float32(10000.0) ** (-np.arange(half, dtype=np.float32) / np.float32(half))).astype(np.float32)
    ang = np.arange(TOKENS, dtype=np.float32)[:, None] * inv[None, :]
    cos, sin = np.cos(ang), np.sin(ang)
    tiles = lambda a: a.reshape(T, P, -1).transpose(1, 0, 2).reshape(P, -1)
    inv_pe = np.float32(10000.0) ** (-np.arange(0, ROPE, 2, dtype=np.float32) / np.float32(ROPE))
    parts = {
        "le": r <= c, "ge": r >= c, "gt": r > c, "lt": r < c, "ident": r == c, "ones": np.ones((P, P)),
        "window": np.concatenate([np.where(abs(q - key) <= WINDOW, 0.0, MASKED) for q in query], 1),
        "causal": np.concatenate([np.where(key <= q, 0.0, MASKED) for q in query], 1),
        "iota": np.broadcast_to(np.arange(CAP), (P, CAP)),
        "swa_cos": tiles(np.concatenate([cos, cos], 1)), "swa_sin": tiles(np.concatenate([-sin, sin], 1)),
        "inv_freq": np.broadcast_to(inv_pe, (P, ROPE // 2)),
    }
    table = np.concatenate([np.asarray(parts[n], np.float32).reshape(P, w) for n, w in CONSTS], 1)
    masks = [(r == c)]
    for h in LEVELS:
        masks.append((r // (2 * h) == c // (2 * h)) & (r % (2 * h) < h) & (c % (2 * h) >= h))
    return np.ascontiguousarray(table), np.ascontiguousarray(np.concatenate(masks, 1).astype(np.int32))


def counter():
    counts = {}

    def told(name):
        counts[name] = counts.get(name, 0) + 1
        return counts[name]

    return told


def gemm_plan():
    plan = []

    def add(name, weight, start, width, k=KD):
        plan.append((name, weight, start, width, k))

    add("gk", "w_in", 512, 512)
    add("gq", "w_in", 0, 512)
    add("lr", "w_in", 3072, 32)
    add("gv0", "w_in", 1024, 512)
    add("gv1", "w_in", 1536, 512)
    add("gr0", "w_in", 2048, 512)
    add("gr1", "w_in", 2560, 512)
    add("sq0", "w_in", 3104, 512)
    add("sq1", "w_in", 3616, 512)
    add("skv", "w_in", 4128, 512)
    add("ga0", "w_in", 4640, 512)
    add("ga1", "w_in", 5152, 512)
    add("gb0", "w_in", 5664, 512)
    add("gb1", "w_in", 6176, 512)
    for i in range(2):
        add(f"og{i}", "w_o_gla", 512 * i, 512)
    for i in range(2):
        add(f"os{i}", "w_o_swa", 512 * i, 512)
    for i in range(2):
        add(f"wo{i}", "w_out", 512 * i, 512)
    add("FFN", "f1", 0, 0)
    for layer in range(2):
        base = Q_RANK + KV_RANK + ROPE
        w = f"w_in_2_{layer}"
        add(f"hf_{layer}", w, base + 512, 512)
        add(f"hq_{layer}", w, base, 512)
        add(f"hg_{layer}", w, base + 1536, 512)
        add(f"c0_{layer}", w, 0, 512)
        add(f"c1_{layer}", w, 512, base - 512)
        add(f"hi_{layer}", w, base + 1024, 512)
        for i in range(2):
            add(f"qb{i}_{layer}", f"w_q_b_2_{layer}", 384 * i, 384, Q_RANK // P)
        for i in range(2):
            add(f"kvb{i}_{layer}", f"w_kv_b_2_{layer}", 512 * i, 512, KV_RANK // P)
        for i in range(2):
            add(f"wo{i}_{layer}", f"w_out_2_{layer}", 512 * i, 512)
        if layer == 0:
            add("FFN", "f2", 0, 0)
    return plan


def pair_plan():
    plan = [("hT_f0", 4), ("lrT", 1), ("z", 4), ("gqT", 2), ("gkT", 2), ("gb", 4), ("tail", 2), ("gsc", 4), ("gst", 4),
            ("go", 4), ("sT", 5), ("ssc", 8), ("goT", 4), ("sP", 8), ("so", 4), ("soT", 4), ("mT", 4), ("hT_f1", 4), ("row_f1", 1)]
    for layer in range(2):
        level = [(f"hlev{n}_{layer}", T) for n in range(len(LEVELS) + 1)]
        plan += [(f"hT_l{layer}", 4), (f"hkT_{layer}", 2), (f"hb_{layer}", 2), (f"ht_{layer}", 1),
                 (f"hqT_{layer}", 2), *level[0:3], (f"cT_{layer}", 3), *level[3:5], (f"hst_{layer}", 1),
                 (f"mqT_{layer}", 2), (f"mkT_{layer}", 2), (f"mpT_{layer}", 3), *level[5:7], (f"msc0_{layer}", 2),
                 level[7], (f"msc1_{layer}", 2), (f"ho_{layer}", 2), (f"mP_{layer}", 4), (f"mo_{layer}", 2),
                 (f"mixT_{layer}", 4),
                 (f"hT_g{layer}", 4)]
        if layer == 0:
            plan += [("row_g0", 1)]
    plan += [("routerT", 1), ("router", 1), ("ranks", 1)]
    return plan


def build(nc, A, out):
    gemms = [g for g in gemm_plan() if g[0] != "FFN"]
    gemm_at = {g[0]: T * i for i, g in enumerate(gemms)}
    pair_at, pair_end, n = {}, {}, 0
    for name, banks in pair_plan():
        pair_at[name], pair_end[name] = n, n + banks
        n += banks

    loads, subs, span = [], [], {}

    def stream(name, src, k_tiles, width, cuts):
        for n, piece in enumerate(cuts):
            subs.append((len(loads), n == 0, piece))
        loads.append((src, k_tiles, width))
        span[name] = (span.get(name, (len(subs) - len(cuts), 0))[0], len(subs))

    ffn_range = {}
    for name, weight, start, width, k in gemm_plan():
        if name != "FFN":
            src = A[weight].rearrange("(k p) n -> p k n", p=P)[:, :, start:start + width]
            if k < KD:
                stream(name, src, k, width, [None])
            elif width == 512:
                for k0 in (0, 4):
                    stream(name, src[:, k0:k0 + 4, :], 4, width, [("k", 0, 2), ("k", 2, 2)])
            else:
                n = KD if KD * width <= SUB else KD // 2
                stream(name, src, KD, width, [("k", k0, n) for k0 in range(0, KD, n)])
            continue
        ffn_range[weight] = [len(subs), 0]
        down = A[f"{weight}_down"].rearrange("(k p) n -> p k n", p=P)
        for u in range(FFN_UNITS + 1):
            if u < FFN_UNITS:
                for kind in ("gate", "up"):
                    src = A[f"{weight}_{kind}"].rearrange("(k p) n -> p k n", p=P)
                    stream(f"{weight}_{kind}{u}", src[:, :, u * FF_UNIT:(u + 1) * FF_UNIT], KD, FF_UNIT,
                           [("n", j * P, P) for j in range(2)])
            if u >= 1:
                stream(f"{weight}_down{u - 1}", down[:, 2 * (u - 1):2 * u, :], 2, D, [("k", 0, 1), ("k", 1, 1)])
        ffn_range[weight][1] = len(subs)
    slot_of = [i % DENSE_SLOTS for i in range(len(loads))]
    landed = [16 * (i // DENSE_SLOTS + 1) for i in range(len(loads))]
    FIRST_SUBS = span["lr"][1]
    hi_count, lo_count, made = [], [], {"w_hi_ready": 0, "w_lo_by_vector": 0, "w_lo_by_gpsimd": 0}
    for j, (_, _, piece) in enumerate(subs):
        by_vector = j < FIRST_SUBS or any(lo + BUFFERS <= j < hi for lo, hi in ffn_range.values())
        maker = "w_lo_by_vector" if by_vector else "w_lo_by_gpsimd"
        if piece is not None:
            made["w_hi_ready"] += 1
            made[maker] += 1
        hi_count.append(made["w_hi_ready"])
        lo_count.append((maker, made[maker]))
    USED0, HI0, LO0 = len(subs), made["w_hi_ready"], made["w_lo_by_vector"]
    load_freed = {}
    for j, (i, _, piece) in enumerate(subs):
        load_freed[i] = lo_count[j] if piece is not None else ("w_used", j + 1)

    with ExitStack() as ctx:
        sems = {}

        def sem(name):
            if name not in sems:
                sems[name] = ctx.enter_context(nc.semaphore(name))
            return sems[name]

        def sb(name, words, dtype=F32):
            return ctx.enter_context(nc.sbuf_tensor(name, [P, words], dtype))

        arena = sb("arena", DENSE_SLOTS * SLOT + SCRATCH + WORK)
        x_sb = sb("x_sb", T * D)
        h_sb = sb("h_sb", T * D)
        left_hi_sb, left_lo_sb = (sb(f"left_{n}_sb", KD * TOKENS, F32R) for n in ("hi", "lo"))
        w_hi_sb, w_lo_sb = (sb(f"w_{n}_sb", BUFFERS * SUB, F32R) for n in ("hi", "lo"))
        router_hi_sb, router_lo_sb = (sb(f"router_{n}_sb", KD * EXPERTS, F32R) for n in ("hi", "lo"))
        hid_hi_sb, hid_lo_sb = (sb(f"hid_{n}_sb", 2 * 512, F32R) for n in ("hi", "lo"))
        const_sb = sb("const_sb", CONST_WORDS)
        level_masks = ctx.enter_context(nc.sbuf_tensor("level_masks", [P, (len(LEVELS) + 1) * P], I32))
        small = sb("small_sb", 304)
        more = sb("more_sb", 256 + 256)
        bank = [ctx.enter_context(nc.psum_tensor(f"bank{i}", [P, 512], F32)) for i in range(8)]
        gemm_bank, pair_bank = bank[0:4], bank[4:8]

        def work(at, words):
            assert at + words <= WORK
            at += DENSE_SLOTS * SLOT + SCRATCH
            return arena[:, at:at + words]

        def scratch(at, words):
            assert at + words <= SCRATCH
            return arena[:, DENSE_SLOTS * SLOT + at:DENSE_SLOTS * SLOT + at + words]

        def slot(i, k, n):
            return arena[:, i * SLOT:i * SLOT + k * n].rearrange("p (k n) -> p k n", k=k)

        def piece_of(view, piece):
            axis, start, size = piece
            return view[:, start:start + size, :] if axis == "k" else view[:, :, start:start + size]

        def sum_bank(tag, half, t):
            return pair_bank[(pair_at[f"hT_l{('f1', 'f2').index(tag)}"] + 2 * half + t) % 4]

        def raw(j):
            i, _, piece = subs[j]
            return piece_of(slot(slot_of[i], *loads[i][1:]), piece)

        def buffer(store, j, k, n):
            at = (j % BUFFERS) * SUB
            return store[:, at:at + k * n].rearrange("p (k n) -> p k n", k=k)

        small_used = [0]

        def tiny(words):
            at = small_used[0]
            small_used[0] += words
            assert small_used[0] <= 304
            return small[:, at:at + words]

        def const(name, *shape):
            at, w = CONST_AT[name]
            return const_sb[:, at:at + w]

        def tiles(ap, t=T):
            return ap.rearrange("p (t n) -> p t n", t=t)

        def over(ap, position, size):
            ap = ap.unsqueeze(position)
            shape = list(ap.shape)
            shape[position] = size
            return ap.to_broadcast(shape)

        le, ge, gt, lt, ident, ones = (const(c) for c in ("le", "ge", "gt", "lt", "ident", "ones"))
        window, causal = tiles(const("window")), tiles(const("causal"))
        swa_cos, swa_sin = tiles(const("swa_cos")), tiles(const("swa_sin"))
        lb_at = CONST_AT["window"][0]
        log_lb, log_rest = const_sb[:, lb_at:lb_at + 512], const_sb[:, lb_at + 512:lb_at + 1024]
        iota, inv_freq = const("iota"), const("inv_freq")
        x, h = tiles(x_sb[:, :]), tiles(h_sb[:, :])
        left_hi, left_lo = tiles(left_hi_sb[:, :], KD), tiles(left_lo_sb[:, :], KD)

        norms = ("f0", "f1", "l0", "g0", "l1", "g1")
        gain_T = {n: tiny(KD) for n in norms}
        c_gain = [tiny(5) for _ in range(2)]
        ss, ms, root, rinv, rinv_q = tiny(2 * T), tiny(T), tiny(T), tiny(T), tiny(T)
        head_ms, head_rinv = tiny(20), tiny(20)
        row_max, sink_exp, row_sum, row_rec = tiny(16), tiny(16), tiny(16), tiny(16)
        sinks = tiny(SWA_HEADS)
        position = tiny(T).bitcast(I32)
        pos_f = tiny(T)
        router_w = tiles(tiny(KD * EXPERTS), KD)
        hg_gain = [more[:, 128 * i:128 * i + 128] for i in range(2)]
        rope_cos, rope_sin = tiles(more[:, 256:384]), tiles(more[:, 384:512])

        g_q, g_k, g_v = tiles(work(0, 1024)), tiles(work(1024, 1024)), tiles(work(2048, 2048))
        g_lg = work(4096, 2048).rearrange("p (a t n) -> p a t n", a=2, t=T)
        g_qT, g_kT = work(6144, 1024), work(7168, 1024)
        g_kt = tiles(work(8192, 1024))
        g_lrT = tiles(work(9216, 512)[0:GLA_RANK, :])
        g_lr = tiles(work(9728, 64))
        g_sr = h
        g_dec = [scratch(2048 * a, 1024) for a in range(2)]
        g_inv = [scratch(2048 * a + 1024, 1024) for a in range(2)]
        g_up = tiles(scratch(4096, 1024)[0:GLA_RANK, :])
        g_bias = tiles(scratch(6144, 1024)[0:1, :])
        g_sc = scratch(4096, 2048).rearrange("p (a t h c) -> p a t h c", a=2, t=T, h=GLA_HEADS)
        g_st = scratch(6144, 2048).rearrange("p (a h e) -> p a h e", a=2, h=GLA_HEADS)
        g_o = work(4096, 2048)
        g_tmp = scratch(0, 2048)
        g_gain = work(13184, 256)
        s_qk = work(9856, 2560).rearrange("p (t h d) -> p t h d", t=T, h=10)
        s_qk_flat = tiles(work(9856, 2560))
        s_v = tiles(work(12416, 512))
        s_gain = tiles(work(12928, 256))
        s_cos, s_sin = (work(at, 512).rearrange("p (n t d) -> p n t d", n=2, t=T) for at in (9216, 13440))
        s_a = scratch(0, 2560).rearrange("p (t h d) -> p t h d", t=T, h=10)
        s_b = scratch(2560, 2560).rearrange("p (t h d) -> p t h d", t=T, h=10)
        s_qkT = tiles(work(6144, 2560), 10)
        s_sc = scratch(4096, 4096).rearrange("p (t h k) -> p t h k", t=T, h=SWA_HEADS)
        s_pT = scratch(0, 4096).rearrange("p (t h b q) -> p t h b q", t=T, h=SWA_HEADS, b=2)
        s_o = tiles(work(4096, 2048))
        gate_a, gate_b = tiles(work(0, 2048)), tiles(work(2048, 2048))
        y_gla, y_swa = tiles(work(9856, 2048)), tiles(work(4096, 2048))
        f_silu = [work(512 * i, 512) for i in range(2)]
        f_hid, f_up = work(1024, 512), work(3072, 512)
        f_gate = [work(2048 + 512 * i, 512) for i in range(2)]
        f_diag, f_row = tiles(work(3584, TOKENS)), work(1536, TOKENS)
        hid_hi, hid_lo = ([a[:, 512 * i:512 * i + 512] for i in range(2)] for a in (hid_hi_sb, hid_lo_sb))
        n_z, n_q, n_v, n_g, n_lf, n_k = (tiles(work(1024 * i, 1024)) for i in range(6))
        n_qT, n_kT, n_bT, n_at = (work(6144 + 1024 * i, 1024) for i in range(4))
        n_kt, n_st = work(10240, 512), work(10752, 512)
        n_c = tiles(work(11264, 1408))
        n_cT = tiles(work(12672, 1280), 5)
        n_tmp = [scratch(1024 * i, 1024) for i in range(4)]
        n_E, n_X = n_tmp[0:2], n_tmp[2:4]
        soft, diff = n_tmp[3][:, 0:512], n_tmp[3][:, 512:1024]
        n_qd = scratch(4096, 512)
        n_qm, n_kvm = tiles(scratch(4608, 1536)), tiles(scratch(6144, 2048))
        n_mqT, n_mkT = tiles(work(4096, 1024), 4), tiles(work(5120, 1024), 4)
        n_pqT = tiles(work(0, 1024)[0:ROPE, :], 4)
        n_pkT = work(1024, 256)[0:ROPE, :]
        n_sc = h_sb[:, :].rearrange("p (t h k) -> p t h k", t=T, h=MLA_HEADS)
        n_pT = scratch(2048, 2048).rearrange("p (t h b q) -> p t h b q", t=T, h=MLA_HEADS, b=2)
        mix, n_o = h, tiles(n_bT)
        n_c_junk = scratch(4096 + 512, 1024)
        e_logit, e_top, e_prob, e_mask, e_pos, e_oh0, e_oh1, e_idf = (tiles(work(16 * i, 16)) for i in range(8))
        e_idx = tiles(work(128, 16)).bitcast(U32)
        e_d, e_g0, e_g1, e_cnt, e_cntx = work(144, 2), work(146, 2), work(148, 2), work(150, 1), work(151, 2)
        e_rounds = work(153, 1).bitcast(I32)
        e_logitT = work(6144, TOKENS)[0:EXPERTS, :]
        e_P, e_G = tiles(work(256, T * CAP)), tiles(work(512, T * CAP))
        e_GT = work(768, 256)[0:CAP, :]
        e_hi, e_lo = left_hi[:, :, 0:CAP], left_lo[:, :, 0:CAP]
        e_silu, e_hid = ([work(1024 * n + 512 * i, 512)[0:CAP, :] for i in range(2)] for n in (1, 2))
        e_y = work(3072, 1024)[0:CAP, :]
        fin_gain, e_gain = work(4096, 1024), work(7168, 1024)

        block = ctx.enter_context(nc.Block())
        dma = ctx.enter_context(nc.allow_non_contiguous_dma("vectors laid over partitions, small"))

        expert_parts = [("gate", 0), ("up", 0)]
        for s in range(1, MOE_STEPS):
            expert_parts += [("gate", s), ("up", s), ("down", s - 1)]
        expert_parts.append(("down", MOE_STEPS - 1))
        part_end = {part: 4 * n + 4 for n, part in enumerate(expert_parts)}

        def expert_source(i, e):
            (kind, s), second = expert_parts[i // 2], i % 2
            if kind == "down":
                at = s * FF_STEP + second * 2 * P
                return A["moe_w_down"][e, at:at + 2 * P, :].rearrange("(k p) n -> p k n", p=P)
            w = A[f"moe_w_{kind}"][e].rearrange("(k p) n -> p k n", p=P)
            return w[:, 4 * second:4 * second + 4, s * FF_STEP:(s + 1) * FF_STEP]

        def expert_shape(i):
            return (2, D) if expert_parts[i // 2][0] == "down" else (4, FF_STEP)

        def expert_piece(j):
            i = j // 2
            k, n = expert_shape(i)
            half = k // 2
            return slot(i % SLOTS, k, n)[:, (j % 2) * half:(j % 2 + 1) * half, :]

        def expert_buffer(store, j):
            k, n = expert_shape((j % MOE_SUBS) // 2)
            return buffer(store, USED0 + j, k // 2, n)

        @block.sync
        def _(sp):
            for half in range(2):
                cols = slice(half * 512, (half + 1) * 512)
                sp.dma_start(x[:, :, cols], A["x"].rearrange("a (t p) d -> p (a t) d", p=P)[:, :, cols]) \
                    .then_inc(sem(f"x_landed{half}"), 16)
            for i, (src, k, width) in enumerate(loads):
                if i >= DENSE_SLOTS:
                    sp.wait_ge(sem(load_freed[i - DENSE_SLOTS][0]), load_freed[i - DENSE_SLOTS][1])
                sp.dma_start(slot(slot_of[i], k, width), src).then_inc(sem(f"landed{slot_of[i]}"), 16)

            def load(e, i):
                sp.dma_start(slot(i % SLOTS, *expert_shape(i)), expert_source(i, e)) \
                    .then_inc(sem(f"expert_landed{i % SLOTS}"), 16)

            def freed(it, i):
                sp.wait_ge(sem("w_lo_by_vector"), it * MOE_SUBS + (LO0 + 2 * i + 2))

            def own(it, e):
                freed(it, 1)
                load(e, SLOTS)
                load(e, SLOTS + 1)
                for i in range(SLOTS + 2, MOE_LOADS):
                    freed(it, i - SLOTS)
                    load(e, i)

            def one_round(first):
                with sp.Fori(0, EXPERTS - 1) as e:
                    it = first + e
                    own(it, e)
                    for i in range(SLOTS):
                        freed(it, i + MOE_LOADS - SLOTS)
                        load(e + 1, i)
                own(first + EXPERTS - 1, EXPERTS - 1)

            for i in range(SLOTS):
                if i < DENSE_SLOTS:
                    last = max(n for n in range(len(loads)) if slot_of[n] == i)
                    sp.wait_ge(sem(load_freed[last][0]), load_freed[last][1])
                else:
                    sp.wait_ge(sem("pair_read"), pair_end["mixT_1"])
                load(0, i)
            one_round(0)
            sp.wait_ge(sem("rounds_known"), 1)
            rounds = sp.value_load(e_rounds[0:1, 0:1], min_val=1, max_val=MAX_ROUNDS)
            with sp.If(rounds > 1):
                with sp.Fori(1, rounds) as r:
                    for i in range(SLOTS):
                        freed(r * EXPERTS - 1, i + MOE_LOADS - SLOTS)
                        load(0, i)
                    one_round(r * EXPERTS)
            for t in range(T):
                sp.wait_ge(sem("result"), t + 1)
                sp.dma_start(out.rearrange("a (t p) d -> p (a t) d", p=P)[:, t, :], x[:, t, :]) \
                    .then_inc(sem("stored"), 16)
            sp.wait_ge(sem("stored"), 16 * T)

        @block.gpsimd
        def _(pool):
            def column(dst, vec):
                pool.dma_start(dst, vec.rearrange("(k p) -> p k", p=P)).then_inc(sem("small_landed"), 16)

            def rows(dst, src, name="small_landed"):
                pool.dma_start(dst, src).then_inc(sem(name), 16)

            rows(level_masks[:, :], A["level_masks"])
            for a, d in enumerate(("fwd", "bwd")):
                rows(g_up[:, a, :], A[f"gla_gate_up_{d}"][0])
                rows(g_bias[:, a, :], A[f"gla_gate_bias_{d}"][0:1, :])
            rows(g_gain, A["gla_out_norm_g"].to_broadcast([P, GLA_DV]))
            rows(s_gain[:, 0, :], A["swa_q_norm_g"].to_broadcast([P, HD]))
            rows(s_gain[:, 1, :], A["swa_k_norm_g"].to_broadcast([P, HD]))
            rows(sinks, A["swa_sinks"].to_broadcast([P, SWA_HEADS]))
            column(gain_T["f1"], A["norm_ffn_g"][0])
            for l in range(2):
                column(gain_T[f"l{l}"], A["mix_norm_2"][l])
                column(gain_T[f"g{l}"], A["ffn_norm_2"][l])
                column(c_gain[l][:, 0:3], A["q_a_norm_2"][l])
                column(c_gain[l][:, 3:5], A["kv_a_norm_2"][l])
                rows(hg_gain[l], A["hg_out_norm_2"][l:l + 1, :].to_broadcast([P, P]))
            rows(position, A["positions_2"].rearrange("a (t p) -> p (a t)", p=P))
            rows(router_w, A["moe_router_2"][0].rearrange("(k p) e -> p k e", p=P))
            rows(const_sb[:, P:], A["const_table"][:, P:])
            for j, (_, _, piece) in enumerate(subs):
                if piece is not None and lo_count[j][0] == "w_lo_by_gpsimd":
                    w = raw(j)
                    k, n = w.shape[1:]
                    pool.wait_ge(sem("w_hi_ready"), hi_count[j])
                    pool.tensor_tensor(buffer(w_lo_sb, j, k, n), w, buffer(w_hi_sb, j, k, n).bitcast(F32),
                                       ALU.subtract).then_inc(sem("w_lo_by_gpsimd"), 1)

            pool.wait_ge(sem("expert_gain_landed"), 16)
            for t in range(T):
                pool.wait_ge(sem("e_scaled"), t + 1)
                pool.tensor_tensor(h[:, t, :], h[:, t, :], e_gain, ALU.mult).then_inc(sem("e_tokens_ready"), 1)

        FIRST_LANDED = 32
        SMALL_LANDED = 16 * (1 + 1 + 4 + 1 + 2 + 1 + 1 + 10 + 2)

        @block.tensor
        def _(pe):
            def three_passes(out, still, moving, start, stop):
                pe.matmul(out, still[0], moving[0], start=start, stop=False)
                pe.matmul(out, still[0], moving[1], start=False, stop=False)
                return pe.matmul(out, still[1], moving[0], start=False, stop=stop)

            def gemm(name, left=None, between={}):
                first, end = span[name]
                k = 0
                for j in range(first, end):
                    size, width = raw(j).shape[1:]
                    pe.wait_ge(sem(lo_count[j][0]), lo_count[j][1])
                    if left is not None:
                        pe.wait_ge(sem("pair_read"), pair_at[left] + (k + size) // 2)
                    w = [buffer(a, j, size, width) for a in (w_hi_sb, w_lo_sb)]
                    for t in range(T):
                        job = gemm_at[name] + t
                        if j == first and job >= 4:
                            pe.wait_ge(sem("gemm_read"), job - 3)
                        for i in range(size):
                            still = [a[:, k + i, t * P:(t + 1) * P] for a in (left_hi, left_lo)]
                            mm = three_passes(gemm_bank[job % 4][:, 0:width], still, [a[:, i, :] for a in w],
                                              k + i == 0, k + i == KD - 1)
                    mm.then_inc(sem("w_used"), 1)
                    k += size
                    if j - first in between:
                        between[j - first]()

            def whole_gemm(name, left):
                i = subs[span[name][0]][0]
                _, k_tiles, width = loads[i]
                w = slot(slot_of[i], k_tiles, width)
                pe.wait_ge(sem(f"landed{slot_of[i]}"), landed[i])
                for t in range(T):
                    job = gemm_at[name] + t
                    pe.wait_ge(sem("gemm_read"), job - 3)
                    for k in range(k_tiles):
                        mm = pe.matmul(gemm_bank[job % 4][:, 0:width], left(k, t), w[:, k, :],
                                       start=(k == 0), stop=(k == k_tiles - 1))
                mm.then_inc(sem("w_used"), 1)

            def pair(name, i):
                j = pair_at[name] + i
                if j >= 4:
                    pe.wait_ge(sem("pair_read"), j - 3)
                return pair_bank[j % 4]

            def transpose_all(name, source, k_tiles, first=0, ready={}, banks=None):
                for i in banks or range(-(-k_tiles // 2)):
                    if i in ready:
                        pe.wait_ge(sem(ready[i][0]), ready[i][1])
                    b = pair(name, first + i)
                    for k in range(2 * i, min(2 * i + 2, k_tiles)):
                        for t in range(T):
                            at = (k % 2) * TOKENS + t * P
                            tr = pe.transpose(b[:, at:at + P], source(k, t), ident)
                    tr.then_inc(sem("pair_full"), 1)

            def natural(a):
                return lambda k, t: a[:, t, k * P:(k + 1) * P]

            def transpose_heads(name, a):
                for t in range(T):
                    b = pair(name, t)
                    for i in range(4):
                        tr = pe.transpose(b[:, i * P:(i + 1) * P], a[:, t, i * P:(i + 1) * P], ident)
                    tr.then_inc(sem("pair_full"), 1)

            def plain(tag, ready):
                transpose_all(f"hT_{tag}", natural(x), KD, ready={0: ready[0], 2: ready[1]})

            pe.wait_ge(sem("first_landed"), FIRST_LANDED)
            plain("f0", (("x_landed0", 16), ("x_landed1", 16)))
            gemm("gk", "hT_f0")
            gemm("gq")
            gemm("lr")
            pe.wait_ge(sem("gemm_read"), gemm_at["lr"] + T)
            b = pair("lrT", 0)
            for a in range(2):
                for t in range(T):
                    at = a * TOKENS + t * P
                    tr = pe.transpose(b[0:GLA_RANK, at:at + P], g_lr[:, t, a * GLA_RANK:(a + 1) * GLA_RANK], ident)
            tr.then_inc(sem("pair_full"), 1)
            gemm("gv0")
            pe.wait_ge(sem("small_landed"), SMALL_LANDED)
            pe.wait_ge(sem("pair_read"), pair_end["lrT"])
            for a in range(2):
                for t in range(T):
                    b = pair("z", 2 * a + t)
                    pe.matmul(b[:, :], g_lrT[:, a, t * P:(t + 1) * P], g_up[:, a, :], start=True, stop=False)
                    pe.matmul(b[:, :], ones[0:1, :], g_bias[:, a, :], start=False, stop=True) \
                        .then_inc(sem("pair_full"), 1)
            transpose_heads("gqT", g_q)
            transpose_heads("gkT", g_k)
            gemm("gv1")
            pe.wait_ge(sem("g_lg_ready"), 2)
            for a in range(2):
                for t in range(T):
                    b = pair("gb", 2 * a + t)
                    for i in range(GLA_HEADS):
                        mm = pe.matmul(b[:, i * P:(i + 1) * P], g_lg[:, a, t, i * P:(i + 1) * P], (le, ge)[a],
                                       start=True, stop=True)
                    mm.then_inc(sem("pair_full"), 1)
            for a in range(2):
                pe.matmul(pair("tail", a)[:, :], (gt, lt)[a], g_lg[:, a, a, :], start=True, stop=True) \
                    .then_inc(sem("pair_full"), 1)
            gemm("gr0")
            gemm("gr1")
            for a in range(2):
                pe.wait_ge(sem("g_dec_ready"), a + 1)
                pe.wait_ge(sem("g_inv_ready"), a + 1)
                for t in range(T):
                    b = pair("gsc", 2 * a + t)
                    for i in range(GLA_HEADS):
                        at = (t * GLA_HEADS + i) * P
                        mm = pe.matmul(b[:, i * P:(i + 1) * P], g_inv[a][:, at:at + P], g_dec[a][:, at:at + P],
                                       start=True, stop=True)
                    mm.then_inc(sem("pair_full"), 1)
            pe.wait_ge(sem("g_kt_ready"), 2)
            for a in range(2):
                for half in range(2):
                    b = pair("gst", 2 * a + half)
                    for i in range(2):
                        head = 2 * half + i
                        mm = pe.matmul(b[:, i * GLA_DV:(i + 1) * GLA_DV], g_kt[:, a, head * P:(head + 1) * P],
                                       g_v[:, a, head * GLA_DV:(head + 1) * GLA_DV], start=True, stop=True)
                    mm.then_inc(sem("pair_full"), 1)
            gemm("sq0")
            gemm("sq1")
            pe.wait_ge(sem("pair_read"), pair_end["gst"])
            for t in range(T):
                for half in range(2):
                    b = pair("go", 2 * t + half)
                    for i in range(2):
                        head = 2 * half + i
                        values = g_v[:, t, head * GLA_DV:(head + 1) * GLA_DV]
                        o = b[:, i * GLA_DV:(i + 1) * GLA_DV]
                        a = 1 - t
                        at = (t * GLA_HEADS + head) * P
                        pe.matmul(o, g_sc[:, 0, t, head, :], values, start=True, stop=False)
                        pe.matmul(o, g_sc[:, 1, t, head, :], values, start=False, stop=False)
                        mm = pe.matmul(o, g_dec[a][:, at:at + P], g_st[:, a, head, :], start=False, stop=True)
                    mm.then_inc(sem("pair_full"), 1)
            gemm("skv")
            gemm("ga0")
            gemm("ga1")
            gemm("gb0")

            def turn_s():
                pe.wait_ge(sem("s_rot"), T)
                transpose_all("sT", lambda k, t: s_a[:, t, k, :], 10)

            gemm("gb1", between={1: turn_s})
            pe.wait_ge(sem("pair_read"), pair_end["sT"])
            for t in range(T):
                for i in range(SWA_HEADS // 2):
                    b = pair("ssc", 4 * t + i)
                    for j in range(2):
                        head = 2 * i + j
                        kv = SWA_HEADS + head // (SWA_HEADS // SWA_KV)
                        mm = pe.matmul(b[:, j * TOKENS:(j + 1) * TOKENS], s_qkT[:, head, t * P:(t + 1) * P],
                                       s_qkT[:, kv, :], start=True, stop=True)
                    mm.then_inc(sem("pair_full"), 1)
            pe.wait_ge(sem("g_out"), 1)
            transpose_all("goT", natural(tiles(g_o)), KD)
            gemm("og0", "goT")
            gemm("og1")

            def attend(names, scores, weightsT, values, heads):
                for t in range(T):
                    for i in range(heads // 2):
                        pe.wait_ge(sem(names[2]), t * heads + 2 * i + 2)
                        b = pair(names[0], t * heads // 2 + i)
                        for j in range(2):
                            for kt in range(2):
                                at = (2 * j + kt) * P
                                tr = pe.transpose(b[:, at:at + P], scores[:, t, 2 * i + j, kt * P:(kt + 1) * P], ident)
                        tr.then_inc(sem("pair_full"), 1)
                pe.wait_ge(sem("pair_read"), pair_end[names[0]])
                for t in range(T):
                    for i in range(heads // 4):
                        b = pair(names[1], t * heads // 4 + i)
                        for j in range(4):
                            for kt in range(2):
                                mm = pe.matmul(b[:, j * P:(j + 1) * P], weightsT[:, t, 4 * i + j, kt, :],
                                               values(kt, 4 * i + j), start=(kt == 0), stop=(kt == 1))
                        mm.then_inc(sem("pair_full"), 1)

            attend(("sP", "so", "s_exp"), s_sc, s_pT,
                   lambda kt, head: s_v[:, kt, (head // 4) * HD:(head // 4 + 1) * HD], SWA_HEADS)
            pe.wait_ge(sem("pair_read"), pair_end["so"])
            transpose_all("soT", natural(s_o), KD)
            gemm("os0", "soT")
            gemm("os1")

            def turn_merged(banks):
                transpose_all("mT", natural(y_gla), KD, ready={0: ("merged", 1), 2: ("merged", 2)}, banks=banks)

            turn_merged(range(0, 2))
            gemm("wo0", "mT", between={1: lambda: turn_merged(range(2, 4))})
            gemm("wo1")

            def ffn(tag, norm):
                def down(u, last):
                    pe.wait_ge(sem(f"{tag}_hid"), u + 1)
                    hid = [tiles(a[u % 2]) for a in (hid_hi, hid_lo)]
                    first = span[f"{tag}_down{u}"][0]
                    for i in range(2):
                        pe.wait_ge(sem(lo_count[first + i][0]), lo_count[first + i][1])
                        w = [buffer(a, first + i, 1, D) for a in (w_hi_sb, w_lo_sb)]
                        for half in range(2):
                            for t in range(T):
                                mm = three_passes(sum_bank(tag, half, t)[:, :],
                                                  [a[:, i, t * P:(t + 1) * P] for a in hid],
                                                  [a[:, 0, half * 512:(half + 1) * 512] for a in w],
                                                  u == 0 and i == 0, last and i == 1)
                            if last and i == 1 and half == 0:
                                mm.then_inc(sem("half_done"), 1)
                        mm.then_inc(sem("w_used"), 1)

                for u in range(FFN_UNITS):
                    for kind in range(2):
                        if u >= 2:
                            pe.wait_ge(sem(f"{tag}_hid"), u - 1)
                        b = gemm_bank[2 * (u % 2) + kind]
                        first = span[f"{tag}_{('gate', 'up')[kind]}{u}"][0]
                        for i in range(2):
                            pe.wait_ge(sem(lo_count[first + i][0]), lo_count[first + i][1])
                            w = [buffer(a, first + i, KD, P) for a in (w_hi_sb, w_lo_sb)]
                            for k in range(KD):
                                if u + kind + i == 0 and k % 2 == 0:
                                    pe.wait_ge(sem("pair_read"), pair_at[f"hT_{norm}"] + k // 2 + 1)
                                mm = three_passes(b[:, i * TOKENS:(i + 1) * TOKENS], [a[:, k, :] for a in w],
                                                  (left_hi[:, k, :], left_lo[:, k, :]), k == 0, k == KD - 1)
                            mm.then_inc(sem("w_used"), 1)
                    if u == 0:
                        pe.wait_ge(sem("diagonals"), T * (norm == "g0") + T)
                        b = pair(f"row_{norm}", 0)
                        for t in range(T):
                            mm = pe.matmul(b[:, t * P:(t + 1) * P], ones, f_diag[:, t, :], start=True, stop=True)
                        mm.then_inc(sem("pair_full"), 1)
                    if u == 1:
                        pe.wait_ge(sem("pair_read"), pair_end[f"row_{norm}"])
                    if u >= 1:
                        down(u - 1, False)
                down(FFN_UNITS - 1, True)

            plain("f1", (("x_mixed_f", 2), ("x_mixed_f", 4)))
            pe.wait_ge(sem("gemm_read"), gemm_at["wo1"] + T)
            ffn("f1", "f1")

            for l in range(2):
                if l == 1:
                    pe.wait_ge(sem("f2_hid"), FFN_UNITS)
                plain(f"l{l}", ((f"x_ffn_{l}", 2), (f"x_ffn_{l}", 4)))
                gemm(f"hf_{l}", f"hT_l{l}")
                gemm(f"hq_{l}")
                gemm(f"hg_{l}")
                def turn_hgrn():
                    pe.wait_ge(sem("n_k_ready"), l + 1)
                    transpose_heads(f"hkT_{l}", n_k)
                    pe.wait_ge(sem(f"n_lf_ready_{l}"), 1)
                    for t in range(T):
                        b = pair(f"hb_{l}", t)
                        for i in range(HG_HEADS):
                            mm = pe.matmul(b[:, i * P:(i + 1) * P], n_lf[:, t, i * P:(i + 1) * P], le,
                                           start=True, stop=True)
                        mm.then_inc(sem("pair_full"), 1)
                    pe.matmul(pair(f"ht_{l}", 0)[:, :], gt, n_lf[:, 0, :], start=True, stop=True) \
                        .then_inc(sem("pair_full"), 1)
                    pe.wait_ge(sem("gemm_read"), gemm_at[f"hq_{l}"] + T)
                    transpose_heads(f"hqT_{l}", n_q)

                def level(n):
                    if n:
                        pe.wait_ge(sem(f"level_ready_{l}"), 2 * n)
                    else:
                        pe.wait_ge(sem("pair_read"), pair_end[f"hqT_{l}"])
                    for t in range(T):
                        b = pair(f"hlev{n}_{l}", t)
                        for i in range(HG_HEADS):
                            at = (t * HG_HEADS + i) * P
                            key, query = (n_X[n % 2], n_X[n % 2]) if n else (n_kT, n_qT)
                            mm = pe.matmul(b[:, i * P:(i + 1) * P], key[:, at:at + P], query[:, at:at + P],
                                           start=True, stop=True)
                        mm.then_inc(sem("pair_full"), 1)

                def turn_c():
                    pe.wait_ge(sem(f"c_normed_{l}"), T * 2)
                    transpose_all(f"cT_{l}", natural(n_c), 5)

                if l == 0:
                    turn_hgrn()
                    gemm("c0_0", between={1: lambda: level(0)})
                else:
                    gemm("c0_1", between={1: turn_hgrn, 3: lambda: level(0)})
                gemm(f"c1_{l}", between={1: lambda: level(1)})
                gemm(f"hi_{l}", between={0: lambda: level(2), 2: turn_c})
                pe.wait_ge(sem("pair_read"), pair_end[f"cT_{l}"])
                for i in range(2):
                    whole_gemm(f"qb{i}_{l}", lambda k, t: n_cT[:, k, t * P:(t + 1) * P])
                    if i == 0:
                        level(3)
                for i in range(2):
                    whole_gemm(f"kvb{i}_{l}", lambda k, t: n_cT[:, 3 + k, t * P:(t + 1) * P])
                    if i == 0:
                        level(4)
                pe.wait_ge(sem("n_kt_ready"), l + 1)
                b = pair(f"hst_{l}", 0)
                for i in range(HG_HEADS):
                    mm = pe.matmul(b[:, i * P:(i + 1) * P], n_kt[:, i * P:(i + 1) * P], n_v[:, 0, i * P:(i + 1) * P],
                                   start=True, stop=True)
                mm.then_inc(sem("pair_full"), 1)
                pe.wait_ge(sem(f"m_rot_{l}"), 2 * T)
                transpose_all(f"mqT_{l}", lambda k, t: n_qm[:, t, k * 192:k * 192 + NOPE], MLA_HEADS)
                pe.wait_ge(sem("gemm_read"), gemm_at[f"kvb1_{l}"] + T)
                transpose_all(f"mkT_{l}", lambda k, t: n_kvm[:, t, k * 256:k * 256 + NOPE], MLA_HEADS)
                for i in range(3):
                    b = pair(f"mpT_{l}", i)
                    for k in range(2 * i, min(2 * i + 2, MLA_HEADS + 1)):
                        for t in range(T):
                            src = n_qm[:, t, k * 192 + NOPE:(k + 1) * 192] if k < MLA_HEADS \
                                else n_c[:, t, Q_RANK + KV_RANK:Q_RANK + KV_RANK + ROPE]
                            at = (k % 2) * TOKENS + t * P
                            tr = pe.transpose(b[0:ROPE, at:at + P], src, ident)
                    tr.then_inc(sem("pair_full"), 1)
                level(5)
                level(6)
                pe.wait_ge(sem("pair_read"), pair_end[f"mpT_{l}"])
                for t in range(T):
                    if t == 1:
                        level(7)
                    for i in range(MLA_HEADS // 2):
                        b = pair(f"msc{t}_{l}", i)
                        for j in range(2):
                            head = 2 * i + j
                            o = b[:, j * TOKENS:(j + 1) * TOKENS]
                            pe.matmul(o, n_mqT[:, head, t * P:(t + 1) * P], n_mkT[:, head, :], start=True, stop=False)
                            mm = pe.matmul(o, n_pqT[:, head, t * P:(t + 1) * P], n_pkT, start=False, stop=True)
                        mm.then_inc(sem("pair_full"), 1)
                pe.wait_ge(sem("pair_read"), pair_end[f"hlev7_{l}"])
                pe.wait_ge(sem("n_qd_ready"), l + 1)
                for t in range(T):
                    b = pair(f"ho_{l}", t)
                    for i in range(HG_HEADS):
                        at = (t * HG_HEADS + i) * P
                        mm = pe.matmul(b[:, i * P:(i + 1) * P], n_at[:, at:at + P], n_v[:, t, i * P:(i + 1) * P],
                                       start=True, stop=(t == 0))
                        if t == 1:
                            mm = pe.matmul(b[:, i * P:(i + 1) * P], n_qd[:, i * P:(i + 1) * P],
                                           n_st[:, i * P:(i + 1) * P], start=False, stop=True)
                    mm.then_inc(sem("pair_full"), 1)
                attend((f"mP_{l}", f"mo_{l}", f"m_exp_{l}"), n_sc, n_pT,
                       lambda kt, head: n_kvm[:, kt, head * 256 + NOPE:(head + 1) * 256], MLA_HEADS)
                pe.wait_ge(sem("pair_read"), pair_end[f"mo_{l}"])

                def turn_mix(banks):
                    transpose_all(f"mixT_{l}", lambda k, t: (mix, n_o)[k // 4][:, t, (k % 4) * P:(k % 4 + 1) * P], KD,
                                  ready={2: (f"hg_mixed_{l}", T)}, banks=banks)

                turn_mix(range(0, 2))
                gemm(f"wo0_{l}", f"mixT_{l}", between={1: lambda: turn_mix(range(2, 4))})
                gemm(f"wo1_{l}")
                if l == 0:
                    plain("g0", (("x_mixed_0", 2), ("x_mixed_0", 4)))
                    pe.wait_ge(sem("gemm_read"), gemm_at["wo1_0"] + T)
                else:
                    plain("g1", (("x_mixed_1", 2), ("x_mixed_1", 4)))
                if l == 0:
                    ffn("f2", "g0")

            b = pair("routerT", 0)
            for k in range(KD):
                if k % 2 == 0:
                    pe.wait_ge(sem("pair_read"), pair_at["hT_g1"] + k // 2 + 1)
                mm = three_passes(b[0:EXPERTS, 0:TOKENS],
                                  [a[:, k * EXPERTS:(k + 1) * EXPERTS] for a in (router_hi_sb, router_lo_sb)],
                                  (left_hi[:, k, :], left_lo[:, k, :]), k == 0, k == KD - 1)
            mm.then_inc(sem("pair_full"), 1)
            pe.wait_ge(sem("pair_read"), pair_end["routerT"])
            b = pair("router", 0)
            for t in range(T):
                tr = pe.transpose(b[:, t * EXPERTS:(t + 1) * EXPERTS], e_logitT[:, t * P:(t + 1) * P],
                                  ident[0:EXPERTS, 0:EXPERTS])
            tr.then_inc(sem("pair_full"), 1)
            pe.wait_ge(sem("e_mask_ready"), 1)
            b = pair("ranks", 0)
            pe.matmul(b[:, 0:8], lt, e_mask[:, 0, :], start=True, stop=True)
            pe.matmul(b[:, 8:16], ones, e_mask[:, 0, :], start=True, stop=False)
            pe.matmul(b[:, 8:16], lt, e_mask[:, 1, :], start=False, stop=True)
            pe.matmul(b[:, 16:24], ones, e_mask[:, 0, :], start=True, stop=False)
            pe.matmul(b[:, 16:24], ones, e_mask[:, 1, :], start=False, stop=True).then_inc(sem("pair_full"), 1)
            pe.wait_ge(sem("pair_read"), pair_end["ranks"])

            y_bank, misc = pair_bank[0:2], pair_bank[2:4]

            def gather(number):
                pe.wait_ge(sem("e_placed"), T * number + T)
                for i in range(2):
                    for k in range(4 * i, 4 * i + 4):
                        for t in range(T):
                            mm = pe.matmul(gemm_bank[2 + i][:, (k % 4) * CAP:(k % 4 + 1) * CAP],
                                           h[:, t, k * P:(k + 1) * P], e_P[:, t, :], start=(t == 0), stop=(t == T - 1))
                    mm.then_inc(sem("e_gathered"), 1)

            def expert(it, more):
                def piece(j):
                    pe.wait_ge(sem("w_lo_by_vector"), it * MOE_SUBS + (LO0 + j + 1))
                    return [expert_buffer(a, j) for a in (w_hi_sb, w_lo_sb)]

                def into_hidden(kind, s):
                    b = gemm_bank[2 * (s % 2) + (kind == "up")]
                    for i in range(4):
                        w = piece(part_end[kind, s] - 4 + i)
                        for k in range(2 * i, 2 * i + 2):
                            mm = three_passes(b[0:CAP, :], (e_hi[:, k, :], e_lo[:, k, :]), [a[:, k % 2, :] for a in w],
                                              k == 0, k == KD - 1)
                        mm.then_inc(sem("w_used"), 1)

                def turn(s):
                    pe.wait_ge(sem("e_hid_ready"), it * MOE_STEPS + s + 1)
                    if s == 0:
                        pe.wait_ge(sem("e_added"), it * 4 + 4)
                    for i in range(4):
                        tr = pe.transpose(misc[s % 2][:, i * CAP:(i + 1) * CAP], e_hid[s % 2][:, i * P:(i + 1) * P],
                                          ident[0:CAP, 0:CAP])
                    tr.then_inc(sem("e_hid_turned"), 1)

                def down(s):
                    pe.wait_ge(sem("e_hid_split"), it * MOE_STEPS + s + 1)
                    hid = [tiles(a[s % 2], 4) for a in (hid_hi, hid_lo)]
                    for i in range(4):
                        w = piece(part_end["down", s] - 4 + i)
                        last = s == MOE_STEPS - 1 and i == 3
                        for half in range(2):
                            mm = three_passes(y_bank[half][0:CAP, :], [a[:, i, :] for a in hid],
                                              [a[:, 0, half * 512:(half + 1) * 512] for a in w],
                                              s == 0 and i == 0, last)
                            if last and half == 0:
                                mm.then_inc(sem("e_y0_done"), 1)
                        mm.then_inc(sem("w_used"), 1)

                pe.wait_ge(sem("e_x_ready"), it * 2 + 2)
                into_hidden("gate", 0)
                into_hidden("up", 0)
                for s in range(MOE_STEPS - 1):
                    into_hidden("gate", s + 1)
                    turn(s)
                    into_hidden("up", s + 1)
                    down(s)
                turn(MOE_STEPS - 1)
                if more:
                    gather(it + 1)
                pe.wait_ge(sem("e_weighted"), it * T + T)
                for t in range(T):
                    tr = pe.transpose(misc[1][0:CAP, t * P:(t + 1) * P], e_G[:, t, :], ident)
                tr.then_inc(sem("e_turned"), 1)
                down(MOE_STEPS - 1)
                pe.wait_ge(sem("e_GT_ready"), it + 1)
                pe.wait_ge(sem("e_y0_ready"), it + 1)
                for t in range(T):
                    for half in range(2):
                        if t == 0 and half == 1:
                            pe.wait_ge(sem("e_y1_ready"), it + 1)
                        pe.matmul((misc, y_bank)[half][t][:, :], e_GT[:, t * P:(t + 1) * P],
                                  e_y[:, half * 512:(half + 1) * 512], start=True, stop=True) \
                            .then_inc(sem("e_scattered"), 1)

            pe.wait_ge(sem("e_tokens_ready"), T)

            def one_round(r):
                gather(r * EXPERTS)
                with pe.Fori(0, EXPERTS - 1) as e:
                    expert(r * EXPERTS + e, True)
                expert(r * EXPERTS + (EXPERTS - 1), False)

            one_round(0)
            pe.wait_ge(sem("rounds_known"), 1)
            rounds = pe.value_load(e_rounds[0:1, 0:1], min_val=1, max_val=MAX_ROUNDS)
            with pe.If(rounds > 1):
                with pe.Fori(1, rounds) as r:
                    one_round(r)

        @block.scalar
        def _(act):
            told = counter()

            def link(instruction):
                instruction.then_inc(sem("scalar_step"), 1)
                act.wait_ge(sem("scalar_step"), told("scalar_step"))

            act.dma_start(ident, A["const_table"][:, 0:P]).then_inc(sem("first_landed"), 16)
            act.dma_start(gain_T["f0"], A["norm_mix_g"][0].rearrange("(k p) -> p k", p=P)) \
                .then_inc(sem("first_landed"), 16)
            act.wait_ge(sem("first_landed"), FIRST_LANDED)

            def squares(quarters, ready, name):
                for q in quarters:
                    half, t = divmod(q, T)
                    act.wait_ge(sem(ready[q][0]), ready[q][1])
                    cols = slice(half * 512, (half + 1) * 512)
                    act.activation(h[:, t, cols], x[:, t, cols], ACT.Square, accum_out=ss[:, q:q + 1]) \
                        .then_inc(sem(name), 1)

            def factor(tag):
                act.wait_ge(sem(f"ms_{tag}"), 1)
                act.activation(root, ms, ACT.Sqrt).then_inc(sem(f"root_{tag}"), 1)
                act.wait_ge(sem(f"rinv_{tag}"), 1)

            def mixed(gemms, product, ready, tag):
                evacuate(gemms[0], into(product, 0))
                quarters = [(ready, q + 1) for q in range(2 * T)]
                squares(range(T), quarters, f"ss_{tag}")
                act.activation(root, ones[:, 0:T], ACT.Sqrt)
                split_to(span[gemms[1]][1] + BUFFERS)
                squares(range(T, 2 * T), quarters, "gemm_read")
                if tag == "g1":
                    expert_split(0, range(BUFFERS))
                factor(tag)

            split = [0]
            misc_bank = pair_bank[2:4]

            def expert_split(it, pieces):
                for j in pieces:
                    i = j // 2
                    if j % 2 == 0:
                        act.wait_ge(sem(f"expert_landed{i % SLOTS}"),
                                    it * (16 * MOE_LOADS // SLOTS) + 16 * (i // SLOTS + 1))
                    act.wait_ge(sem("w_used"), it * MOE_SUBS + (USED0 + j - BUFFERS + 1))
                    act.activation(expert_buffer(w_hi_sb, j), expert_piece(j % MOE_SUBS), ACT.Copy) \
                        .then_inc(sem("w_hi_ready"), 1)

            def gathered_hi(number):
                for i in range(2):
                    act.wait_ge(sem("e_gathered"), number * 2 + i + 1)
                    act.activation(e_hi[:, 4 * i:4 * i + 4, :], tiles(gemm_bank[2 + i][:, 0:4 * CAP], 4), ACT.Copy) \
                        .then_inc(sem("e_hi_ready"), 1)

            def split_to(end):
                for j in range(split[0], min(end, len(subs))):
                    i, first_of_load, piece = subs[j]
                    if piece is not None:
                        w = raw(j)
                        if first_of_load:
                            act.wait_ge(sem(f"landed{slot_of[i]}"), landed[i])
                        if j >= BUFFERS:
                            act.wait_ge(sem("w_used"), j - BUFFERS + 1)
                        act.activation(buffer(w_hi_sb, j, *w.shape[1:]), w, ACT.Copy).then_inc(sem("w_hi_ready"), 1)
                    split[0] = j + 1

            def evacuate(name, parts):
                split_to(span[name][1] + BUFFERS)
                act.wait_ge(sem("w_used"), span[name][1])
                for t in range(T):
                    j = gemm_at[name] + t
                    todo = parts(t)
                    for n, (dst, lo, hi, func, scale) in enumerate(todo):
                        ins = act.activation(dst, gemm_bank[j % 4][:, lo:hi], func, scale=scale)
                        if n == len(todo) - 1:
                            ins.then_inc(sem("gemm_read"), 1)

            def into(dst, at, width=512, func=ACT.Copy, scale=1.0):
                return lambda t: [(dst[:, t, at:at + width], 0, width, func, scale)]

            def by_token(dst, at, width=512, func=ACT.Identity, factors=rinv):
                return lambda t: [(dst[:, t, at:at + width], 0, width, func, factors[:, t:t + 1])]

            squares(range(2 * T), [(f"x_landed{q // T}", 16) for q in range(2 * T)], "ss_f0")
            act.activation(root, ident[:, 0:T], ACT.Sqrt)
            split_to(BUFFERS)
            factor("f0")
            evacuate("gk", by_token(g_k, 0))
            act.wait_ge(sem("rinv_q_ready"), 1)
            evacuate("gq", by_token(g_q, 0, factors=rinv_q))
            evacuate("lr", by_token(g_lr, 0, 2 * GLA_RANK))
            evacuate("gv0", by_token(g_v, 0))
            for d in range(2):
                act.wait_ge(sem("pair_read"), pair_at["z"] + 2 * d + 2)
                link(act.activation(g_lg[:, d, :, :], g_lg[:, d, :, :], ACT.Exp, scale=-1.0))
                act.activation(g_lg[:, d, :, :], g_lg[:, d, :, :], ACT.Ln, bias=1.0).then_inc(sem("g_soft"), 1)
                act.wait_ge(sem("g_soft"), told("g_soft"))
            evacuate("gv1", by_token(g_v, 512))
            for d in range(2):
                act.wait_ge(sem("pair_read"), pair_at["gb"] + 2 * d + 2)
                link(act.activation(g_inv[d], g_dec[d], ACT.Exp, scale=-1.0))
                act.activation(g_dec[d], g_dec[d], ACT.Exp).then_inc(sem("g_exp"), 1)
                act.wait_ge(sem("g_exp"), told("g_exp"))
            for d in range(2):
                act.wait_ge(sem("pair_read"), pair_at["tail"] + d + 1)
                act.activation(g_kt[:, d, :], g_kt[:, d, :], ACT.Exp).then_inc(sem("g_tail_exp"), 1)
                act.wait_ge(sem("g_tail_exp"), told("g_tail_exp"))
            for i in range(2):
                evacuate(f"gr{i}", by_token(g_sr, 512 * i, func=ACT.Silu))
            for i in range(2):
                evacuate(f"sq{i}", by_token(s_qk_flat, 512 * i))
            evacuate("skv", lambda t: [(s_qk_flat[:, t, 1024:1280], 0, 256, ACT.Identity, rinv[:, t:t + 1]),
                                       (s_v[:, t, :], 256, 512, ACT.Identity, rinv[:, t:t + 1])])

            def head_norm(tag, n):
                act.wait_ge(sem(f"head_ms_{tag}"), 1)
                link(act.activation(head_rinv[:, 0:n], head_ms[:, 0:n], ACT.Ln))
                act.activation(head_rinv[:, 0:n], head_rinv[:, 0:n], ACT.Exp, scale=-0.5) \
                    .then_inc(sem(f"head_rinv_{tag}"), 1)
                act.wait_ge(sem(f"head_rinv_{tag}"), told(f"head_rinv_{tag}"))

            head_norm("g", 8)
            act.wait_ge(sem("g_kt_ready"), 2)
            for i in range(2):
                evacuate(f"ga{i}", by_token(gate_a, 512 * i, func=ACT.Sigmoid))
            head_norm("s", 20)
            act.wait_ge(sem("pair_full"), pair_end["go"])
            for i in range(2):
                evacuate(f"gb{i}", by_token(gate_b, 512 * i, func=ACT.Sigmoid))

            def softmax(scores, heads, negmax, ready, done, sink=None):
                for t in range(T):
                    if sink is None:
                        act.wait_ge(sem(ready), t + 1)
                    elif t == 0:
                        act.wait_ge(sem(ready), 1)
                        link(act.activation(sink, sink, ACT.Exp))
                    for i in range(heads):
                        at = t * heads + i
                        act.activation(scores[:, t, i, :], scores[:, t, i, :], ACT.Exp, bias=negmax[:, at:at + 1],
                                       accum_out=row_sum[:, at:at + 1]).then_inc(sem(done), 1)

            act.wait_ge(sem("pair_read"), pair_end["sT"])
            evacuate("og0", into(y_gla, 0))
            softmax(s_sc, SWA_HEADS, row_max, "s_max_ready", "s_exp", sink_exp)
            evacuate("og1", into(y_gla, 512))
            for i in range(2):
                evacuate(f"os{i}", into(y_swa, 512 * i))
            act.wait_ge(sem("merged"), 2)
            mixed(("wo0", "wo1"), gate_a, "x_mixed_f", "f1")

            def ffn(tag):
                for u in range(FFN_UNITS):
                    gate_end = span[f"{tag}_gate{u}"][1]
                    split_to(gate_end + BUFFERS)
                    act.wait_ge(sem("f_scaled"), FFN_UNITS * (tag == "f2") + u + 1)
                    if u >= 2:
                        act.wait_ge(sem(f"{tag}_hid"), u - 1)
                    act.activation(f_silu[u % 2], f_gate[u % 2], ACT.Silu) \
                        .then_inc(sem(f"{tag}_silu"), 1)
                split_to(ffn_range[tag][1] + BUFFERS)

            act.wait_ge(sem("pair_read"), pair_end["so"])
            act.dma_start(log_lb, A["hg_lower_bounds_2"][0:1, :].to_broadcast([P, 512])) \
                .then_inc(sem("bounds_landed"), 16)
            act.dma_start(log_rest, A["hg_lower_bounds_2"][1:2, :].to_broadcast([P, 512])) \
                .then_inc(sem("bounds_landed"), 16)
            ffn("f1")

            act.wait_ge(sem("angle_ready"), 2)
            link(act.activation(rope_sin[:, :, 32:64], rope_sin[:, :, 32:64], ACT.Sin))
            act.activation(rope_cos[:, :, 0:32], rope_cos[:, :, 0:32], ACT.Sin).then_inc(sem("sines"), 1)
            act.wait_ge(sem("sines"), told("sines"))

            for l in range(2):
                squares(range(2 * T), [(f"x_ffn_{l}", q + 1) for q in range(2 * T)], f"ss_l{l}")
                factor(f"l{l}")
                evacuate(f"hf_{l}", by_token(n_z, 0))
                next_gemm = span[f"hg_{l}"][0]
                split_to(next_gemm + 1)
                act.wait_ge(sem("z_abs"), l + 1)
                link(act.activation(n_tmp[0], n_tmp[0], ACT.Exp, scale=-1.0))
                if l == 0:
                    act.wait_ge(sem("bound_abs"), 1)
                    link(act.activation(soft, soft, ACT.Exp, scale=-1.0))
                act.activation(n_tmp[0], n_tmp[0], ACT.Ln, bias=1.0).then_inc(sem("z_soft"), 1)
                act.wait_ge(sem("z_soft"), told("z_soft"))
                if l == 0:
                    act.activation(soft, soft, ACT.Ln, bias=1.0).then_inc(sem("bound_soft"), 1)
                    act.wait_ge(sem("bound_soft"), told("bound_soft"))
                split_to(next_gemm + 2)
                if l == 1:
                    evacuate("hq_1", by_token(n_q, 0, func=ACT.Silu))
                    split_to(next_gemm + 5)
                    act.wait_ge(sem("mix_abs"), 1)
                    link(act.activation(n_tmp[1], n_tmp[1], ACT.Exp, scale=-1.0))
                    act.activation(n_tmp[1], n_tmp[1], ACT.Ln, bias=1.0).then_inc(sem("mix_soft"), 1)
                    act.wait_ge(sem("mix_soft"), told("mix_soft"))
                split_to(next_gemm + (3, 6)[l])
                act.wait_ge(sem(f"ln_k_{l}"), 1)
                act.activation(n_k[:, :, :], n_k[:, :, :], ACT.Exp).then_inc(sem("n_k_ready"), 1)
                act.wait_ge(sem("n_k_ready"), told("n_k_ready"))
                if l == 0:
                    evacuate("hq_0", by_token(n_q, 0, func=ACT.Silu))
                evacuate(f"hg_{l}", by_token(n_g, 0, func=ACT.Silu))
                act.wait_ge(sem("pair_read"), pair_end[f"ht_{l}"])
                act.activation(n_kt, n_kt, ACT.Exp).then_inc(sem("n_tail_exp"), 1)
                act.wait_ge(sem("n_tail_exp"), told("n_tail_exp"))
                act.activation(n_qd, n_bT[:, 512:1024], ACT.Exp).then_inc(sem("n_qd_exp"), 1)
                act.wait_ge(sem("n_qd_exp"), told("n_qd_exp"))

                def level_exp(n):
                    half = LEVELS[n - 1]
                    E = n_E[n % 2].rearrange("p (n s c) -> p n s c", s=2, c=half)
                    X = n_X[n % 2].rearrange("p (n s c) -> p n s c", s=2, c=half)
                    act.wait_ge(sem(f"level_diff_{l}"), n)
                    if n >= 3:
                        act.wait_ge(sem("pair_full"), pair_end[f"hlev{n - 2}_{l}"])
                    act.activation(X[:, :, 0, :], E[:, :, 0, :], ACT.Exp, scale=-1.0) \
                        .then_inc(sem(f"level_exp_{l}"), 1)
                    act.wait_ge(sem(f"level_exp_{l}"), told(f"level_exp_{l}"))
                    act.activation(X[:, :, 1, :], E[:, :, 1, :], ACT.Exp).then_inc(sem(f"level_exp_{l}"), 1)
                    act.wait_ge(sem(f"level_exp_{l}"), told(f"level_exp_{l}"))

                level_exp(1)
                level_exp(2)
                evacuate(f"c0_{l}", by_token(n_c, 0))
                evacuate(f"c1_{l}", by_token(n_c, 512, Q_RANK + KV_RANK + ROPE - 512))
                act.wait_ge(sem("gemm_read"), gemm_at[f"c1_{l}"] + T)
                for t in range(T):
                    for n, (lo, hi) in enumerate(((0, Q_RANK), (Q_RANK, Q_RANK + KV_RANK))):
                        act.activation(n_c_junk[:, lo:hi], n_c[:, t, lo:hi], ACT.Square,
                                       accum_out=head_ms[:, 8 + 2 * n + t:9 + 2 * n + t]) \
                                           .then_inc(sem(f"c_ss_{l}"), 1)
                        act.wait_ge(sem(f"c_ss_{l}"), told(f"c_ss_{l}"))
                act.wait_ge(sem("c_ms"), l + 1)
                link(act.activation(head_rinv[:, 8:12], head_ms[:, 8:12], ACT.Ln))
                act.activation(head_rinv[:, 8:12], head_rinv[:, 8:12], ACT.Exp, scale=-0.5) \
                    .then_inc(sem("c_rinv"), 1)
                act.wait_ge(sem("c_rinv"), told("c_rinv"))
                level_exp(3)
                evacuate(f"hi_{l}", by_token(n_v, 0))
                level_exp(4)
                evacuate(f"qb0_{l}", into(n_qm, 0, 384))
                level_exp(5)
                evacuate(f"qb1_{l}", into(n_qm, 384, 384))
                evacuate(f"kvb0_{l}", into(n_kvm, 0))
                level_exp(6)
                evacuate(f"kvb1_{l}", into(n_kvm, 512))
                level_exp(7)
                softmax(n_sc, MLA_HEADS, row_max, f"m_max_ready_{l}", f"m_exp_{l}")
                act.activation(root, ones[:, 0:T], ACT.Sqrt)
                act.wait_ge(sem(f"head_ms_h{l}"), 1)
                act.activation(head_rinv[:, 0:8], head_ms[:, 0:8], ACT.Sqrt).then_inc(sem(f"head_root_{l}"), 1)
                act.wait_ge(sem(f"head_root_{l}"), told(f"head_root_{l}"))
                if l == 1:
                    act.dma_start(e_gain, A["ffn_norm_2"][1:2, :].to_broadcast([P, D])) \
                        .then_inc(sem("expert_gain_landed"), 16)
                act.wait_ge(sem("pair_read"), pair_end[f"mixT_{l}"])
                mixed((f"wo0_{l}", f"wo1_{l}"), tiles(work(4096, 2048)), f"x_mixed_{l}", f"g{l}")
                if l == 0:
                    ffn("f2")

            act.dma_start(fin_gain, A["final_norm_2"].rearrange("(a n) -> a n", a=1).to_broadcast([P, D])) \
                .then_inc(sem("final_gain_landed"), 16)
            act.activation(root, ones[:, 0:T], ACT.Exp)
            for t in range(T):
                act.activation(h[:, t, :], x[:, t, :], ACT.Identity, scale=rinv[:, t:t + 1]).then_inc(sem("e_scaled"), 1)
            act.wait_ge(sem("e_gap"), 1)
            act.activation(e_g1, e_d, ACT.Exp).then_inc(sem("e_odds"), 1)
            act.wait_ge(sem("e_odds"), told("e_odds"))

            def expert(it, e, more):
                def finished(part):
                    act.wait_ge(sem("w_used"), it * MOE_SUBS + (USED0 + part_end[part]))

                def silu(s):
                    finished(("gate", s))
                    act.activation(e_silu[s % 2], gemm_bank[2 * (s % 2)][0:CAP, :], ACT.Silu) \
                        .then_inc(sem("e_silu_ready"), 1)

                def hidden_hi(s):
                    act.wait_ge(sem("e_hid_turned"), it * MOE_STEPS + s + 1)
                    act.activation(hid_hi[s % 2], misc_bank[s % 2][:, 0:4 * CAP], ACT.Copy) \
                        .then_inc(sem("e_hid_hi"), 1)

                at = BUFFERS
                for s in range(MOE_STEPS):
                    until = part_end["gate", s] + BUFFERS
                    expert_split(it, range(at, until))
                    silu(s)
                    if s >= 1:
                        expert_split(it, range(until, until + 1))
                        until += 1
                        hidden_hi(s - 1)
                    at = until
                expert_split(it, range(at, MOE_SUBS - 2))
                hidden_hi(MOE_STEPS - 1)
                expert_split(it, range(MOE_SUBS - 2, MOE_SUBS))
                if more:
                    gathered_hi(it + 1)
                act.wait_ge(sem("e_turned"), it + 1)
                act.activation(e_GT, pair_bank[3][0:CAP, 0:TOKENS], ACT.Copy).then_inc(sem("e_GT_ready"), 1)
                if more:
                    expert_split(it, range(MOE_SUBS, MOE_SUBS + BUFFERS - 1))
                act.wait_ge(sem("e_y0_done"), it + 1)
                act.activation(e_y[:, 0:512], pair_bank[0][0:CAP, :], ACT.Copy).then_inc(sem("e_y0_ready"), 1)
                finished(("down", MOE_STEPS - 1))
                act.activation(e_y[:, 512:1024], pair_bank[1][0:CAP, :], ACT.Copy).then_inc(sem("e_y1_ready"), 1)
                if more:
                    expert_split(it, range(MOE_SUBS + BUFFERS - 1, MOE_SUBS + BUFFERS))

            def one_round(r, again):
                if again:
                    expert_split(r * EXPERTS, range(BUFFERS))
                gathered_hi(r * EXPERTS)
                with act.Fori(0, EXPERTS - 1) as e:
                    expert(r * EXPERTS + e, e, True)
                expert(r * EXPERTS + (EXPERTS - 1), EXPERTS - 1, False)

            one_round(0, False)
            act.wait_ge(sem("rounds_known"), 1)
            rounds = act.value_load(e_rounds[0:1, 0:1], min_val=1, max_val=MAX_ROUNDS)
            with act.If(rounds > 1):
                with act.Fori(1, rounds) as r:
                    one_round(r, True)
            act.activation(root, ones[:, 0:T], ACT.Sqrt)
            for t in range(T):
                act.wait_ge(sem("e_added"), rounds * (4 * EXPERTS) + (4 - 2 * T + 2 * (t + 1)))
                act.activation(h[:, t, :], x[:, t, :], ACT.Square, accum_out=ss[:, t:t + 1]) \
                    .then_inc(sem("ss_last"), 1)
                act.wait_ge(sem("ss_last"), told("ss_last"))
            act.wait_ge(sem("ms_last"), 1)
            act.activation(root, ms, ACT.Sqrt).then_inc(sem("root_last"), 1)

        @block.vector
        def _(dve):
            told = counter()

            def link(instruction):
                instruction.then_inc(sem("vector_step"), 1)
                dve.wait_ge(sem("vector_step"), told("vector_step"))
            TWO_PI = 2 * np.pi

            def bank_of(name, i):
                j = pair_at[name] + i
                dve.wait_ge(sem("pair_full"), j + 1)
                return pair_bank[j % 4]

            def copy_out(name, i, dst, rows=P, width=512):
                dve.tensor_copy(dst, bank_of(name, i)[0:rows, 0:width]).then_inc(sem("pair_read"), 1)
                dve.wait_ge(sem("pair_read"), told("pair_read"))

            def mul(dst, one, two, name="vector_step"):
                dve.tensor_tensor(dst, one, two, ALU.mult).then_inc(sem(name), 1)
                dve.wait_ge(sem(name), told(name))

            def mean(dst, src, count, name):
                dve.tensor_scalar(dst, src, 1.0 / count, EPS, ALU.mult, ALU.add).then_inc(sem(name), 1)
                dve.wait_ge(sem(name), told(name))

            def negate(dst, src, name="vector_step"):
                dve.tensor_scalar(dst, src, -1.0, None, ALU.mult).then_inc(sem(name), 1)
                dve.wait_ge(sem(name), told(name))

            def absolute(dst, src, name="vector_step"):
                dve.scalar_tensor_tensor(dst, src, -1.0, src, ALU.mult, ALU.max).then_inc(sem(name), 1)
                dve.wait_ge(sem(name), told(name))

            def split_out(name, gain=None, banks=range(KD // 2), pieces=0):
                for i in banks:
                    b = tiles(bank_of(name, i)[:, :], 2)
                    k = slice(2 * i, 2 * i + 2)
                    hi, lo = left_hi[:, k, :], left_lo[:, k, :]
                    if gain is None:
                        link(dve.tensor_copy(hi, b))
                        dve.tensor_tensor(lo, b, hi.bitcast(F32), ALU.subtract).then_inc(sem("pair_read"), 1)
                    else:
                        mul(hi, b, over(gain[:, k], 2, TOKENS))
                        for n in range(2):
                            ins = dve.scalar_tensor_tensor(lo[:, n, :], b[:, n, :], gain[:, 2 * i + n:2 * i + n + 1],
                                                           hi[:, n, :].bitcast(F32), ALU.mult, ALU.subtract)
                        ins.then_inc(sem("pair_read"), 1)
                    dve.wait_ge(sem("pair_read"), told("pair_read"))
                    if pieces:
                        lo_to(low[0] + pieces)

            def expert_lo(it, pieces):
                for j in pieces:
                    dve.wait_ge(sem("w_hi_ready"), it * MOE_SUBS + (HI0 + j + 1))
                    dve.tensor_tensor(expert_buffer(w_lo_sb, j), expert_piece(j % MOE_SUBS),
                                      expert_buffer(w_hi_sb, j).bitcast(F32), ALU.subtract) \
                        .then_inc(sem("w_lo_by_vector"), 1)

            low = [0]

            def lo_to(end):
                for j in range(low[0], end):
                    if subs[j][2] is not None and lo_count[j][0] == "w_lo_by_vector":
                        w = raw(j)
                        dve.wait_ge(sem("w_hi_ready"), hi_count[j])
                        dve.tensor_tensor(buffer(w_lo_sb, j, *w.shape[1:]), w,
                                          buffer(w_hi_sb, j, *w.shape[1:]).bitcast(F32), ALU.subtract) \
                            .then_inc(sem("w_lo_by_vector"), 1)
                    low[0] = j + 1

            def mean_square(tag):
                if f"ss_{tag}_halves" in by_halves:
                    dve.wait_ge(sem("gemm_read"), by_halves[f"ss_{tag}_halves"])
                    dve.wait_ge(sem(f"ss_{tag}"), T)
                else:
                    dve.wait_ge(sem(f"ss_{tag}"), 2 * T)
                link(dve.tensor_tensor(ms, ss[:, 0:T], ss[:, T:2 * T], ALU.add))
                mean(ms, ms, D, f"ms_{tag}")

            def factor(tag):
                dve.wait_ge(sem(f"root_{tag}"), 1)
                dve.reciprocal(rinv, root).then_inc(sem(f"rinv_{tag}"), 1)
                dve.wait_ge(sem(f"rinv_{tag}"), told(f"rinv_{tag}"))

            by_halves = {"ss_f1_halves": gemm_at["wo1"] + T, "ss_g0_halves": gemm_at["wo1_0"] + T,
                         "ss_g1_halves": gemm_at["wo1_1"] + T}

            def norm(tag):
                split_out(f"hT_{tag}", gain_T[tag])
                mean_square(tag)
                factor(tag)
                for t in range(T):
                    dve.tensor_scalar(f_diag[:, t, :], ident, rinv[:, t:t + 1], None, ALU.mult) \
                        .then_inc(sem("diagonals"), 1)
                    dve.wait_ge(sem("diagonals"), told("diagonals"))

            dve.wait_ge(sem("first_landed"), FIRST_LANDED)
            split_out("hT_f0", gain_T["f0"], pieces=1)
            mean_square("f0")
            factor("f0")
            dve.tensor_scalar(rinv_q, rinv, GLA_DK ** -0.5, None, ALU.mult).then_inc(sem("rinv_q_ready"), 1)
            dve.wait_ge(sem("rinv_q_ready"), told("rinv_q_ready"))
            lo_to(FIRST_SUBS)
            copy_out("lrT", 0, g_lrT[:, :, :].rearrange("p a c -> p (a c)"), GLA_RANK)
            for a in range(2):
                for t in range(T):
                    b = bank_of("z", 2 * a + t)
                    dve.tensor_scalar(g_lg[:, a, t, :], b[:, :], -30.0, None, ALU.max).then_inc(sem("pair_read"), 1)
                    dve.wait_ge(sem("pair_read"), told("pair_read"))
            for t in range(T):
                copy_out("gqT", t, g_qT[:, t * 512:(t + 1) * 512])
            for t in range(T):
                copy_out("gkT", t, g_kT[:, t * 512:(t + 1) * 512])
            for a in range(2):
                dve.wait_ge(sem("g_soft"), a + 1)
                dve.tensor_scalar(g_lg[:, a, :, :], g_lg[:, a, :, :], -1.0 / 16, -0.5, ALU.mult, ALU.max) \
                    .then_inc(sem("g_lg_ready"), 1)
                dve.wait_ge(sem("g_lg_ready"), told("g_lg_ready"))
            for a in range(2):
                for t in range(T):
                    copy_out("gb", 2 * a + t, g_dec[a][:, t * 512:(t + 1) * 512])
            for a in range(2):
                copy_out("tail", a, g_kt[:, a, :])
            dve.wait_ge(sem("small_landed"), SMALL_LANDED)
            flat_w = router_w[:, :, :].rearrange("p k e -> p (k e)")
            link(dve.tensor_copy(router_hi_sb[:, :], flat_w))
            link(dve.tensor_tensor(router_lo_sb[:, :], flat_w, router_hi_sb[:, :].bitcast(F32), ALU.subtract))
            for n in range(2):
                for t in range(T):
                    gain = s_gain[:, n, :]
                    dve.tensor_tensor(s_cos[:, n, t, :], swa_cos[:, t, :], gain, ALU.mult)
                    dve.tensor_tensor(s_sin[:, n, t, 0:64], swa_sin[:, t, 0:64], gain[:, 64:128], ALU.mult)
                    mul(s_sin[:, n, t, 64:128], swa_sin[:, t, 64:128], gain[:, 0:64])
            for a in range(2):
                dve.wait_ge(sem("g_exp"), a + 1)
                mul(g_inv[a], g_inv[a], g_kT, "g_inv_ready")
                mul(g_dec[a], g_dec[a], g_qT, "g_dec_ready")
            for a in range(2):
                dve.wait_ge(sem("g_tail_exp"), a + 1)
                mul(g_kt[:, a, :], g_kt[:, a, :], g_k[:, a, :], "g_kt_ready")
            for a in range(2):
                for t in range(T):
                    b = tiles(bank_of("gsc", 2 * a + t)[:, :], 4)
                    mul(g_sc[:, a, t, :, :], b, over((le, gt)[a], 1, 4), "pair_read")
            for i in range(4):
                copy_out("gst", i, g_st[:, i // 2, 2 * (i % 2):2 * (i % 2) + 2, :].rearrange("p h e -> p (h e)"))
            dve.wait_ge(sem("gemm_read"), gemm_at["gr1"] + T)
            for t in range(T):
                silu = g_sr[:, t, :].rearrange("p (h e) -> p h e", e=GLA_DV)
                mul(silu, silu, over(g_gain, 1, GLA_HEADS))
            for i in range(4):
                copy_out("go", i, g_o[:, i * 512:(i + 1) * 512])
            heads = g_o.rearrange("p (g e) -> p g e", e=GLA_DV)
            mul(g_tmp, g_o, g_o)
            link(dve.tensor_reduce(head_ms[:, 0:8], g_tmp.rearrange("p (g e) -> p g e", e=GLA_DV), AX_X, ALU.add))
            mean(head_ms[:, 0:8], head_ms[:, 0:8], GLA_DV, "head_ms_g")
            dve.wait_ge(sem("head_rinv_g"), 1)
            mul(heads, heads, over(head_rinv[:, 0:8], 2, GLA_DV))
            mul(g_o, g_o, h_sb[:, :], "g_out")
            dve.wait_ge(sem("gemm_read"), gemm_at["skv"] + T)
            flat = lambda a: a[:, :, :, :].rearrange("p t h d -> p (t h) d")
            mul(flat(s_b), flat(s_qk), flat(s_qk))
            link(dve.tensor_reduce(head_ms[:, 0:20], flat(s_b), AX_X, ALU.add))
            mean(head_ms[:, 0:20], head_ms[:, 0:20], HD, "head_ms_s")
            dve.wait_ge(sem("head_rinv_s"), 1)
            mul(flat(s_qk), flat(s_qk), over(head_rinv[:, 0:20], 2, HD))
            for t in range(T):
                for n, heads in enumerate((slice(0, 8), slice(8, 10))):
                    part, a_, b_ = (z[:, t, heads, :] for z in (s_qk, s_a, s_b))
                    count = heads.stop - heads.start
                    dve.tensor_tensor(a_, part, over(s_cos[:, n, t, :], 1, count), ALU.mult)
                    dve.tensor_tensor(b_[:, :, 0:64], part[:, :, 64:128], over(s_sin[:, n, t, 0:64], 1, count), ALU.mult)
                    mul(b_[:, :, 64:128], part[:, :, 0:64], over(s_sin[:, n, t, 64:128], 1, count))
                dve.tensor_tensor(s_a[:, t, :, :], s_a[:, t, :, :], s_b[:, t, :, :], ALU.add) \
                    .then_inc(sem("s_rot"), 1)
                dve.wait_ge(sem("s_rot"), told("s_rot"))
            for i in range(5):
                copy_out("sT", i, s_qkT[:, 2 * i:2 * i + 2, :].rearrange("p k c -> p (k c)"))

            def masked_scores(name, scores, n_heads, scale, mask, tiles_of=range(T)):
                for t in tiles_of:
                    for i in range(n_heads // 2):
                        b = tiles(bank_of(name, (t - tiles_of[0]) * n_heads // 2 + i)[:, :], 2)
                        dve.scalar_tensor_tensor(scores[:, t, 2 * i:2 * i + 2, :], b, scale,
                                                 over(mask[:, t, :], 1, 2), ALU.mult, ALU.add) \
                                                     .then_inc(sem("pair_read"), 1)
                        dve.wait_ge(sem("pair_read"), told("pair_read"))

            def row_maxima(scores, n_heads):
                link(dve.tensor_reduce(row_max[:, 0:T * n_heads], scores[:, :, :, :].rearrange("p t h k -> p (t h) k"),
                                       AX_X, ALU.max))

            def attended(names, weightsT, n_heads, to, between=None):
                for t in range(T):
                    for i in range(n_heads // 2):
                        copy_out(names[0], t * n_heads // 2 + i,
                                 weightsT[:, t, 2 * i:2 * i + 2, :, :].rearrange("p h b q -> p (h b q)"))
                if between is not None:
                    between()
                for t in range(T):
                    for i in range(n_heads // 4):
                        b = tiles(bank_of(names[1], t * n_heads // 4 + i)[:, :], 4)
                        at = t * n_heads + 4 * i
                        mul(to[:, t, 512 * i:512 * (i + 1)].rearrange("p (h d) -> p h d", h=4), b,
                            over(row_rec[:, at:at + 4], 2, P), "pair_read")

            masked_scores("ssc", s_sc, SWA_HEADS, HD ** -0.5, window)
            split_out("goT")
            row_maxima(s_sc, SWA_HEADS)
            sink_all = over(sinks, 1, T)
            link(dve.tensor_tensor(tiles(row_max), tiles(row_max), sink_all, ALU.max))
            link(dve.tensor_tensor(tiles(sink_exp), sink_all, tiles(row_max), ALU.subtract))
            negate(row_max, row_max, "s_max_ready")
            dve.wait_ge(sem("s_exp"), T * SWA_HEADS)
            link(dve.tensor_tensor(row_sum, row_sum, sink_exp, ALU.add))
            link(dve.reciprocal(row_rec, row_sum))
            attended(("sP", "so"), s_pT, SWA_HEADS, s_o)
            split_out("soT")
            dve.wait_ge(sem("gemm_read"), gemm_at["og1"] + T)
            mul(y_gla, y_gla, gate_a)
            for half in range(2):
                cols = slice(half * 512, (half + 1) * 512)
                dve.wait_ge(sem("gemm_read"), gemm_at[f"os{half}"] + T)
                mul(y_swa[:, :, cols], y_swa[:, :, cols], gate_b[:, :, cols])
                dve.tensor_tensor(y_gla[:, :, cols], y_gla[:, :, cols], y_swa[:, :, cols], ALU.add) \
                    .then_inc(sem("merged"), 1)
                dve.wait_ge(sem("merged"), told("merged"))
                split_out("mT", banks=range(2 * half, 2 * half + 2))

            def residual(product, gemms, name):
                dve.wait_ge(sem("gemm_read"), gemm_at[gemms[0]] + T)
                for t in range(T):
                    dve.tensor_tensor(x[:, t, 0:512], x[:, t, 0:512], product[:, t, 0:512], ALU.add) \
                        .then_inc(sem(name), 1)
                dve.wait_ge(sem("w_used"), span[gemms[1]][1])
                for t in range(T):
                    dve.tensor_tensor(x[:, t, 512:1024], x[:, t, 512:1024],
                                      gemm_bank[(gemm_at[gemms[1]] + t) % 4][:, :], ALU.add).then_inc(sem(name), 1)
                dve.wait_ge(sem(name), 2 * T)

            def ffn(tag, norm_tag, done):
                for u in range(FFN_UNITS):
                    gate_end, up_end = (span[f"{tag}_{kind}{u}"][1] for kind in ("gate", "up"))
                    row = over(f_row, 1, 2)
                    lo_to(min(gate_end + BUFFERS, ffn_range[tag][1]))
                    if u == 0:
                        copy_out(f"row_{norm_tag}", 0, f_row, P, TOKENS)
                    dve.wait_ge(sem("w_used"), gate_end)
                    mul(tiles(f_gate[u % 2]), tiles(gemm_bank[2 * (u % 2)][:, :]), row, "f_scaled")
                    lo_to(min(up_end + BUFFERS, ffn_range[tag][1]))
                    dve.wait_ge(sem("w_used"), up_end)
                    mul(tiles(f_up), tiles(gemm_bank[2 * (u % 2) + 1][:, :]), row)
                    dve.wait_ge(sem(f"{tag}_silu"), u + 1)
                    mul(f_hid, f_silu[u % 2], f_up)
                    link(dve.tensor_copy(hid_hi[u % 2], f_hid))
                    dve.tensor_tensor(hid_lo[u % 2], f_hid, hid_hi[u % 2].bitcast(F32), ALU.subtract) \
                        .then_inc(sem(f"{tag}_hid"), 1)
                    dve.wait_ge(sem(f"{tag}_hid"), told(f"{tag}_hid"))
                lo_to(ffn_range[tag][1])
                dve.wait_ge(sem("half_done"), ("f1", "f2").index(tag) + 1)
                for half in range(2):
                    if half == 1:
                        dve.wait_ge(sem("w_used"), ffn_range[tag][1])
                    for t in range(T):
                        part = x[:, t, half * 512:(half + 1) * 512]
                        dve.tensor_tensor(part, part, sum_bank(tag, half, t)[:, :], ALU.add).then_inc(sem(done), 1)
                        dve.wait_ge(sem(done), told(done))

            residual(gate_a, ("wo0", "wo1"), "x_mixed_f")
            norm("f1")
            ang, turns, rest = (tiles(scratch(64 * i, 64)) for i in range(3))
            link(dve.tensor_copy(pos_f, position))
            for t in range(T):
                link(dve.tensor_scalar(ang[:, t, :], inv_freq, pos_f[:, t:t + 1], None, ALU.mult))
            magic = float(1.5 * 2 ** 23)
            link(dve.tensor_scalar(turns, ang, 1.0 / TWO_PI, None, ALU.mult))
            link(dve.tensor_scalar(turns, turns, magic, None, ALU.add))
            link(dve.tensor_scalar(turns, turns, magic, None, ALU.subtract))
            part1 = 6.28125
            part2 = float(np.float32(round((TWO_PI - part1) * 2 ** 20) / 2 ** 20))
            for n, part in enumerate((part1, part2, TWO_PI - part1 - part2)):
                link(dve.scalar_tensor_tensor(rest, turns, -part, ang if n == 0 else rest, ALU.mult, ALU.add))
            edge = 3.1415925
            dve.tensor_scalar(rope_sin[:, :, 32:64], rest, edge, -edge, ALU.min, ALU.max) \
                .then_inc(sem("angle_ready"), 1)
            dve.wait_ge(sem("angle_ready"), told("angle_ready"))
            link(dve.tensor_scalar(rest, rest, np.pi / 2, None, ALU.add))
            link(dve.tensor_scalar(turns, rest, edge, -TWO_PI, ALU.is_gt, ALU.mult))
            link(dve.tensor_tensor(rest, rest, turns, ALU.add))
            dve.tensor_scalar(rope_cos[:, :, 0:32], rest, edge, -edge, ALU.min, ALU.max) \
                .then_inc(sem("angle_ready"), 1)
            dve.wait_ge(sem("angle_ready"), told("angle_ready"))
            ffn("f1", "f1", "x_ffn_0")
            dve.wait_ge(sem("sines"), 1)
            link(dve.tensor_copy(rope_cos[:, :, 32:64], rope_cos[:, :, 0:32]))
            negate(rope_sin[:, :, 0:32], rope_sin[:, :, 32:64])

            for l in range(2):
                split_out(f"hT_l{l}", gain_T[f"l{l}"])
                mean_square(f"l{l}")
                factor(f"l{l}")
                if l == 0:
                    dve.wait_ge(sem("bounds_landed"), 32)
                    link(dve.tensor_tensor(diff, log_rest, log_lb, ALU.subtract))
                    absolute(soft, diff, "bound_abs")
                flat_z, flat_lf, flat_k = (a[:, :, :].rearrange("p t n -> p (t n)") for a in (n_z, n_lf, n_k))
                dve.wait_ge(sem("gemm_read"), gemm_at[f"hf_{l}"] + T)
                absolute(n_tmp[0], flat_z, "z_abs")
                dve.wait_ge(sem("z_soft"), l + 1)
                link(dve.scalar_tensor_tensor(flat_lf, flat_z, 0.0, n_tmp[0], ALU.min, ALU.subtract))
                link(dve.scalar_tensor_tensor(flat_k, flat_z, 0.0, n_tmp[0], ALU.max, ALU.add))
                if l == 0:
                    negate(flat_k, flat_k, "ln_k_0")
                    dve.tensor_scalar(flat_lf, flat_lf, LN_F_FLOOR, None, ALU.max).then_inc(sem("n_lf_ready_0"), 1)
                    dve.wait_ge(sem("n_lf_ready_0"), told("n_lf_ready_0"))
                    dve.wait_ge(sem("bound_soft"), 1)
                    link(dve.scalar_tensor_tensor(log_lb, diff, 0.0, soft, ALU.min, ALU.subtract))
                    link(dve.scalar_tensor_tensor(log_rest, diff, 0.0, soft, ALU.max, ALU.add))
                    negate(log_rest, log_rest)
                else:
                    link(dve.tensor_tensor(n_lf, n_lf, over(log_rest, 1, T), ALU.add))
                    link(dve.tensor_tensor(tiles(n_tmp[2]), over(log_lb, 1, T), n_lf, ALU.subtract))
                    absolute(n_tmp[1], n_tmp[2], "mix_abs")
                    link(dve.tensor_tensor(n_lf, n_lf, over(log_lb, 1, T), ALU.max))
                    dve.scalar_tensor_tensor(n_k, n_k, -1.0, over(log_rest, 1, T), ALU.mult, ALU.add) \
                        .then_inc(sem("ln_k_1"), 1)
                    dve.wait_ge(sem("ln_k_1"), told("ln_k_1"))
                    dve.wait_ge(sem("mix_soft"), 1)
                    link(dve.tensor_tensor(flat_lf, flat_lf, n_tmp[1], ALU.add))
                    dve.tensor_scalar(flat_lf, flat_lf, LN_F_FLOOR, None, ALU.max).then_inc(sem("n_lf_ready_1"), 1)
                    dve.wait_ge(sem("n_lf_ready_1"), told("n_lf_ready_1"))
                for t in range(T):
                    copy_out(f"hkT_{l}", t, n_kT[:, t * 512:(t + 1) * 512])
                for t in range(T):
                    copy_out(f"hb_{l}", t, n_bT[:, t * 512:(t + 1) * 512])
                copy_out(f"ht_{l}", 0, n_kt)

                def blocks(a, half):
                    return a.rearrange("p (n c) -> p n c", c=2 * half)

                def halves(a, half):
                    return a.rearrange("p (n s c) -> p n s c", s=2, c=half)

                def level_diff(n):
                    half = LEVELS[n - 1]
                    if n >= 3:
                        dve.wait_ge(sem(f"level_exp_{l}"), 2 * (n - 2))
                    b = blocks(n_bT, half)
                    middle = b[:, :, half - 1]
                    dve.tensor_tensor(blocks(n_E[n % 2], half), b, over(middle, 2, 2 * half), ALU.subtract) \
                        .then_inc(sem(f"level_diff_{l}"), 1)
                    dve.wait_ge(sem(f"level_diff_{l}"), told(f"level_diff_{l}"))

                def level_scale(n):
                    half = LEVELS[n - 1]
                    dve.wait_ge(sem(f"level_exp_{l}"), 2 * n)
                    for side, other in enumerate((n_kT, n_qT)):
                        part = halves(n_X[n % 2], half)[:, :, side, :]
                        mul(part, part, halves(other, half)[:, :, side, :], f"level_ready_{l}")

                def level_take(n):
                    for t in range(T):
                        b = tiles(bank_of(f"hlev{n}_{l}", t)[:, :], 4)
                        to = tiles(n_at[:, t * 512:(t + 1) * 512], 4)
                        if n == 0:
                            mul(to, b, over(ident, 1, 4), "pair_read")
                        else:
                            mask = over(level_masks[:, n * P:(n + 1) * P], 1, 4)
                            dve.copy_predicated(to, mask, b).then_inc(sem("pair_read"), 1)
                            dve.wait_ge(sem("pair_read"), told("pair_read"))

                def rotate(part, heads):
                    ra, rb = work(1280, 256), work(1536, 256)
                    for t in range(T):
                        a_, b_ = (r[:, 0:heads * ROPE].rearrange("p (h d) -> p h d", h=heads) for r in (ra, rb))
                        mul(a_, part(t), over(rope_cos[:, t, :], 1, heads))
                        mul(b_[:, :, 0:32], part(t)[:, :, 32:64], over(rope_sin[:, t, 0:32], 1, heads))
                        mul(b_[:, :, 32:64], part(t)[:, :, 0:32], over(rope_sin[:, t, 32:64], 1, heads))
                        dve.tensor_tensor(part(t), a_, b_, ALU.add).then_inc(sem(f"m_rot_{l}"), 1)
                        dve.wait_ge(sem(f"m_rot_{l}"), told(f"m_rot_{l}"))

                def normalize_c():
                    dve.wait_ge(sem(f"c_ss_{l}"), 2 * T)
                    mean(head_ms[:, 8:10], head_ms[:, 8:10], Q_RANK, "vector_step")
                    mean(head_ms[:, 10:12], head_ms[:, 10:12], KV_RANK, "c_ms")
                    dve.wait_ge(sem("c_rinv"), l + 1)
                    for n, (lo, hi) in enumerate(((0, Q_RANK), (Q_RANK, Q_RANK + KV_RANK))):
                        for t in range(T):
                            at = 8 + 2 * n + t
                            dve.tensor_scalar(n_c[:, t, lo:hi], n_c[:, t, lo:hi], head_rinv[:, at:at + 1], None,
                                              ALU.mult).then_inc(sem(f"c_normed_{l}"), 1)
                            dve.wait_ge(sem(f"c_normed_{l}"), told(f"c_normed_{l}"))

                def gate_hgrn():
                    dve.wait_ge(sem(f"head_root_{l}"), 1)
                    link(dve.reciprocal(head_rinv[:, 0:8], head_rinv[:, 0:8]))
                    for t in range(T):
                        o = n_o[:, t, :].rearrange("p (g d) -> p g d", d=P)
                        mul(o, o, over(head_rinv[:, 4 * t:4 * t + 4], 2, P))
                    for t in range(T):
                        mul(n_o[:, t, :], n_o[:, t, :], n_g[:, t, :], f"hg_mixed_{l}")

                level_diff(1)
                level_diff(2)
                for t in range(T):
                    copy_out(f"hqT_{l}", t, n_qT[:, t * 512:(t + 1) * 512])
                level_scale(1)
                level_take(0)
                dve.wait_ge(sem("n_tail_exp"), l + 1)
                mul(n_kt, n_kt, n_k[:, 0, :], "n_kt_ready")
                dve.wait_ge(sem("n_qd_exp"), l + 1)
                mul(n_qd, n_qd, n_qT[:, 512:1024], "n_qd_ready")
                level_diff(3)
                level_scale(2)
                normalize_c()
                rotate(lambda t: n_c[:, t, Q_RANK + KV_RANK:].rearrange("p (h d) -> p h d", h=1), 1)
                level_take(1)
                level_diff(4)
                level_take(2)
                for i in range(3):
                    n = min(2, 5 - 2 * i)
                    b = tiles(bank_of(f"cT_{l}", i)[:, 0:n * TOKENS], n)
                    mul(n_cT[:, 2 * i:2 * i + n, :], b, over(c_gain[l][:, 2 * i:2 * i + n], 2, TOKENS), "pair_read")
                level_scale(3)
                level_diff(5)
                level_scale(4)
                gains = n_g[:, :, :].rearrange("p t (g d) -> p (t g) d", d=P)
                mul(gains, gains, over(hg_gain[l], 1, 8))
                level_take(3)
                level_diff(6)
                level_scale(5)
                dve.wait_ge(sem("gemm_read"), gemm_at[f"qb1_{l}"] + T)
                rotate(lambda t: n_qm[:, t, :].rearrange("p (h d) -> p h d", h=MLA_HEADS)[:, :, NOPE:192], MLA_HEADS)
                level_take(4)
                level_diff(7)
                level_scale(6)
                copy_out(f"hst_{l}", 0, n_st)
                for name, to in ((f"mqT_{l}", n_mqT), (f"mkT_{l}", n_mkT)):
                    for i in range(2):
                        copy_out(name, i, to[:, 2 * i:2 * i + 2, :].rearrange("p k c -> p (k c)"))
                for i in range(2):
                    copy_out(f"mpT_{l}", i, n_pqT[:, 2 * i:2 * i + 2, :].rearrange("p k c -> p (k c)"), ROPE)
                copy_out(f"mpT_{l}", 2, n_pkT, ROPE, TOKENS)
                level_take(5)
                level_scale(7)
                level_take(6)
                for t in range(T):
                    if t == 1:
                        level_take(7)
                    masked_scores(f"msc{t}_{l}", n_sc, MLA_HEADS, (NOPE + ROPE) ** -0.5, causal, [t])
                    part = row_max[:, t * MLA_HEADS:(t + 1) * MLA_HEADS]
                    link(dve.tensor_reduce(part, n_sc[:, t, :, :], AX_X, ALU.max))
                    negate(part, part, f"m_max_ready_{l}")
                for t in range(T):
                    copy_out(f"ho_{l}", t, n_o[:, t, :])

                def between():
                    for t in range(T):
                        mul(tiles(n_tmp[0])[:, t, :], n_o[:, t, :], n_o[:, t, :])
                    link(dve.tensor_reduce(head_ms[:, 0:8], n_tmp[0].rearrange("p (g d) -> p g d", d=P), AX_X, ALU.add))
                    mean(head_ms[:, 0:8], head_ms[:, 0:8], P, f"head_ms_h{l}")
                    dve.wait_ge(sem(f"m_exp_{l}"), T * MLA_HEADS)
                    link(dve.reciprocal(row_rec[:, 0:8], row_sum[:, 0:8]))

                attended((f"mP_{l}", f"mo_{l}"), n_pT, MLA_HEADS, mix, between)
                split_out(f"mixT_{l}", banks=range(0, 2))
                gate_hgrn()
                split_out(f"mixT_{l}", banks=range(2, 4))
                residual(tiles(work(4096, 2048)), (f"wo0_{l}", f"wo1_{l}"), f"x_mixed_{l}")
                if l == 0:
                    norm("g0")
                    ffn("f2", "g0", "x_ffn_1")

            split_out("hT_g1", gain_T["g1"])
            mean_square("g1")
            factor("g1")
            copy_out("routerT", 0, e_logitT, EXPERTS, TOKENS)
            b = bank_of("router", 0)
            for t in range(T):
                ins = dve.tensor_scalar(e_logit[:, t, :], b[:, t * EXPERTS:(t + 1) * EXPERTS], rinv[:, t:t + 1], None,
                                        ALU.mult)
            ins.then_inc(sem("pair_read"), 1)
            dve.wait_ge(sem("pair_read"), told("pair_read"))
            for t in range(T):
                link(dve.max(e_top[:, t, :], e_logit[:, t, :]))
                link(dve.max_index(e_idx[:, t, :], e_top[:, t, :], e_logit[:, t, :]))
            link(dve.tensor_copy(e_idf, e_idx))
            dve.tensor_tensor(e_d, e_top[:, :, 1], e_top[:, :, 0], ALU.subtract).then_inc(sem("e_gap"), 1)
            dve.wait_ge(sem("e_gap"), told("e_gap"))
            for t in range(T):
                for n, one_hot in enumerate((e_oh0, e_oh1)):
                    link(dve.tensor_scalar(one_hot[:, t, :], iota[:, 0:EXPERTS], e_idf[:, t, n:n + 1], None, ALU.is_equal))
            dve.tensor_tensor(e_mask, e_oh0, e_oh1, ALU.add).then_inc(sem("e_mask_ready"), 1)
            dve.wait_ge(sem("e_mask_ready"), told("e_mask_ready"))
            dve.wait_ge(sem("e_odds"), 1)
            link(dve.tensor_scalar(e_g0, e_g1, 1.0, None, ALU.add))
            link(dve.reciprocal(e_g0, e_g0))
            mul(e_g1, e_g1, e_g0)
            for t in range(T):
                link(dve.tensor_scalar(e_prob[:, t, :], e_oh0[:, t, :], e_g0[:, t:t + 1], None, ALU.mult))
                link(dve.scalar_tensor_tensor(e_prob[:, t, :], e_oh1[:, t, :], e_g1[:, t:t + 1], e_prob[:, t, :],
                                              ALU.mult, ALU.add))
            b = bank_of("ranks", 0)
            far = float(4 * TOKENS)
            link(dve.tensor_reduce(e_cnt, b[:, 16:24], AX_X, ALU.max))
            dve.scalar_tensor_tensor(e_pos, e_mask, -far, tiles(b[:, 0:16]), ALU.mult, ALU.add) \
                .then_inc(sem("pair_read"), 1)
            dve.wait_ge(sem("pair_read"), told("pair_read"))
            dve.tensor_scalar(e_pos, e_pos, far, None, ALU.add).then_inc(sem("e_added"), 4)
            dve.wait_ge(sem("e_added"), 4)
            def count_rounds():
                link(dve.tensor_scalar(e_cntx[:, 0:1], e_cnt, float(CAP), 1.0, ALU.is_gt, ALU.add))
                for n in range(2, MAX_ROUNDS):
                    link(dve.tensor_scalar(e_cntx[:, 1:2], e_cnt, float(n * CAP), None, ALU.is_gt))
                    link(dve.tensor_tensor(e_cntx[:, 0:1], e_cntx[:, 0:1], e_cntx[:, 1:2], ALU.add))
                dve.tensor_copy(e_rounds, e_cntx[:, 0:1]).then_inc(sem("rounds_known"), 1)
                dve.wait_ge(sem("rounds_known"), told("rounds_known"))

            def place(number, e):
                for t in range(T):
                    dve.tensor_scalar(e_P[:, t, :], iota, e_pos[:, t, bass.ds(e, 1)], None, ALU.is_equal) \
                        .then_inc(sem("e_placed"), 1)
                    dve.wait_ge(sem("e_placed"), T * number + t + 1)

            def gathered_lo(number):
                for i in range(2):
                    dve.wait_ge(sem("e_hi_ready"), number * 2 + i + 1)
                    k = slice(4 * i, 4 * i + 4)
                    dve.tensor_tensor(e_lo[:, k, :], tiles(gemm_bank[2 + i][:, 0:4 * CAP], 4),
                                      e_hi[:, k, :].bitcast(F32), ALU.subtract).then_inc(sem("e_x_ready"), 1)

            def expert(it, e, more):
                def multiply(s):
                    dve.wait_ge(sem("e_silu_ready"), it * MOE_STEPS + s + 1)
                    dve.wait_ge(sem("w_used"), it * MOE_SUBS + (USED0 + part_end["up", s]))
                    dve.tensor_tensor(e_hid[s % 2], e_silu[s % 2], gemm_bank[2 * (s % 2) + 1][0:CAP, :], ALU.mult) \
                        .then_inc(sem("e_hid_ready"), 1)

                def hidden_lo(s):
                    dve.wait_ge(sem("e_hid_hi"), it * MOE_STEPS + s + 1)
                    dve.tensor_tensor(hid_lo[s % 2], pair_bank[2 + s % 2][:, 0:4 * CAP], hid_hi[s % 2].bitcast(F32),
                                      ALU.subtract).then_inc(sem("e_hid_split"), 1)

                at = BUFFERS
                for s in range(MOE_STEPS):
                    if s >= 1:
                        until = part_end["gate", s] + BUFFERS + 1
                        expert_lo(it, range(at, until))
                        hidden_lo(s - 1)
                        at = until
                    until = part_end["up", s] + BUFFERS
                    expert_lo(it, range(at, until))
                    multiply(s)
                    at = until
                    if s == 2:
                        for t in range(T):
                            dve.tensor_scalar(e_G[:, t, :], e_P[:, t, :], e_prob[:, t, bass.ds(e, 1)], None, ALU.mult) \
                                .then_inc(sem("e_weighted"), 1)
                            dve.wait_ge(sem("e_weighted"), T * it + t + 1)
                    if s == 4 and more:
                        place(it + 1, e + 1)
                expert_lo(it, range(at, MOE_SUBS - 2))
                hidden_lo(MOE_STEPS - 1)
                expert_lo(it, range(MOE_SUBS - 2, MOE_SUBS))
                if more:
                    gathered_lo(it + 1)
                    expert_lo(it, range(MOE_SUBS, MOE_SUBS + BUFFERS))
                for t in range(T):
                    for half in range(2):
                        dve.wait_ge(sem("e_scattered"), 4 * it + (2 * t + half + 1))
                        part = x[:, t, half * 512:(half + 1) * 512]
                        b = pair_bank[(2, 0)[half] + t]
                        dve.tensor_tensor(part, part, b[:, :], ALU.add).then_inc(sem("e_added"), 1)
                dve.wait_ge(sem("e_added"), 4 * it + 8)

            def one_round(r, first=False):
                place(r * EXPERTS, 0)
                if first:
                    count_rounds()
                expert_lo(r * EXPERTS, range(BUFFERS))
                gathered_lo(r * EXPERTS)
                with dve.Fori(0, EXPERTS - 1) as e:
                    expert(r * EXPERTS + e, e, True)
                expert(r * EXPERTS + (EXPERTS - 1), EXPERTS - 1, False)

            one_round(0, True)
            rounds = dve.value_load(e_rounds[0:1, 0:1], min_val=1, max_val=MAX_ROUNDS)
            with dve.If(rounds > 1):
                with dve.Fori(1, rounds) as r:
                    dve.tensor_scalar(e_pos, e_pos, float(CAP), None, ALU.subtract).then_inc(sem("e_shifted"), 1)
                    dve.wait_ge(sem("e_shifted"), r)
                    one_round(r)
            dve.wait_ge(sem("ss_last"), T)
            mean(ms, ss[:, 0:T], D, "ms_last")
            factor("last")
            dve.wait_ge(sem("final_gain_landed"), 16)
            for t in range(T):
                dve.scalar_tensor_tensor(x[:, t, :], x[:, t, :], rinv[:, t:t + 1], fin_gain, ALU.mult, ALU.mult) \
                    .then_inc(sem("result"), 1)


_OUTS = [((1, TOKENS, D), "float32")]


def kernel(**inputs):
    import concourse.bacc as _bacc
    from concourse.bass_utils import run_bass_kernel_spmd as _run

    nc = _bacc.Bacc("TRN2", target_bir_lowering=False, num_devices=1)
    table, masks = constants()
    arrays, A = {}, {}
    for name, value in {**inputs, "const_table": table, "level_masks": masks}.items():
        a = np.ascontiguousarray(value)
        arrays[f"in_{name}"] = a
        A[name] = nc.dram_tensor(f"in_{name}", a.shape, mybir.dt.from_np(a.dtype), kind="ExternalInput").ap()
    out = nc.dram_tensor("out_0", _OUTS[0][0], F32, kind="ExternalOutput").ap()
    for name in ("w_in", "w_o_gla", "w_o_swa", "w_out"):
        A[name] = A[name][0]
    A["f1_gate"], A["f1_up"] = A["w_ffn_in"][0][:, 0:D_FF], A["w_ffn_in"][0][:, D_FF:2 * D_FF]
    A["f1_down"] = A["w_ffn_out"][0]
    for part in ("gate", "up", "down"):
        A[f"f2_{part}"] = A[f"dense_w_{part}_2"][0]
        A[f"moe_w_{part}"] = A[f"moe_w_{part}_2"][0]
    for l in range(2):
        for name in ("w_in", "w_q_b", "w_kv_b", "w_out"):
            A[f"{name}_2_{l}"] = A[f"{name}_2"][l]
    build(nc, A, out)
    r = _run(nc, [arrays], core_ids=[0])
    return r.results[0]["out_0"]
```
